# Optimizing a Trainium2 kernel written in Bass

```python
import jax, jax.numpy as jnp
from jax import lax
import numpy as np
import math
import jax
import jax.numpy as jnp

D_MODEL = 1024
BATCH = 1
SEQ = 512
DEPTH = 2

GRID_W = 64
CTX_LEN = 256
N_MIXERS = 4
EPS = 1e-6
ROPE_THETA = 10000.0
NEG_INF = -1e30
Q_BLOCK = 128
HEAD_DIM = 64
D_FF = -(-(8 * D_MODEL) // (3 * 256)) * 256
SWA_HEADS = D_MODEL // HEAD_DIM
SWA_KV_HEADS = 4
SWA_WINDOW = 128
NA_HEADS = D_MODEL // HEAD_DIM
NA_KH = 8
NA_KW = 16
NA_QCB = 16
NA_SLAB = 2 * NA_KW
POOL_WINDOWS = (2, 4, 8, 16)
POOL_GROUPS = len(POOL_WINDOWS)
POOL_DG = D_MODEL // POOL_GROUPS
MLA_HEADS = 16
MLA_NOPE = 64
MLA_ROPE = 32
MLA_V = 64
MLA_Q_RANK = 256
MLA_KV_RANK = 128


def n_layers_of(m):
    return len(range(m, DEPTH, N_MIXERS))

def rms_norm(x, g):
    xf = x.astype(jnp.float32)
    y = xf * lax.rsqrt(jnp.mean(xf * xf, axis=-1, keepdims=True) + EPS)
    return (y * g.astype(jnp.float32)).astype(x.dtype)

def modulate(x, g, shift, scale):
    return rms_norm(x, g) * (1 + scale) + shift

def rope_1d(x, pos):
    half = x.shape[-1] // 2
    freqs = ROPE_THETA ** (-jnp.arange(half, dtype=jnp.float32) / half)
    ang = pos.astype(jnp.float32)[:, None] * freqs[None, :]
    cos = jnp.cos(ang)[:, None, :]
    sin = jnp.sin(ang)[:, None, :]
    xf = x.astype(jnp.float32)
    x1, x2 = xf[..., :half], xf[..., half:]
    return jnp.concatenate([x1 * cos - x2 * sin, x1 * sin + x2 * cos], -1).astype(x.dtype)

def rope_2d_axial(x, length):
    t = jnp.arange(length)
    d = x.shape[-1] // 2
    return jnp.concatenate([rope_1d(x[..., :d], t // GRID_W), rope_1d(x[..., d:], t % GRID_W)], -1)

def softmax_f32(s, sink=None):
    if sink is None:
        return jax.nn.softmax(s, axis=-1)
    sink = jnp.broadcast_to(sink, s.shape[:-1] + (1,))
    return jax.nn.softmax(jnp.concatenate([s, sink], -1), axis=-1)[..., :-1]

def swiglu(h, w_gu, w_down):
    gu = h @ w_gu
    return (jax.nn.silu(gu[..., :D_FF]) * gu[..., D_FF:]) @ w_down

def swa_mixer(a_lat, a_ctx, w_qkv, g_q, g_k, sink, w_o, need_ctx):
    B, L, _ = a_lat.shape
    Lc = a_ctx.shape[1]
    Hq, Hk, dh = SWA_HEADS, SWA_KV_HEADS, HEAD_DIM
    G = Hq // Hk
    nq, nk = Hq * dh, Hk * dh
    scale = dh ** -0.5
    qkv = a_lat @ w_qkv
    q = rope_2d_axial(rms_norm(qkv[..., :nq].reshape(B, L, Hq, dh), g_q), L)
    k = rope_2d_axial(rms_norm(qkv[..., nq:nq + nk].reshape(B, L, Hk, dh), g_k), L)
    v = qkv[..., nq + nk:].reshape(B, L, Hk, dh)
    kv_c = a_ctx @ w_qkv[:, nq:]
    k_c = rms_norm(kv_c[..., :nk].reshape(B, Lc, Hk, dh), g_k)
    v_c = kv_c[..., nk:].reshape(B, Lc, Hk, dh)
    sink_g = sink.astype(jnp.float32).reshape(Hk, G)[None, :, :, None, None]
    nb = L // Q_BLOCK
    span = Q_BLOCK + 2 * SWA_WINDOW
    pad = ((0, 0), (SWA_WINDOW, SWA_WINDOW), (0, 0), (0, 0))
    k_p = jnp.pad(k, pad)
    v_p = jnp.pad(v, pad)
    q_blocks = jnp.moveaxis(q.reshape(B, nb, Q_BLOCK, Hk, G, dh), 1, 0)
    ctx_valid = jnp.ones((Q_BLOCK, Lc), bool)

    def block(args):
        b, q_b = args
        start = b * Q_BLOCK
        k_b = jnp.concatenate([lax.dynamic_slice_in_dim(k_p, start, span, 1), k_c], 1)
        v_b = jnp.concatenate([lax.dynamic_slice_in_dim(v_p, start, span, 1), v_c], 1)
        q_pos = start + jnp.arange(Q_BLOCK)
        k_pos = start - SWA_WINDOW + jnp.arange(span)
        valid = (jnp.abs(q_pos[:, None] - k_pos[None, :]) <= SWA_WINDOW) & (k_pos >= 0) & (k_pos < L)
        valid = jnp.concatenate([valid, ctx_valid], 1)
        s = jnp.einsum('bqhgd,bkhd->bhgqk', q_b, k_b, preferred_element_type=jnp.float32) * scale
        p = softmax_f32(jnp.where(valid, s, NEG_INF), sink_g).astype(v_b.dtype)
        return jnp.einsum('bhgqk,bkhd->bqhgd', p, v_b)

    o = lax.map(block, (jnp.arange(nb), q_blocks))
    y_lat = jnp.moveaxis(o, 0, 1).reshape(B, L, nq) @ w_o
    y_ctx = None
    if need_ctx:
        q_c = rms_norm((a_ctx @ w_qkv[:, :nq]).reshape(B, Lc, Hk, G, dh), g_q)
        s = jnp.einsum('bqhgd,bkhd->bhgqk', q_c, k_c, preferred_element_type=jnp.float32) * scale
        p = softmax_f32(s, sink_g).astype(v_c.dtype)
        y_ctx = jnp.einsum('bhgqk,bkhd->bqhgd', p, v_c).reshape(B, Lc, nq) @ w_o
    return y_lat, y_ctx

def na_mixer(a_lat, a_ctx, w_qkv, g_q, g_k, rpb, w_o, need_ctx):
    B, L, _ = a_lat.shape
    Lc = a_ctx.shape[1]
    H, dh = NA_HEADS, HEAD_DIM
    n = H * dh
    scale = dh ** -0.5
    rows = L // GRID_W
    kh = min(NA_KH, rows)
    qkv = a_lat @ w_qkv
    q = rms_norm(qkv[..., :n].reshape(B, rows, GRID_W, H, dh), g_q)
    k = rms_norm(qkv[..., n:2 * n].reshape(B, rows, GRID_W, H, dh), g_k)
    v = qkv[..., 2 * n:].reshape(B, rows, GRID_W, H, dh)
    kv_c = a_ctx @ w_qkv[:, n:]
    k_c = rms_norm(kv_c[..., :n].reshape(B, Lc, H, dh), g_k)
    v_c = kv_c[..., n:].reshape(B, Lc, H, dh)
    ncb = GRID_W // NA_QCB
    q_col = np.arange(GRID_W).reshape(ncb, NA_QCB)
    slab0 = [int(s) for s in np.clip(np.arange(ncb) * NA_QCB - NA_KW // 2, 0, GRID_W - NA_SLAB)]
    col_start = np.clip(q_col - NA_KW // 2, 0, GRID_W - NA_KW)
    key_col = np.asarray(slab0)[:, None] + np.arange(NA_SLAB)
    kc3 = key_col[:, None, :]
    col_valid = (kc3 >= col_start[..., None]) & (kc3 < col_start[..., None] + NA_KW)
    dc_idx = (np.clip(kc3 - q_col[..., None], -(NA_KW - 1), NA_KW - 1) + NA_KW - 1)[:, :, None, :]
    nkey = kh * NA_SLAB
    valid_lat = np.broadcast_to(col_valid[:, :, None, :], (ncb, NA_QCB, kh, NA_SLAB)).reshape(ncb, NA_QCB, nkey)
    valid = jnp.asarray(np.concatenate([valid_lat, np.ones((ncb, NA_QCB, Lc), bool)], -1))
    rpb_f = rpb.astype(jnp.float32)

    def slabs(t):
        return jnp.stack([t[:, :, s:s + NA_SLAB] for s in slab0], 1).reshape(B, ncb, nkey, H, dh)

    def row_step(args):
        r, q_r = args
        r0 = jnp.clip(r - kh // 2, 0, rows - kh)
        k_s = slabs(lax.dynamic_slice_in_dim(k, r0, kh, 1))
        v_s = slabs(lax.dynamic_slice_in_dim(v, r0, kh, 1))
        dr_idx = (r0 + jnp.arange(kh) - r + NA_KH - 1)[None, None, :, None]
        bias = rpb_f[:, dr_idx, dc_idx].reshape(H, ncb, NA_QCB, nkey)
        q_b = q_r.reshape(B, ncb, NA_QCB, H, dh)
        s_lat = jnp.einsum('bjqhd,bjkhd->bhjqk', q_b, k_s, preferred_element_type=jnp.float32) * scale + bias
        s_ctx = jnp.einsum('bjqhd,bkhd->bhjqk', q_b, k_c, preferred_element_type=jnp.float32) * scale
        p = softmax_f32(jnp.where(valid, jnp.concatenate([s_lat, s_ctx], -1), NEG_INF)).astype(v.dtype)
        o = (jnp.einsum('bhjqk,bjkhd->bjqhd', p[..., :nkey], v_s)
             + jnp.einsum('bhjqk,bkhd->bjqhd', p[..., nkey:], v_c))
        return o.reshape(B, GRID_W, H, dh)

    o = lax.map(row_step, (jnp.arange(rows), jnp.moveaxis(q, 1, 0)))
    y_lat = jnp.moveaxis(o, 0, 1).reshape(B, L, n) @ w_o
    y_ctx = None
    if need_ctx:
        q_c = rms_norm((a_ctx @ w_qkv[:, :n]).reshape(B, Lc, H, dh), g_q)
        s = jnp.einsum('bqhd,bkhd->bhqk', q_c, k_c, preferred_element_type=jnp.float32) * scale
        p = softmax_f32(s).astype(v_c.dtype)
        y_ctx = jnp.einsum('bhqk,bkhd->bqhd', p, v_c).reshape(B, Lc, n) @ w_o
    return y_lat, y_ctx

def multi_pool(h):
    B, L, _ = h.shape
    hf = h.astype(jnp.float32)
    cs = jnp.pad(lax.cumsum(hf, axis=1), ((0, 0), (1, 0), (0, 0)))
    t = jnp.arange(L)
    outs = []
    for g, w in enumerate(POOL_WINDOWS):
        lo = jnp.clip(t - w // 2, 0, L)
        hi = jnp.clip(t - w // 2 + w, 0, L)
        cg = cs[..., g * POOL_DG:(g + 1) * POOL_DG]
        outs.append((cg[:, hi] - cg[:, lo]) / (hi - lo).astype(jnp.float32)[None, :, None])
    return (jnp.concatenate(outs, -1) - hf).astype(h.dtype)

def pool_mixer(a_lat, a_ctx, w, b, scale, need_ctx):
    def mix(h):
        B, L, _ = h.shape
        p = multi_pool(h).reshape(B, L, POOL_GROUPS, POOL_DG)
        y = jnp.einsum('blgc,gcd->blgd', p, w) + b
        return y.reshape(B, L, D_MODEL) * scale
    return mix(a_lat), (mix(a_ctx) if need_ctx else None)

def mla_mixer(a_lat, a_ctx, w_a, g_cq, g_ckv, w_uq, w_ukv, g_q, g_k, w_o, need_ctx):
    H, dn, dr, dv = MLA_HEADS, MLA_NOPE, MLA_ROPE, MLA_V
    dqk = dn + dr
    qr = MLA_Q_RANK
    scale = dqk ** -0.5

    def queries(cq_raw):
        B_, L_, _ = cq_raw.shape
        c_q = rms_norm(cq_raw, g_cq)
        return rms_norm((c_q @ w_uq).reshape(B_, L_, H, dqk), g_q)

    def keys_values(kv_raw):
        B_, L_, _ = kv_raw.shape
        c_kv = rms_norm(kv_raw[..., :MLA_KV_RANK], g_ckv)
        k_r = jnp.broadcast_to(kv_raw[..., MLA_KV_RANK:][:, :, None, :], (B_, L_, H, dr))
        kv = (c_kv @ w_ukv).reshape(B_, L_, H, dn + dv)
        k = rms_norm(jnp.concatenate([kv[..., :dn], k_r], -1), g_k)
        return k, kv[..., dn:]

    def rope_part(t):
        return jnp.concatenate([t[..., :dn], rope_2d_axial(t[..., dn:], t.shape[1])], -1)

    B, L, _ = a_lat.shape
    Lc = a_ctx.shape[1]
    proj = a_lat @ w_a
    q = rope_part(queries(proj[..., :qr]))
    k, v = keys_values(proj[..., qr:])
    k = rope_part(k)
    if need_ctx:
        proj_c = a_ctx @ w_a
        q_c = queries(proj_c[..., :qr])
        kv_raw_c = proj_c[..., qr:]
    else:
        kv_raw_c = a_ctx @ w_a[:, qr:]
    k_c, v_c = keys_values(kv_raw_c)
    k_all = jnp.concatenate([k, k_c], 1)
    v_all = jnp.concatenate([v, v_c], 1)
    nb = L // Q_BLOCK
    q_blocks = jnp.moveaxis(q.reshape(B, nb, Q_BLOCK, H, dqk), 1, 0)

    def block(q_b):
        s = jnp.einsum('bqhd,bkhd->bhqk', q_b, k_all, preferred_element_type=jnp.float32) * scale
        p = softmax_f32(s).astype(v_all.dtype)
        return jnp.einsum('bhqk,bkhd->bqhd', p, v_all)

    o = lax.map(block, q_blocks)
    y_lat = jnp.moveaxis(o, 0, 1).reshape(B, L, H * dv) @ w_o
    y_ctx = None
    if need_ctx:
        s = jnp.einsum('bqhd,bkhd->bhqk', q_c, k_c, preferred_element_type=jnp.float32) * scale
        p = softmax_f32(s).astype(v_c.dtype)
        y_ctx = jnp.einsum('bhqk,bkhd->bqhd', p, v_c).reshape(B, Lc, H * dv) @ w_o
    return y_lat, y_ctx

def first_inputs(seed: int = 0) -> dict:
    key = jax.random.key(seed)
    ks = iter(jax.random.split(key, 48))
    f32 = jnp.float32

    def nrm(shape, fan_in, gain=1.0):
        return jax.random.normal(next(ks), shape, f32) * (gain * fan_in ** -0.5)

    def gains(shape):
        return 1.0 + 0.05 * jax.random.normal(next(ks), shape, f32)

    def small(shape, s=0.01):
        return s * jax.random.normal(next(ks), shape, f32)

    D = D_MODEL
    nA, nB, nC, nD = (n_layers_of(m) for m in range(N_MIXERS))
    dqk = MLA_NOPE + MLA_ROPE
    return {
        'x': jax.random.normal(next(ks), (BATCH, SEQ, D), f32),
        'c': jax.random.normal(next(ks), (BATCH, D), f32),
        'ctx': jax.random.normal(next(ks), (BATCH, CTX_LEN, D), f32),
        'c_ctx': jax.random.normal(next(ks), (D,), f32),
        'w_ada': nrm((DEPTH, D, 6 * D), D, 0.5),
        'b_ada': small((DEPTH, 6 * D)),
        'g_mix': gains((DEPTH, D)),
        'g_ffn': gains((DEPTH, D)),
        'w_gate_up': nrm((DEPTH, D, 2 * D_FF), D),
        'w_down': nrm((DEPTH, D_FF, D), D_FF),
        'swa_w_qkv': nrm((nA, D, (SWA_HEADS + 2 * SWA_KV_HEADS) * HEAD_DIM), D),
        'swa_g_q': gains((nA, HEAD_DIM)),
        'swa_g_k': gains((nA, HEAD_DIM)),
        'swa_sink': small((nA, SWA_HEADS), 0.5),
        'swa_w_o': nrm((nA, SWA_HEADS * HEAD_DIM, D), SWA_HEADS * HEAD_DIM),
        'na_w_qkv': nrm((nB, D, 3 * NA_HEADS * HEAD_DIM), D),
        'na_g_q': gains((nB, HEAD_DIM)),
        'na_g_k': gains((nB, HEAD_DIM)),
        'na_rpb': small((nB, NA_HEADS, 2 * NA_KH - 1, 2 * NA_KW - 1), 0.1),
        'na_w_o': nrm((nB, NA_HEADS * HEAD_DIM, D), NA_HEADS * HEAD_DIM),
        'pool_w': nrm((nC, POOL_GROUPS, POOL_DG, POOL_DG), POOL_DG),
        'pool_b': small((nC, POOL_GROUPS, POOL_DG)),
        'pool_scale': gains((nC, D)),
        'mla_w_a': nrm((nD, D, MLA_Q_RANK + MLA_KV_RANK + MLA_ROPE), D),
        'mla_g_cq': gains((nD, MLA_Q_RANK)),
        'mla_g_ckv': gains((nD, MLA_KV_RANK)),
        'mla_w_uq': nrm((nD, MLA_Q_RANK, MLA_HEADS * dqk), MLA_Q_RANK),
        'mla_w_ukv': nrm((nD, MLA_KV_RANK, MLA_HEADS * (MLA_NOPE + MLA_V)), MLA_KV_RANK),
        'mla_g_q': gains((nD, dqk)),
        'mla_g_k': gains((nD, dqk)),
        'mla_w_o': nrm((nD, MLA_HEADS * MLA_V, D), MLA_HEADS * MLA_V),
    }

def first_block(x, c, ctx, c_ctx, w_ada, b_ada, g_mix, g_ffn, w_gate_up, w_down,
              swa_w_qkv, swa_g_q, swa_g_k, swa_sink, swa_w_o,
              na_w_qkv, na_g_q, na_g_k, na_rpb, na_w_o,
              pool_w, pool_b, pool_scale,
              mla_w_a, mla_g_cq, mla_g_ckv, mla_w_uq, mla_w_ukv, mla_g_q, mla_g_k, mla_w_o):
    cond = jax.nn.silu(c)
    cond_c = jax.nn.silu(c_ctx)
    h, hc = x, ctx
    for i in range(DEPTH):
        m, j = i % N_MIXERS, i // N_MIXERS
        need_ctx = i < DEPTH - 1
        mod = (cond @ w_ada[i] + b_ada[i])[:, None, :]
        mod_c = cond_c @ w_ada[i] + b_ada[i]
        sh1, sc1, gt1, sh2, sc2, gt2 = jnp.split(mod, 6, axis=-1)
        sh1c, sc1c, gt1c, sh2c, sc2c, gt2c = jnp.split(mod_c, 6, axis=-1)
        a = modulate(h, g_mix[i], sh1, sc1)
        ac = modulate(hc, g_mix[i], sh1c, sc1c)
        if m == 0:
            y, yc = swa_mixer(a, ac, swa_w_qkv[j], swa_g_q[j], swa_g_k[j], swa_sink[j], swa_w_o[j], need_ctx)
        elif m == 1:
            y, yc = na_mixer(a, ac, na_w_qkv[j], na_g_q[j], na_g_k[j], na_rpb[j], na_w_o[j], need_ctx)
        elif m == 2:
            y, yc = pool_mixer(a, ac, pool_w[j], pool_b[j], pool_scale[j], need_ctx)
        else:
            y, yc = mla_mixer(a, ac, mla_w_a[j], mla_g_cq[j], mla_g_ckv[j], mla_w_uq[j], mla_w_ukv[j],
                              mla_g_q[j], mla_g_k[j], mla_w_o[j], need_ctx)
        h = h + gt1 * y
        h = h + gt2 * swiglu(modulate(h, g_ffn[i], sh2, sc2), w_gate_up[i], w_down[i])
        if need_ctx:
            hc = hc + gt1c * yc
            hc = hc + gt2c * swiglu(modulate(hc, g_ffn[i], sh2c, sc2c), w_gate_up[i], w_down[i])
    return h


DEPTH_2 = 1

NSA_HEADS = 8
NSA_KV_GROUPS = 2
NSA_HPG = NSA_HEADS // NSA_KV_GROUPS
CMP_STRIDE = 16
CMP_BLOCK = 2 * CMP_STRIDE
CMP_HIDDEN = 256
SEL_BLOCK = 64
SEL_TOPK = 16
SEL_LOCAL = 2
WINDOW = 512
NSA_QBLOCK = 64
DN_HEADS = 8
DN_CONV = 4
DN_CHUNK = 64
REL_BUCKETS = 32
REL_MAX_DIST = 1024
N_EXPERTS = 16
N_GROUPS = 4
EXPERTS_PER_GROUP = N_EXPERTS // N_GROUPS
TOPK_GROUPS = 1
TOPK = 2
D_EXPERT = 512
MOE_BLOCK = 256

NORM_EPS = 1e-6
FORCE_SCORE = 1e9
NEG = -1e30

NSA_Q = NSA_HEADS * HEAD_DIM
NSA_KV = NSA_KV_GROUPS * HEAD_DIM
DN_W = DN_HEADS * HEAD_DIM
IN_SIZES = (NSA_Q, 6 * NSA_KV, 3 * NSA_HEADS, 3 * DN_W, DN_HEADS, DN_HEADS, DN_W, 2 * D_MODEL)
IN_SPLITS = tuple(sum(IN_SIZES[:i + 1]) for i in range(len(IN_SIZES) - 1))
D_IN = sum(IN_SIZES)


def _rms(x, g):
    xf = x.astype(jnp.float32)
    y = xf * lax.rsqrt(jnp.mean(xf * xf, axis=-1, keepdims=True) + NORM_EPS)
    return (y * g.astype(jnp.float32)).astype(x.dtype)

def _l2n(x):
    xf = x.astype(jnp.float32)
    return xf * lax.rsqrt(jnp.sum(xf * xf, axis=-1, keepdims=True) + NORM_EPS)

def _masked_softmax(logits, mask):
    p = jax.nn.softmax(jnp.where(mask, logits.astype(jnp.float32), NEG), axis=-1)
    return jnp.where(mask, p, 0.0)

def _rel_bucket(dist):
    exact = REL_BUCKETS // 2
    dist = jnp.maximum(dist, 0)
    far = jnp.maximum(dist, exact).astype(jnp.float32)
    large = exact + (jnp.log(far / exact) / math.log(REL_MAX_DIST / exact) * (REL_BUCKETS - exact)).astype(jnp.int32)
    return jnp.where(dist < exact, dist, jnp.minimum(large, REL_BUCKETS - 1))

def _compress(t, pos, w1, w2):
    b, s, g, d = t.shape
    ch = t.reshape(b, s // CMP_STRIDE, CMP_STRIDE, g, d)
    blk = jnp.concatenate([ch[:, :-1], ch[:, 1:]], axis=2) + pos[:, None, :]
    flat = jnp.swapaxes(blk, 2, 3).reshape(b, s // CMP_STRIDE - 1, g, CMP_BLOCK * d)
    return jax.nn.gelu(flat @ w1) @ w2

def _nsa(q, kv, gate, rel_bias, qk_g, cmp_pos, cmp_w1, cmp_w2):
    b, s, _ = q.shape
    G, HPG, dh, QB = NSA_KV_GROUPS, NSA_HPG, HEAD_DIM, NSA_QBLOCK
    n_cmp = s // CMP_STRIDE - 1
    n_blk = s // SEL_BLOCK
    n_sel = min(SEL_TOPK, n_blk)
    n_qb = s // QB
    q = _rms(q.reshape(b, s, G, HPG, dh), qk_g[0]) * (dh ** -0.5)
    kv = kv.reshape(b, s, 6, G, dh)
    k_cmp = _rms(_compress(kv[:, :, 0], cmp_pos[0], cmp_w1[0], cmp_w2[0]), qk_g[1])
    v_cmp = _compress(kv[:, :, 1], cmp_pos[1], cmp_w1[1], cmp_w2[1])
    k_slc = _rms(kv[:, :, 2], qk_g[2]).reshape(b, n_blk, SEL_BLOCK, G, dh).transpose(0, 3, 1, 2, 4)
    v_slc = kv[:, :, 3].reshape(b, n_blk, SEL_BLOCK, G, dh).transpose(0, 3, 1, 2, 4)
    pad = ((0, 0), (WINDOW, 0), (0, 0), (0, 0))
    k_win = jnp.pad(_rms(kv[:, :, 4], qk_g[3]), pad)
    v_win = jnp.pad(kv[:, :, 5], pad)
    gate = jax.nn.sigmoid(gate).reshape(b, s, G, HPG, 3)
    bias_g = rel_bias.reshape(REL_BUCKETS, G, HPG)
    ratio, nsub = SEL_BLOCK // CMP_STRIDE, CMP_BLOCK // CMP_STRIDE
    delta = jnp.arange(n_cmp)[:, None] - ratio * jnp.arange(n_blk)[None, :]
    m_idx = delta[..., None] + jnp.arange(nsub)
    overlap = jnp.sum((m_idx >= 0) & (m_idx < ratio), axis=-1).astype(jnp.float32)
    cmp_end = jnp.arange(n_cmp) * CMP_STRIDE + CMP_BLOCK - 1
    b_ix = jnp.arange(b)[:, None, None, None]
    g_ix = jnp.arange(G)[None, None, :, None]

    def head_bias(dist):
        return rel_bias[_rel_bucket(dist)].reshape(dist.shape[0], dist.shape[1], G, HPG).transpose(0, 2, 3, 1)

    def block(args):
        qb, gb, blk = args
        t = blk * QB + jnp.arange(QB)
        dist_c = t[:, None] - cmp_end[None, :]
        s_c = jnp.einsum('bqghd,bngd->bqghn', qb, k_cmp) + head_bias(dist_c)
        p_c = _masked_softmax(s_c, (dist_c >= 0)[:, None, None, :])
        o_c = jnp.einsum('bqghn,bngd->bqghd', p_c.astype(v_cmp.dtype), v_cmp)
        imp = jnp.einsum('bqghn,nj->bqgj', p_c, overlap)
        cur = t // SEL_BLOCK
        jb = jnp.arange(n_blk)[None, :]
        valid = (jb <= cur[:, None])[:, None, :]
        forced = valid & ((jb == 0) | (jb > cur[:, None] - SEL_LOCAL))[:, None, :]
        score = jnp.where(forced, FORCE_SCORE, jnp.where(valid, imp, -1.0))
        _, idx = lax.top_k(score, n_sel)
        kb = k_slc[b_ix, g_ix, idx]
        vb = v_slc[b_ix, g_ix, idx]
        pos = idx[..., None] * SEL_BLOCK + jnp.arange(SEL_BLOCK)
        dist_s = t[None, :, None, None, None] - pos
        bias_s = jnp.moveaxis(bias_g[_rel_bucket(dist_s), g_ix[..., None]], -1, 3)
        s_s = jnp.einsum('bqghd,bqgnkd->bqghnk', qb, kb) + bias_s
        mask_s = (dist_s >= 0).reshape(b, QB, G, 1, n_sel * SEL_BLOCK)
        p_s = _masked_softmax(s_s.reshape(b, QB, G, HPG, n_sel * SEL_BLOCK), mask_s)
        o_s = jnp.einsum('bqghm,bqgmd->bqghd', p_s.astype(vb.dtype), vb.reshape(b, QB, G, n_sel * SEL_BLOCK, dh))
        kw = lax.dynamic_slice_in_dim(k_win, blk * QB, WINDOW + QB, axis=1)
        vw = lax.dynamic_slice_in_dim(v_win, blk * QB, WINDOW + QB, axis=1)
        kpos = blk * QB - WINDOW + jnp.arange(WINDOW + QB)
        dist_w = t[:, None] - kpos[None, :]
        mask_w = (dist_w >= 0) & (dist_w < WINDOW) & (kpos[None, :] >= 0)
        s_w = jnp.einsum('bqghd,bkgd->bqghk', qb, kw) + head_bias(dist_w)
        p_w = _masked_softmax(s_w, mask_w[:, None, None, :])
        o_w = jnp.einsum('bqghk,bkgd->bqghd', p_w.astype(vw.dtype), vw)
        return gb[..., 0:1] * o_c + gb[..., 1:2] * o_s + gb[..., 2:3] * o_w

    q_blocks = jnp.moveaxis(q.reshape(b, n_qb, QB, G, HPG, dh), 1, 0)
    g_blocks = jnp.moveaxis(gate.reshape(b, n_qb, QB, G, HPG, 3), 1, 0)
    o = lax.map(block, (q_blocks, g_blocks, jnp.arange(n_qb)))
    return jnp.moveaxis(o, 0, 1).reshape(b, s, NSA_Q)

def _gated_deltanet(qkv, beta_raw, a_raw, z, conv_w, a_log, dt_bias, norm_g):
    b, s, ch = qkv.shape
    H, d, C = DN_HEADS, HEAD_DIM, DN_CHUNK
    n_ch = s // C
    qkv = jax.nn.silu(lax.conv_general_dilated(
        qkv, conv_w.reshape(DN_CONV, 1, ch), window_strides=(1,), padding=[(DN_CONV - 1, 0)],
        dimension_numbers=('NWC', 'WIO', 'NWC'), feature_group_count=ch))
    qkv = qkv.reshape(b, s, 3, H, d)
    q = _l2n(qkv[:, :, 0]) * (d ** -0.5)
    k = _l2n(qkv[:, :, 1])
    v = qkv[:, :, 2].astype(jnp.float32)
    beta = jax.nn.sigmoid(beta_raw.astype(jnp.float32))
    g = -jnp.exp(a_log.astype(jnp.float32)) * jax.nn.softplus(a_raw.astype(jnp.float32) + dt_bias.astype(jnp.float32))

    def chunks(t):
        return jnp.moveaxis(t.reshape(b, n_ch, C, H, *t.shape[3:]), 3, 1)

    q, k, v, beta, g = chunks(q), chunks(k), chunks(v), chunks(beta), chunks(g)
    g_cum = jnp.cumsum(g, axis=-1)
    causal = jnp.tril(jnp.ones((C, C), dtype=bool))
    strict = jnp.tril(jnp.ones((C, C), dtype=bool), -1)
    decay = jnp.where(causal, jnp.exp(jnp.where(causal, g_cum[..., :, None] - g_cum[..., None, :], 0.0)), 0.0)
    k_beta = k * beta[..., None]
    lower = jnp.where(strict, jnp.einsum('bhnid,bhnjd->bhnij', k_beta, k) * decay, 0.0)
    eye = jnp.eye(C, dtype=jnp.float32)
    t_inv = lax.linalg.triangular_solve(lower + eye, jnp.broadcast_to(eye, lower.shape),
                                        left_side=True, lower=True, unit_diagonal=True)
    u = t_inv @ (v * beta[..., None])
    w = t_inv @ (k_beta * jnp.exp(g_cum)[..., None])
    attn = jnp.where(causal, jnp.einsum('bhnid,bhnjd->bhnij', q, k) * decay, 0.0)
    g_last = g_cum[..., -1:]
    q_dec = q * jnp.exp(g_cum)[..., None]
    k_dec = k * jnp.exp(g_last - g_cum)[..., None]

    def step(state, xs):
        qd, kd, uc, wc, ac, gl = xs
        v_new = uc - wc @ state
        out = qd @ state + ac @ v_new
        state = state * jnp.exp(gl)[..., None] + jnp.swapaxes(kd, -1, -2) @ v_new
        return state, out

    xs = tuple(jnp.moveaxis(t, 2, 0) for t in (q_dec, k_dec, u, w, attn, g_last))
    _, o = lax.scan(step, jnp.zeros((b, H, d, d), jnp.float32), xs)
    o = jnp.moveaxis(o, 0, 2).reshape(b, H, s, d).transpose(0, 2, 1, 3)
    o = _rms(o, norm_g) * jax.nn.silu(z.astype(jnp.float32)).reshape(b, s, H, d)
    return o.reshape(b, s, DN_W).astype(z.dtype)

def _mixer(h, w_in, rel_bias, qk_g, cmp_pos, cmp_w1, cmp_w2, conv_w, a_log, dt_bias, dn_norm_g,
           w_br_a, w_br_b, w_out):
    b, s, _ = h.shape
    q_a, kv_a, gate_a, qkv_b, beta_b, a_b, z_b, merge = jnp.split(h @ w_in, IN_SPLITS, axis=-1)
    y_a = _nsa(q_a, kv_a, gate_a, rel_bias, qk_g, cmp_pos, cmp_w1, cmp_w2)
    y_b = _gated_deltanet(qkv_b, beta_b, a_b, z_b, conv_w, a_log, dt_bias, dn_norm_g)
    merge = jax.nn.sigmoid(merge).reshape(b, s, 2, D_MODEL)
    y = merge[:, :, 0] * (y_a @ w_br_a) + merge[:, :, 1] * (y_b @ w_br_b)
    return y @ w_out

def _moe(h, router_w, router_b, w_gate, w_up, w_down):
    b, s, D = h.shape
    T = b * s
    xt = h.reshape(T, D)
    scores = jax.nn.sigmoid((xt @ router_w).astype(jnp.float32))
    sel = scores + router_b.astype(jnp.float32)
    grp_score = lax.top_k(sel.reshape(T, N_GROUPS, EXPERTS_PER_GROUP), 2)[0].sum(-1)
    _, top_grp = lax.top_k(grp_score, TOPK_GROUPS)
    grp_mask = jnp.any(top_grp[..., None] == jnp.arange(N_GROUPS), axis=1)
    masked = jnp.where(jnp.repeat(grp_mask, EXPERTS_PER_GROUP, axis=1), sel, -jnp.inf)
    _, e_idx = lax.top_k(masked, TOPK)
    wts = jnp.take_along_axis(scores, e_idx, axis=1)
    wts = wts / jnp.sum(wts, axis=-1, keepdims=True)
    A = T * TOPK
    e_flat = e_idx.reshape(A)
    order = jnp.argsort(e_flat)
    e_s = e_flat[order]
    tok_s = jnp.repeat(jnp.arange(T, dtype=jnp.int32), TOPK)[order]
    w_s = wts.reshape(A)[order]
    counts = jnp.zeros((N_EXPERTS,), jnp.int32).at[e_flat].add(1)
    padded = (counts + MOE_BLOCK - 1) // MOE_BLOCK * MOE_BLOCK
    p_end = jnp.cumsum(padded)
    dest = (p_end - padded)[e_s] + jnp.arange(A) - (jnp.cumsum(counts) - counts)[e_s]
    P = A + N_EXPERTS * MOE_BLOCK
    NB = P // MOE_BLOCK
    buf_tok = jnp.full((P,), T, jnp.int32).at[dest].set(tok_s)
    buf_w = jnp.zeros((P,), h.dtype).at[dest].set(w_s.astype(h.dtype))
    blk_e = jnp.minimum(jnp.searchsorted(p_end, jnp.arange(NB) * MOE_BLOCK, side='right'), N_EXPERTS - 1)
    xb = jnp.concatenate([xt, jnp.zeros((1, D), h.dtype)], axis=0)[buf_tok].reshape(NB, MOE_BLOCK, D)

    def expert_block(args):
        xblk, e = args
        return (jax.nn.silu(xblk @ w_gate[e]) * (xblk @ w_up[e])) @ w_down[e]

    yb = lax.map(expert_block, (xb, blk_e)).reshape(P, D) * buf_w[:, None]
    out = jnp.zeros((T + 1, D), h.dtype).at[buf_tok].add(yb)[:T]
    return out.reshape(b, s, D)

def second_inputs(seed: int = 0) -> dict:
    key = jax.random.key(seed)
    ks = jax.random.split(key, 24)
    L, D, E, F = DEPTH_2, D_MODEL, N_EXPERTS, D_EXPERT

    def nrm(k, shape, scale):
        return jax.random.normal(k, shape, jnp.float32) * scale

    dt = jnp.exp(jax.random.uniform(ks[16], (L, DN_HEADS), jnp.float32, math.log(1e-3), math.log(1e-1)))
    return {
        'x': nrm(ks[0], (BATCH, SEQ, D), 1.0),
        'c': nrm(ks[1], (BATCH, D), 1.0),
        'rel_bias': nrm(ks[2], (REL_BUCKETS, NSA_HEADS), 0.2),
        'router_w': nrm(ks[3], (D, E), D ** -0.5),
        'router_b': nrm(ks[4], (E,), 0.01),
        'ada_w': nrm(ks[5], (L, D, 6 * D), 0.2 * D ** -0.5),
        'ada_b': nrm(ks[6], (L, 6 * D), 0.02),
        'norm1_g': 1.0 + nrm(ks[7], (L, D), 0.02),
        'norm2_g': 1.0 + nrm(ks[8], (L, D), 0.02),
        'w_in': nrm(ks[9], (L, D, D_IN), D ** -0.5),
        'qk_norm_g': 1.0 + nrm(ks[10], (L, 4, HEAD_DIM), 0.02),
        'cmp_pos': nrm(ks[11], (L, 2, CMP_BLOCK, HEAD_DIM), 0.1),
        'cmp_w1': nrm(ks[12], (L, 2, CMP_BLOCK * HEAD_DIM, CMP_HIDDEN), (CMP_BLOCK * HEAD_DIM) ** -0.5),
        'cmp_w2': nrm(ks[13], (L, 2, CMP_HIDDEN, HEAD_DIM), CMP_HIDDEN ** -0.5),
        'dn_conv_w': nrm(ks[14], (L, DN_CONV, 3 * DN_W), DN_CONV ** -0.5),
        'dn_a_log': jnp.log(jax.random.uniform(ks[15], (L, DN_HEADS), jnp.float32, 1.0, 16.0)),
        'dn_dt_bias': dt + jnp.log(-jnp.expm1(-dt)),
        'dn_norm_g': 1.0 + nrm(ks[17], (L, HEAD_DIM), 0.02),
        'w_branch_a': nrm(ks[18], (L, NSA_Q, D), NSA_Q ** -0.5),
        'w_branch_b': nrm(ks[19], (L, DN_W, D), DN_W ** -0.5),
        'w_out': nrm(ks[20], (L, D, D), D ** -0.5),
        'moe_w_gate': nrm(ks[21], (L, E, D, F), D ** -0.5),
        'moe_w_up': nrm(ks[22], (L, E, D, F), D ** -0.5),
        'moe_w_down': nrm(ks[23], (L, E, F, D), F ** -0.5),
    }

def second_block(x, c, rel_bias, router_w, router_b, ada_w, ada_b, norm1_g, norm2_g, w_in, qk_norm_g,
              cmp_pos, cmp_w1, cmp_w2, dn_conv_w, dn_a_log, dn_dt_bias, dn_norm_g, w_branch_a,
              w_branch_b, w_out, moe_w_gate, moe_w_up, moe_w_down):
    c_act = jax.nn.silu(c)
    for l in range(DEPTH_2):
        mod = (c_act @ ada_w[l] + ada_b[l])[:, None, :]
        sh1, sc1, g1, sh2, sc2, g2 = jnp.split(mod, 6, axis=-1)
        h = _rms(x, norm1_g[l]) * (1.0 + sc1) + sh1
        x = x + g1 * _mixer(h, w_in[l], rel_bias, qk_norm_g[l], cmp_pos[l], cmp_w1[l], cmp_w2[l],
                            dn_conv_w[l], dn_a_log[l], dn_dt_bias[l], dn_norm_g[l],
                            w_branch_a[l], w_branch_b[l], w_out[l])
        h = _rms(x, norm2_g[l]) * (1.0 + sc2) + sh2
        x = x + g2 * _moe(h, router_w, router_b, moe_w_gate[l], moe_w_up[l], moe_w_down[l])
    return x


def setup_inputs(seed=0):
    out = dict(first_inputs(seed))
    for name, value in second_inputs(seed + 1).items():
        if name != "x":
            out[name + "_2"] = value
    return out


def reference(
    x, c, ctx, c_ctx, w_ada, b_ada, g_mix, g_ffn, w_gate_up, w_down, swa_w_qkv, swa_g_q,
    swa_g_k, swa_sink, swa_w_o, na_w_qkv, na_g_q, na_g_k, na_rpb, na_w_o, pool_w, pool_b,
    pool_scale, mla_w_a, mla_g_cq, mla_g_ckv, mla_w_uq, mla_w_ukv, mla_g_q, mla_g_k, mla_w_o,
    c_2, rel_bias_2, router_w_2, router_b_2, ada_w_2, ada_b_2, norm1_g_2, norm2_g_2, w_in_2,
    qk_norm_g_2, cmp_pos_2, cmp_w1_2, cmp_w2_2, dn_conv_w_2, dn_a_log_2, dn_dt_bias_2,
    dn_norm_g_2, w_branch_a_2, w_branch_b_2, w_out_2, moe_w_gate_2, moe_w_up_2, moe_w_down_2,
):
    x = first_block(
        x, c, ctx, c_ctx, w_ada, b_ada, g_mix, g_ffn, w_gate_up, w_down, swa_w_qkv, swa_g_q,
        swa_g_k, swa_sink, swa_w_o, na_w_qkv, na_g_q, na_g_k, na_rpb, na_w_o, pool_w, pool_b,
        pool_scale, mla_w_a, mla_g_cq, mla_g_ckv, mla_w_uq, mla_w_ukv, mla_g_q, mla_g_k,
        mla_w_o,
    )
    return second_block(
        x, c_2, rel_bias_2, router_w_2, router_b_2, ada_w_2, ada_b_2, norm1_g_2, norm2_g_2,
        w_in_2, qk_norm_g_2, cmp_pos_2, cmp_w1_2, cmp_w2_2, dn_conv_w_2, dn_a_log_2,
        dn_dt_bias_2, dn_norm_g_2, w_branch_a_2, w_branch_b_2, w_out_2, moe_w_gate_2,
        moe_w_up_2, moe_w_down_2,
    )


_drawn_inputs = setup_inputs


def setup_inputs(seed=0):
    import zlib

    import numpy as np

    out = dict(_drawn_inputs(seed))
    spreads = {}
    factors = {'b_ada': 4.002,
     'g_mix': 8.0,
     'swa_g_q': 8.0,
     'swa_g_k': 8.0,
     'swa_sink': 8.0,
     'na_g_q': 8.0,
     'na_g_k': 8.0,
     'na_rpb': 8.0,
     'rel_bias_2': 8.0,
     'router_b_2': 3.879,
     'ada_b_2': 3.364,
     'norm1_g_2': 8.0,
     'norm2_g_2': 18.497,
     'qk_norm_g_2': 8.0,
     'cmp_pos_2': 8.0,
     'cmp_w1_2': 5.227,
     'cmp_w2_2': 4.178,
     'dn_a_log_2': 4.887,
     'dn_dt_bias_2': 5.21,
     'dn_norm_g_2': 47.952,
     'w_branch_a_2': 3.055}
    for name, (base, spread) in spreads.items():
        noise = np.random.default_rng([zlib.crc32(name.encode()), seed]).standard_normal(out[name].shape)
        drawn = base * np.exp(spread * noise) if base else spread * noise
        out[name] = jnp.asarray(drawn.astype(out[name].dtype))
    for name, factor in factors.items():
        out[name] = (out[name] * factor).astype(out[name].dtype)
    return out
```

```python
from contextlib import ExitStack, contextmanager

import numpy as np

import concourse.bass as bass
from concourse import mybir

ALU = mybir.AluOpType
ACT = mybir.ActivationFunctionType
AX = mybir.AxisListType
F32 = mybir.dt.float32

P = 128
D = 1024
KD = D // P
LAT = 512
CTX = 256
TOK = LAT + CTX
D_FF = 2816
KF = D_FF // P
DH = 64
SCALE = DH ** -0.5
EPS = 1e-6
NEG = -1e30
GRID_W = 64
SWA_KV = 4
BAND = 3 * P
RING = 4
SLAB = KF * P
BANK = 512
N_EXP = 16
D_EXP = 512
CHUNK = 64
N_CMP = LAT // 16 - 1
GDN_H = 8

IN_Q, IN_KV, IN_GATE, IN_DN, IN_BETA, IN_Z, IN_MERGE = 0, 512, 1280, 1304, 2840, 2856, 3368


def bucket(dist):
    exact = 16
    far = np.maximum(dist, exact).astype(np.float32)
    large = exact + (np.log(far / np.float32(exact)) / np.float32(np.log(1024 / exact)) * np.float32(32 - exact)).astype(np.int32)
    return np.where(dist < exact, np.maximum(dist, 0), np.minimum(large, 31))


def tables():
    out = {}
    out["ident"] = np.eye(P)
    out["ones"] = np.ones((P, P))
    i = np.arange(P)
    out["blk64"] = (i[:, None] // DH == i[None, :] // DH)
    rot = np.zeros((P, P))
    for m in range(P):
        if m % 32 < 16:
            rot[m + 16, m] = -1.0
        else:
            rot[m - 16, m] = 1.0
    out["rot"] = rot
    t = np.arange(LAT)
    freqs = np.float32(10000.0) ** (-np.arange(16, dtype=np.float32) / np.float32(16))
    pos = np.where((i[:, None] % DH) < 32, t[None, :] // GRID_W, t[None, :] % GRID_W).astype(np.float32)
    ang = (pos * freqs[i % 16][:, None]).astype(np.float32)
    out["cos"], out["sin"] = np.cos(ang), np.sin(ang)
    j = np.arange(BAND)
    out["swa_mask"] = np.where(np.abs(i[:, None] + P - j[None, :]) <= P, 0.0, NEG / SCALE)
    na = np.zeros((P, 3, BAND))
    for kind, cb in enumerate((0, 1, 3)):
        qc = 16 * cb + i % 16
        start = np.clip(qc - 8, 0, GRID_W - 16)
        kc = 16 * (cb + j // P - 1) + j % 16
        ok = (kc[None, :] >= start[:, None]) & (kc[None, :] < start[:, None] + 16)
        na[:, kind] = np.where(ok, 0.0, NEG / SCALE)
    out["na_mask"] = na.reshape(P, 3 * BAND)
    a = i % CHUNK
    same = i[:, None] // CHUNK == i[None, :] // CHUNK
    lev = np.zeros((P, 6, P))
    for n in range(6):
        s = 1 << n
        lev[:, n] = same & (a[:, None] // (2 * s) == a[None, :] // (2 * s)) & (a[:, None] // s % 2 == 1) & (a[None, :] // s % 2 == 0)
    out["lev"] = lev.reshape(P, -1)
    half = np.arange(CHUNK)
    out["tri"] = a[:, None] <= half[None, :]
    out["low"] = a[:, None] > half[None, :]
    out["eye2"] = a[:, None] == half[None, :]
    out["last2"] = same & (a[:, None] == CHUNK - 1)
    out["cmp_ok"] = (np.arange(4)[None, :] * P + i[:, None] >= 31)
    out["eps"] = np.full((P, 1), EPS)
    out["iota16"] = np.arange(16) + np.zeros((P, 1))
    def hot(dist):
        o = np.zeros((P, dist.size))
        o[:32] = (bucket(dist)[None, :] == np.arange(32)[:, None]) & (dist >= 0)[None, :]
        o[32] = dist < 0
        return o
    out["hot_rev"] = hot(511 - np.arange(640))
    out["hot_fwd"] = hot(np.arange(992) - 511)
    return {k: np.ascontiguousarray(v, np.float32) for k, v in out.items()}


RESIDENT = ["ident", "ones", "blk64", "rot", "cos", "sin", "tri", "low", "eye2", "last2", "cmp_ok", "iota16", "eps"]
LOADED = ["lev", "swa_mask", "na_mask", "hot_rev", "hot_fwd"]


def pack(names):
    t = tables()
    at, where = 0, {}
    for n in names:
        where[n] = (at, t[n].shape[1])
        at += t[n].shape[1]
    return where, at


class Net:

    def __init__(self, nc, ctx, dram, debug=None):
        self.nc, self.dram, self.stages, self.used = nc, dram, 0, []
        sb = lambda name, shape: ctx.enter_context(nc.sbuf_tensor(name, shape, F32))
        self.h = sb("residual", [P, KD, TOK])
        self.a = sb("normed", [P, KD, TOK])
        self.arena = sb("arena", [P, RING * SLAB + KF * TOK])
        self.ring = self.arena[:, 0:RING * SLAB].rearrange("p (s n) -> p s n", s=RING)
        self.big = self.arena[:, RING * SLAB:]
        self.where, n = pack(RESIDENT)
        self.extras, _ = pack(LOADED)
        self.const = sb("const", [P, n])
        self.vt = sb("vectors", [P, 3, P])
        self.mod = sb("mods", [P, 3, 48, 2])
        self.vec = sb("scales", [P, 9, KD])
        self.cond = sb("cond", [P, 3, KD, 2])
        self.work = sb("work", [P, 3840])
        self.ps = ctx.enter_context(nc.psum_tensor("ps", [P, 8, BANK], F32))

    def c(self, name, rows=P):
        at, n = self.where[name]
        return self.const[0:rows, at:at + n]

    def extra(self, name, rows=P):
        at, n = self.extras[name]
        return self.dram["more_tables"][0:rows, at:at + n]

    @contextmanager
    def stage(self, *names):
        self.stages += 1
        sems = [self.nc.alloc_semaphore(f"{n}_{self.stages}") for n in names]
        if self.used:
            self.nc.clear_and_free_semaphores(self.used)
        with self.nc.Block() as block:
            yield (block, *sems)
        self.used = sems


def newton(nc, dve, rstd, mean, temp, step, at):
    nc.vector.tensor_tensor(temp, rstd, rstd, ALU.mult).then_inc(step, 1)
    dve.wait_ge(step, at + 1)
    nc.vector.scalar_tensor_tensor(out=temp, in0=temp, scalar=-0.5, in1=mean, op0=ALU.mult, op1=ALU.mult).then_inc(step, 1)
    dve.wait_ge(step, at + 2)
    nc.vector.scalar_tensor_tensor(out=rstd, in0=temp, scalar=1.5, in1=rstd, op0=ALU.add, op1=ALU.mult).then_inc(step, 1)
    dve.wait_ge(step, at + 3)


V_BADA, V_GMIX, V_GFFN = 0, 96, 112
V_ADA2, V_N1, V_N2, V_C, V_CC, V_C2 = 0, 48, 56, 64, 72, 80
V_CONV, V_GAIN, V_POS = 0, 48, 57
G_SWA_Q, G_SWA_K, G_NA_Q, G_NA_K, G_QK0, G_DN = 0, 1, 2, 3, 4, 8


def load_inputs(net):
    nc, d = net.nc, net.dram
    rows = net.work[:, 0:3 * P].rearrange("p (s n) -> p s n", s=3)
    xin = net.big[:, 0:4 * D].rearrange("p (t n) -> p t n", t=4)
    cin = net.big[:, 4 * D:6 * D].rearrange("p (t n) -> p t n", t=2)
    names = ("tables_in", "rows_in", "tokens_in", "rows_zero", "turned", "copied", "vecs_done", "silu_done")
    with net.stage(*names) as (block, tables_in, rows_in, tokens_in, rows_zero, turned, copied, vecs_done, silu_done):
        fold = lambda ap: ap.rearrange("(r n) -> r n", n=P)
        loads = [
            (rows[0:96, 0, :], d["b_ada"].rearrange("l (r n) -> (l r) n", n=P)),
            (rows[96:112, 0, :], d["g_mix"].rearrange("l (r n) -> (l r) n", n=P)),
            (rows[112:128, 0, :], d["g_ffn"].rearrange("l (r n) -> (l r) n", n=P)),
            (rows[0:48, 1, :], fold(d["ada_b_2"][0])),
            (rows[48:56, 1, :], fold(d["norm1_g_2"][0])),
            (rows[56:64, 1, :], fold(d["norm2_g_2"][0])),
            (rows[64:72, 1, :], fold(d["c"][0])),
            (rows[72:80, 1, :], fold(d["c_ctx"])),
            (rows[80:88, 1, :], fold(d["c_2"][0])),
            (rows[0:48, 2, :], d["dn_conv_w_2"][0].rearrange("j (r n) -> (j r) n", n=P)),
            (rows[57:121, 2, 0:DH], d["cmp_pos_2"][0].rearrange("i j n -> (i j) n")),
        ]
        for half in range(2):
            cols = slice(half * DH, half * DH + DH)
            loads += [
                (rows[48:49, 2, cols], d["swa_g_q"]),
                (rows[49:50, 2, cols], d["swa_g_k"]),
                (rows[50:51, 2, cols], d["na_g_q"]),
                (rows[51:52, 2, cols], d["na_g_k"]),
                (rows[52:56, 2, cols], d["qk_norm_g_2"][0]),
                (rows[56:57, 2, cols], d["dn_norm_g_2"]),
            ]

        @block.sync
        def _(sp):
            sp.dma_start(net.const[:], d["tables"]).then_inc(tables_in, 16)
            sp.dma_start(xin, d["x"][0].rearrange("(t p) n -> p t n", p=P)).then_inc(tokens_in, 16)
            sp.dma_start(cin, d["ctx"][0].rearrange("(t p) n -> p t n", p=P)).then_inc(tokens_in, 16)

        @block.gpsimd
        def _(pool):
            nc.gpsimd.memset(rows[:], 0.0).then_inc(rows_zero, 1)

        @block.scalar
        def _(act):
            act.wait_ge(rows_zero, 1)
            for dst, src in loads:
                act.dma_start(dst, src).then_inc(rows_in, 16)
            for g in range(1, 16, 2):
                act.wait_ge(turned, 3 + g + 1)
                n = 4 if g < 8 else 2
                dst = net.h[:, g % 8, 0:LAT] if g < 8 else net.h[:, g % 8, LAT:TOK]
                nc.scalar.activation(dst, net.ps[:, g % 8, 0:n * P], ACT.Copy).then_inc(copied, 1)
            act.wait_ge(vecs_done, 3)
            for n, at in enumerate((V_C, V_CC, V_C2, V_C2)):
                l = 2 if n >= 2 else 0
                for ll in ((0, 1) if n < 2 else (2,)):
                    nc.scalar.activation(net.cond[:, ll, :, n % 2], net.vt[:, 1, at:at + KD], ACT.Silu).then_inc(silu_done, 1)

        @block.tensor
        def _(pe):
            pe.wait_ge(tables_in, 16)
            pe.wait_ge(rows_in, 16 * len(loads))
            for s in range(3):
                nc.tensor.transpose(net.ps[:, s, 0:P], rows[:, s, :], net.c("ident")).then_inc(turned, 1)
            pe.wait_ge(tokens_in, 32)
            for g in range(16):
                if g < 3:
                    pe.wait_ge(vecs_done, g + 1)
                if g >= 8:
                    pe.wait_ge(copied, 8)
                src, n = (xin, 4) if g < 8 else (cin, 2)
                for t in range(n):
                    mm = nc.tensor.transpose(net.ps[:, g % 8, t * P:(t + 1) * P], src[:, t, (g % 8) * P:(g % 8 + 1) * P], net.c("ident"))
                mm.then_inc(turned, 1)

        @block.vector
        def _(dve):
            for s in range(3):
                dve.wait_ge(turned, s + 1)
                nc.vector.tensor_copy(net.vt[:, s, :], net.ps[:, s, 0:P]).then_inc(vecs_done, 1)
            for g in range(0, 16, 2):
                dve.wait_ge(turned, 3 + g + 1)
                n = 4 if g < 8 else 2
                dst = net.h[:, g % 8, 0:LAT] if g < 8 else net.h[:, g % 8, LAT:TOK]
                nc.vector.tensor_copy(dst, net.ps[:, g % 8, 0:n * P]).then_inc(copied, 1)


def modulation(net):
    nc, d = net.nc, net.dram
    WIDE = 256
    PER = WIDE // P
    STEPS = 6 * D // WIDE // RING
    mats = [d["w_ada"][0], d["w_ada"][1], d["ada_w_2"][0]]
    slab = lambda s: net.ring[:, s, 0:KD * WIDE].rearrange("p (k n) -> p k n", k=KD)
    with net.stage(*[f"ada_in{s}" for s in range(RING)], "slab_used", "mod_done") as (block, *sems):
        ada_in, slab_used, mod_done = sems[:RING], sems[RING], sems[RING + 1]

        @block.sync
        def _(sp):
            for l, w in enumerate(mats):
                wv = w.rearrange("(k p) n -> p k n", p=P)
                for s in range(RING):
                    if l:
                        sp.wait_ge(slab_used, (l * STEPS - 1) * RING + s + 1)
                    sp.dma_start(slab(s), wv[:, :, s * WIDE:(s + 1) * WIDE]).then_inc(ada_in[s], 16)
                with sp.Fori(1, STEPS) as i:
                    for s in range(RING):
                        sp.wait_ge(slab_used, (i + (l * STEPS - 1)) * RING + s + 1)
                        sp.dma_start(slab(s), wv[:, :, bass.ds((i * RING + s) * WIDE, WIDE)]).then_inc(ada_in[s], 16)

        @block.tensor
        def _(pe):
            for l in range(3):
                with pe.Fori(0, STEPS) as i:
                    for s in range(RING):
                        pe.wait_ge(ada_in[s], (i + (l * STEPS + 1)) * 16)
                        for m in range(PER):
                            for k in range(KD):
                                mm = nc.tensor.matmul(net.ps[:, l, bass.ds((i * RING * PER + s * PER + m) * 2, 2)],
                                                      slab(s)[:, k, m * P:(m + 1) * P], net.cond[:, l, k, :],
                                                      start=(k == 0), stop=(k == KD - 1))
                        mm.then_inc(slab_used, 1)

        @block.vector
        def _(dve):
            for l in range(3):
                dve.wait_ge(slab_used, (l + 1) * STEPS * RING)
                bias = net.vt[:, 0, l * 48:(l + 1) * 48] if l < 2 else net.vt[:, 1, V_ADA2:V_ADA2 + 48]
                for w in range(2):
                    nc.vector.tensor_tensor(net.mod[:, l, :, w], net.ps[:, l, 0:96].rearrange("p (n w) -> p n w", w=2)[:, :, w],
                                            bias, ALU.add).then_inc(mod_done, 1)
            dve.wait_ge(mod_done, 6)
            for n, (l, w, j, gain) in enumerate(SCALES):
                g = net.vt[:, gain[0], gain[1]:gain[1] + KD]
                nc.vector.scalar_tensor_tensor(out=net.vec[:, n, :], in0=net.mod[:, l, j * KD:(j + 1) * KD, w],
                                               scalar=1.0, in1=g, op0=ALU.add, op1=ALU.mult)


SCALES = [
    (0, 0, 1, (0, V_GMIX)), (0, 1, 1, (0, V_GMIX)), (0, 0, 4, (0, V_GFFN)), (0, 1, 4, (0, V_GFFN)),
    (1, 0, 1, (0, V_GMIX + KD)), (1, 1, 1, (0, V_GMIX + KD)), (1, 0, 4, (0, V_GFFN + KD)),
    (2, 0, 1, (1, V_N1)), (2, 0, 4, (1, V_N2)),
]


def by_column_block(ap):
    return ap.rearrange("p (r b c) -> p r b c", b=4, c=16)


def modulate(net, layer, shift, scales, tokens, permute=False):
    nc = net.nc
    sq = net.work[:, 0:2 * TOK].rearrange("p (s n) -> p s n", s=2)
    ln, rstd, mean = (net.work[:, n * TOK:n * TOK + tokens] for n in (2, 3, 4))
    segs = [(0, LAT)] + ([(LAT, TOK)] if tokens > LAT else [])
    with net.stage("squared", "summed", "mean_done", "ln_done", "rstd_done", "newton_step", "scaled") as (
            block, squared, summed, mean_done, ln_done, rstd_done, newton_step, scaled):
        sums = net.ps[:, 0:2, :].rearrange("p b n -> p (b n)")[:, 0:tokens]

        @block.scalar
        def _(act):
            for c in range(KD):
                if c >= 2:
                    act.wait_ge(summed, c - 1)
                nc.scalar.activation(sq[:, c % 2, 0:tokens], net.h[:, c, 0:tokens], ACT.Square).then_inc(squared, 1)
            act.wait_ge(mean_done, 1)
            nc.scalar.activation(ln, mean, ACT.Ln).then_inc(ln_done, 1)
            act.wait_ge(ln_done, 1)
            nc.scalar.activation(rstd, ln, ACT.Exp, scale=-0.5).then_inc(rstd_done, 1)
            for c in range(KD):
                act.wait_ge(scaled, c + 1)
                for n, (lo, hi) in enumerate(segs):
                    nc.scalar.activation(net.a[:, c, lo:hi], net.a[:, c, lo:hi], ACT.Identity,
                                         scale=net.vec[:, scales[n], c:c + 1],
                                         bias=net.mod[:, layer, shift * KD + c, n:n + 1])

        @block.tensor
        def _(pe):
            for c in range(KD):
                pe.wait_ge(squared, c + 1)
                for lo, hi in segs:
                    mm = nc.tensor.matmul(sums[:, lo:hi], net.c("ones"), sq[:, c % 2, lo:hi], start=(c == 0), stop=(c == KD - 1))
                mm.then_inc(summed, 1)

        @block.vector
        def _(dve):
            dve.wait_ge(summed, KD)
            nc.vector.tensor_scalar(mean, sums, 1.0 / D, EPS, ALU.mult, ALU.add).then_inc(mean_done, 1)
            dve.wait_ge(rstd_done, 1)
            newton(nc, dve, rstd, mean, sq[:, 0, 0:tokens], newton_step, 0)
            for c in range(KD):
                if permute:
                    dst = net.a[:, c, 0:LAT].rearrange("p (b r c) -> p r b c", r=8, c=16)
                    mm = nc.vector.tensor_tensor(dst, by_column_block(net.h[:, c, 0:LAT]), by_column_block(rstd[:, 0:LAT]), ALU.mult)
                    if tokens > LAT:
                        mm = nc.vector.tensor_tensor(net.a[:, c, LAT:TOK], net.h[:, c, LAT:TOK], rstd[:, LAT:TOK], ALU.mult)
                else:
                    mm = nc.vector.tensor_tensor(net.a[:, c, 0:tokens], net.h[:, c, 0:tokens], rstd[:, 0:tokens], ALU.mult)
                mm.then_inc(scaled, 1)


def slab_loads(w, columns):
    wv = w.rearrange("(k p) n -> p k n", p=P)
    out, at = [], 0
    for first, count in columns:
        out.append((at, count, wv[:, :, first:first + count]))
        at += count
    return out


def ring_slab(net, slot, k, n):
    return net.ring[:, slot, 0:k * n].rearrange("p (k n) -> p k n", k=k)


def load_slabs(net, sp, slabs, k, width, loaded, slab_used):
    for n, loads in enumerate(slabs):
        if n >= RING:
            sp.wait_ge(slab_used, n - RING + 1)
        for at, count, src in loads:
            sp.dma_start(ring_slab(net, n % RING, k, width)[:, :, at:at + count], src).then_inc(loaded[n % RING], 16)


def slab_counts(slabs):
    total, out = [0] * RING, []
    for n, loads in enumerate(slabs):
        total[n % RING] += 16 * len(loads)
        out.append(total[n % RING])
    return out


def heads_qk(net, jobs):
    nc = net.nc
    N = len(jobs)
    slabs = [slab_loads(w, cols) for w, cols, *_ in jobs]
    counts = slab_counts(slabs)
    sq = net.work[:, 0:2 * TOK].rearrange("p (s n) -> p s n", s=2)
    ln = net.work[:, 2 * TOK:3 * TOK]
    rstd = net.work[:, 3 * TOK:5 * TOK].rearrange("p (s n) -> p s n", s=2)
    scaled = net.ring[:, 0, KD * P:KD * P + 2 * LAT].rearrange("p (s n) -> p s n", s=2)
    by_cos = net.ring[:, 1, KD * P:KD * P + LAT]
    by_sin = net.ring[:, 1, KD * P + LAT:KD * P + 2 * LAT]
    proj = lambda n: net.ps[:, 2 * (n % 2):2 * (n % 2) + 2, :].rearrange("p b n -> p (b n)")
    sums = net.ps[:, 4:6, :].rearrange("p b n -> p (b n)")
    turned = net.ps[:, 6, :]
    mean, temp = (net.ring[:, s, KD * P:KD * P + TOK] for s in (2, 3))
    names = [f"slab_in{s}" for s in range(RING)] + ["slab_used", "squared", "summed", "mean_done", "ln_done", "rstd_done",
                                                    "newton_step", "normed", "rotated", "sin_done", "cos_done", "roped"]
    rope_before = [sum(j[5] for j in jobs[:n]) for n in range(N + 1)]
    with net.stage(*names) as (block, *sems):
        slab_in, (slab_used, squared, summed, mean_done, ln_done, rstd_done, newton_step, normed, rotated, sin_done, cos_done, roped) = sems[:RING], sems[RING:]

        @block.sync
        def _(sp):
            load_slabs(net, sp, slabs, KD, P, slab_in, slab_used)

        @block.tensor
        def _(pe):
            for n in range(N + 2):
                if n < N:
                    pe.wait_ge(slab_in[n % RING], counts[n])
                    if n >= 2:
                        pe.wait_ge(normed, n - 1)
                    w, t = ring_slab(net, n % RING, KD, P), jobs[n][4]
                    for k in range(KD):
                        for lo in range(0, t, LAT):
                            hi = min(lo + LAT, t)
                            mm = nc.tensor.matmul(proj(n)[:, lo:hi], w[:, k, :], net.a[:, k, lo:hi], start=(k == 0), stop=(k == KD - 1))
                    mm.then_inc(slab_used, 1)
                if 1 <= n <= N:
                    m, t = n - 1, jobs[n - 1][4]
                    pe.wait_ge(squared, m + 1)
                    if m >= 1:
                        pe.wait_ge(mean_done, m)
                    for lo in range(0, t, LAT):
                        hi = min(lo + LAT, t)
                        mm = nc.tensor.matmul(sums[:, lo:hi], net.c("blk64"), sq[:, m % 2, lo:hi], start=True, stop=True)
                    mm.then_inc(summed, 1)
                if n >= 2 and jobs[n - 2][5]:
                    m = n - 2
                    pe.wait_ge(normed, m + 1)
                    if rope_before[m]:
                        pe.wait_ge(sin_done, rope_before[m])
                    nc.tensor.matmul(turned, net.c("rot"), scaled[:, m % 2, :], start=True, stop=True).then_inc(rotated, 1)

        @block.scalar
        def _(act):
            def square(n):
                act.wait_ge(slab_used, n + 1)
                if n >= 2:
                    act.wait_ge(summed, n - 1)
                t = jobs[n][4]
                nc.scalar.activation(sq[:, n % 2, 0:t], proj(n)[:, 0:t], ACT.Square).then_inc(squared, 1)

            square(0)
            for n in range(N):
                t = jobs[n][4]
                act.wait_ge(mean_done, n + 1)
                if n >= 1:
                    act.wait_ge(rstd_done, n)
                nc.scalar.activation(ln[:, 0:t], mean[:, 0:t], ACT.Ln).then_inc(ln_done, 1)
                act.wait_ge(ln_done, n + 1)
                if n >= 2:
                    act.wait_ge(normed, n - 1)
                nc.scalar.activation(rstd[:, n % 2, 0:t], ln[:, 0:t], ACT.Exp, scale=-0.5).then_inc(rstd_done, 1)
                if n + 1 < N:
                    square(n + 1)

        @block.vector
        def _(dve):
            def by_sine(m):
                dve.wait_ge(rotated, rope_before[m] + 1)
                if rope_before[m]:
                    dve.wait_ge(roped, rope_before[m])
                nc.vector.tensor_tensor(by_sin, turned, net.c("sin"), ALU.mult).then_inc(sin_done, 1)

            for n in range(N):
                _, _, gain, dst, t, rope = jobs[n]
                dve.wait_ge(summed, n + 1)
                nc.vector.tensor_scalar(mean[:, 0:t], sums[:, 0:t], 1.0 / DH, EPS, ALU.mult, ALU.add).then_inc(mean_done, 1)
                dve.wait_ge(rstd_done, n + 1)
                newton(nc, dve, rstd[:, n % 2, 0:t], mean[:, 0:t], temp[:, 0:t], newton_step, 3 * n)
                if rope and rope_before[n] >= 2:
                    dve.wait_ge(cos_done, rope_before[n] - 1)
                    dve.wait_ge(rotated, rope_before[n] - 1)
                spans = [(0, LAT, scaled[:, n % 2, :])] if rope else [(0, LAT, dst[:, 0:LAT])]
                if t > LAT:
                    spans.append((LAT, t, dst[:, LAT:t]))
                for lo, hi, to in spans:
                    mm = nc.vector.scalar_tensor_tensor(out=to, in0=proj(n)[:, lo:hi], scalar=gain, in1=rstd[:, n % 2, lo:hi],
                                                        op0=ALU.mult, op1=ALU.mult)
                mm.then_inc(normed, 1)
                if n >= 1 and jobs[n - 1][5]:
                    by_sine(n - 1)
            if jobs[N - 1][5]:
                by_sine(N - 1)

        @block.gpsimd
        def _(pool):
            for n in range(N):
                if jobs[n][5]:
                    pool.wait_ge(normed, n + 1)
                    if rope_before[n]:
                        pool.wait_ge(roped, rope_before[n])
                    nc.gpsimd.tensor_tensor(by_cos, scaled[:, n % 2, :], net.c("cos"), ALU.mult).then_inc(cos_done, 1)
                    pool.wait_ge(cos_done, rope_before[n] + 1)
                    pool.wait_ge(sin_done, rope_before[n] + 1)
                    nc.gpsimd.tensor_tensor(jobs[n][3][:, 0:LAT], by_cos, by_sin, ALU.add).then_inc(roped, 1)


def token_major(net, jobs, width, func=ACT.Copy):
    nc = net.nc
    slabs = [slab_loads(w, cols) for w, cols, _ in jobs]
    counts = slab_counts(slabs)
    names = [f"slab_in{s}" for s in range(RING)] + ["slab_used", "tile_done", "even_out", "odd_out"]
    with net.stage(*names) as (block, *sems):
        slab_in, (slab_used, tile_done, even_out, odd_out) = sems[:RING], sems[RING:]
        tiles = [(n, t, m, dst) for n, (_, _, ts) in enumerate(jobs) for t, m, dst in ts]
        n_cols = [sum(c for _, c in cols) for _, cols, _ in jobs]

        @block.sync
        def _(sp):
            load_slabs(net, sp, slabs, KD, width, slab_in, slab_used)

        @block.tensor
        def _(pe):
            for i, (n, t, m, _) in enumerate(tiles):
                if i == 0 or tiles[i - 1][0] != n:
                    pe.wait_ge(slab_in[n % RING], counts[n])
                if i >= 8:
                    pe.wait_ge(even_out if i % 2 == 0 else odd_out, (i - 8) // 2 + 1)
                for k in range(KD):
                    mm = nc.tensor.matmul(net.ps[0:m, i % 8, 0:n_cols[n]], net.a[:, k, t:t + m],
                                          ring_slab(net, n % RING, KD, width)[:, k, 0:n_cols[n]], start=(k == 0), stop=(k == KD - 1))
                mm.then_inc(tile_done, 1)
                if i + 1 == len(tiles) or tiles[i + 1][0] != n:
                    pe.wait_ge(tile_done, i + 1)
                    pe.sem_inc(slab_used, 1)

        @block.scalar
        def _(act):
            for i in range(0, len(tiles), 2):
                n, _, m, dst = tiles[i]
                act.wait_ge(tile_done, i + 1)
                nc.scalar.activation(dst, net.ps[0:m, i % 8, 0:n_cols[n]], func).then_inc(even_out, 1)

        @block.vector
        def _(dve):
            for i in range(1, len(tiles), 2):
                n, _, m, dst = tiles[i]
                dve.wait_ge(tile_done, i + 1)
                nc.vector.tensor_copy(dst, net.ps[0:m, i % 8, 0:n_cols[n]]).then_inc(odd_out, 1)


class Unit:

    def __init__(self, pair, b, qt, keys, biased, blocks, start=None, gate=None, first=True, last=True):
        self.pair, self.b, self.qt, self.keys, self.biased, self.blocks = pair, b, qt, keys, biased, blocks
        self.start, self.gate, self.first, self.last = start, gate, first, last
        self.lo, self.hi = keys[0][0], keys[-1][0] + keys[-1][1]
        self.steps = 2 + (start is not None) + (gate is not None)


def attention(net, groups, q_in, copies, biases, make_units, buf, out):
    nc = net.nc
    at = [0]

    def take(*shape):
        n = int(np.prod(shape))
        ap = buf[:, at[0]:at[0] + n]
        at[0] += n
        return ap if len(shape) == 1 else ap.rearrange("p (s n) -> p s n", s=shape[0])

    qs = take(2, q_in.shape[2])
    probs, turned_probs = take(2, TOK), take(2, 5 * P)
    mixed_heads = take(2, P)
    stats = take(4, 10)
    units = make_units(None)
    NU = len(units)
    NS = sum(u.steps for u in units)
    ends = [n for n, u in enumerate(units) if u.b == 1 and u.last]
    NE = len(ends)
    NC = len(copies(0)) + 1
    NB = len(biases(0))
    scores = lambda n: net.ps[:, 2 * (n % 2):2 * (n % 2) + 2, :].rearrange("p b n -> p (b n)")
    turn = net.ps[:, 4:6, :].rearrange("p b n -> p (b n)")
    mix, back = net.ps[:, 6, 0:DH], net.ps[:, 7, 0:P]
    names = ("fixed_ready", "bias_in", "vector_free", "scalar_free", "scored", "maxed", "exped", "probs_turned", "probs_copied",
             "mixed", "step", "head_scaled", "heads_turned", "heads_out")
    with net.stage(*names) as (block, fixed_ready, bias_in, vector_free, scalar_free, scored, maxed, exped, probs_turned,
                               probs_copied, mixed, step, head_scaled, heads_turned, heads_out):

        @block.sync
        def _(sp):
            if NB:
                with sp.Fori(0, groups) as g:
                    sp.wait_ge(vector_free, g + 1)
                    for dst, src in biases(g):
                        sp.dma_start(dst, src).then_inc(bias_in, 16)

        @block.gpsimd
        def _(pool):
            with pool.Fori(0, groups) as g:
                pool.wait_ge(vector_free, g + 1)
                pool.wait_ge(scalar_free, g + 1)
                nc.gpsimd.tensor_copy(qs, q_in[:, bass.ds(2 * g, 2), :]).then_inc(fixed_ready, 1)
                if NB:
                    pool.wait_ge(bias_in, (g + 1) * 16 * NB)
                for op in copies(g):
                    op().then_inc(fixed_ready, 1)

        @block.tensor
        def _(pe):
            with pe.Fori(0, groups) as g:
                valued = make_units(g)
                pe.wait_ge(fixed_ready, (g + 1) * NC)
                for s in range(NU + 3):
                    if s < NU:
                        u = units[s]
                        if s >= 2:
                            pe.wait_ge(maxed, g * NU + (s - 1))
                        for lo, n, key in u.keys:
                            mm = nc.tensor.matmul(scores(s)[:, lo:lo + n], qs[u.b * DH:(u.b + 1) * DH, u.pair, u.qt * P:(u.qt + 1) * P],
                                                  key, start=True, stop=True)
                        mm.then_inc(scored, 1)
                    if 1 <= s <= NU:
                        n, u = s - 1, units[s - 1]
                        pe.wait_ge(exped, g * NU + (n + 1))
                        if n >= 1:
                            pe.wait_ge(probs_copied, g * NU + n)
                        for j, (lo, w, _) in enumerate(u.blocks):
                            mm = nc.tensor.transpose(turn[0:w, j * P:(j + 1) * P], probs[:, n % 2, lo:lo + w], net.c("ident"))
                        mm.then_inc(probs_turned, 1)
                    if 2 <= s <= NU + 1:
                        n, u = s - 2, units[s - 2]
                        values = valued[n].blocks
                        pe.wait_ge(probs_copied, g * NU + (n + 1))
                        if n >= 1:
                            pe.wait_ge(head_scaled, g * NU + n)
                        for j, (_, w, value) in enumerate(values):
                            mm = nc.tensor.matmul(mix, turned_probs[0:w, n % 2, j * P:(j + 1) * P], value,
                                                  start=(j == 0), stop=(j == len(values) - 1))
                        mm.then_inc(mixed, 1)
                    if s >= 3 and s - 3 in ends:
                        e = ends.index(s - 3)
                        pe.wait_ge(head_scaled, g * NU + (s - 2))
                        if e >= 1:
                            pe.wait_ge(heads_out, g * NE + e)
                        nc.tensor.transpose(back, mixed_heads[:, e % 2, :], net.c("ident")).then_inc(heads_turned, 1)

        @block.scalar
        def _(act):
            act.sem_inc(scalar_free, 1)
            with act.Fori(0, groups) as g:
                act.wait_ge(fixed_ready, (g + 1) * NC)
                for s in range(NU + 3):
                    if s < NU:
                        u, st = units[s], stats[:, s % 4, :]
                        act.wait_ge(maxed, g * NU + (s + 1))
                        if u.start is not None:
                            nc.scalar.activation(st[:, 8:9], u.start, ACT.Exp, bias=st[:, 1:2])
                        nc.scalar.activation(probs[:, s % 2, u.lo:u.hi], probs[:, s % 2, u.lo:u.hi], ACT.Exp, bias=st[:, 1:2],
                                             accum_out=st[:, 2:3]).then_inc(exped, 1)
                    if 1 <= s <= NU:
                        n, u = s - 1, units[s - 1]
                        act.wait_ge(probs_turned, g * NU + (n + 1))
                        if n >= 2:
                            act.wait_ge(mixed, g * NU + (n - 1))
                        w = min(u.blocks[0][1], P)
                        nc.scalar.activation(turned_probs[0:w, n % 2, 0:len(u.blocks) * P], turn[0:w, 0:len(u.blocks) * P],
                                             ACT.Copy).then_inc(probs_copied, 1)
                    if s >= 3 and s - 3 in ends:
                        e, u = ends.index(s - 3), units[s - 3]
                        act.wait_ge(heads_turned, g * NE + (e + 1))
                        nc.scalar.activation(out[:, bass.ds(2 * g + u.pair, 1), u.qt * P:(u.qt + 1) * P],
                                             back.unsqueeze(1), ACT.Copy).then_inc(heads_out, 1)
                act.wait_ge(heads_out, g * NE + NE)
                act.sem_inc(scalar_free, 1)

        @block.vector
        def _(dve):
            dve.sem_inc(vector_free, 1)
            with dve.Fori(0, groups) as g:
                dve.wait_ge(fixed_ready, (g + 1) * NC)
                done = 0
                for s in range(NU + 2):
                    if s < NU:
                        u, st = units[s], stats[:, s % 4, :]
                        dve.wait_ge(scored, g * NU + (s + 1))
                        if s >= 2:
                            dve.wait_ge(probs_turned, g * NU + (s - 1))
                        if u.start is not None:
                            nc.vector.tensor_copy(st[:, 3:4], u.start)
                        else:
                            nc.vector.memset(st[:, 3:4], -3.0e38)
                        for n, (lo, hi, bias) in enumerate(u.biased):
                            mm = nc.vector.tensor_tensor_reduce(probs[:, s % 2, lo:hi], scores(s)[:, lo:hi], bias, SCALE, -3.0e38,
                                                                ALU.add, ALU.max, st[:, 4 + n:5 + n])
                        mm.then_inc(step, 1)
                        done += 1
                        dve.wait_ge(step, g * NS + done)
                        nc.vector.tensor_reduce(st[:, 1:2], st[:, 3:4 + len(u.biased)], AX.X, ALU.max, negate=True).then_inc(maxed, 1)
                    if s >= 2:
                        n, u = s - 2, units[s - 2]
                        st, e = stats[:, n % 4, :], sum(x < n for x in ends)
                        total = st[:, 2:3]
                        dve.wait_ge(exped, g * NU + (n + 1))
                        if u.start is not None:
                            nc.vector.tensor_tensor(st[:, 7:8], total, st[:, 8:9], ALU.add).then_inc(step, 1)
                            done += 1
                            dve.wait_ge(step, g * NS + done)
                            total = st[:, 7:8]
                        nc.vector.reciprocal(st[:, 0:1], total).then_inc(step, 1)
                        done += 1
                        dve.wait_ge(step, g * NS + done)
                        share = st[:, 0:1]
                        if u.gate is not None:
                            nc.vector.tensor_tensor(st[:, 6:7], share, u.gate, ALU.mult).then_inc(step, 1)
                            done += 1
                            dve.wait_ge(step, g * NS + done)
                            share = st[:, 6:7]
                        dve.wait_ge(mixed, g * NU + (n + 1))
                        to = mixed_heads[:, e % 2, u.b * DH:(u.b + 1) * DH]
                        if u.first:
                            if e >= 2:
                                dve.wait_ge(heads_turned, g * NE + (e - 1))
                            nc.vector.tensor_scalar(to, mix, share, None, ALU.mult).then_inc(head_scaled, 1)
                        else:
                            dve.wait_ge(head_scaled, g * NU + n)
                            nc.vector.scalar_tensor_tensor(out=to, in0=mix, scalar=share, in1=to, op0=ALU.mult,
                                                           op1=ALU.add).then_inc(head_scaled, 1)
                assert done == NS
                dve.wait_ge(head_scaled, g * NU + NU)
                dve.sem_inc(vector_free, 1)


def gate_of(net, layer, which, n, w):
    return net.mod[:, layer, which * KD + n, w:w + 1]


def project_back(net, w, k_chunks, source, layer, which, tokens, permuted=False):
    nc = net.nc
    slabs = [slab_loads(w, [(n * P, P)]) for n in range(KD)]
    counts = slab_counts(slabs)
    segs = [(0, LAT)] + ([(LAT, tokens)] if tokens > LAT else [])
    temp = net.work[:, 0:2 * LAT].rearrange("p (s n) -> p s n", s=2)
    out = lambda n: net.ps[:, 2 * (n % 4):2 * (n % 4) + 2, :].rearrange("p b n -> p (b n)")
    names = [f"slab_in{s}" for s in range(RING)] + ["product", "added", "gated"]
    with net.stage(*names) as (block, *sems):
        slab_in, (product, added, gated) = sems[:RING], sems[RING:]

        @block.sync
        def _(sp):
            load_slabs(net, sp, slabs, k_chunks, P, slab_in, product)

        @block.tensor
        def _(pe):
            for n in range(KD):
                pe.wait_ge(slab_in[n % RING], counts[n])
                if n >= 4:
                    pe.wait_ge(added, n - 3)
                slab = ring_slab(net, n % RING, k_chunks, P)
                for k in range(k_chunks):
                    for lo, hi in segs:
                        mm = nc.tensor.matmul(out(n)[:, lo:hi], slab[:, k, :], source(k)[:, lo:hi], start=(k == 0), stop=(k == k_chunks - 1))
                mm.then_inc(product, 1)

        @block.vector
        def _(dve):
            for n in range(KD):
                dve.wait_ge(product, n + 1)
                if permuted:
                    nc.vector.tensor_scalar(temp[:, n % 2, :], out(n)[:, 0:LAT], gate_of(net, layer, which, n, 0), None,
                                            ALU.mult).then_inc(gated, 1)
                    dve.wait_ge(gated, n + 1)
                    grid = by_column_block(net.h[:, n, 0:LAT])
                    nc.vector.tensor_tensor(grid, grid, temp[:, n % 2, :].rearrange("p (b r c) -> p r b c", r=8, c=16),
                                            ALU.add).then_inc(added, 1)
                    continue
                for m, (lo, hi) in enumerate(segs):
                    mm = nc.vector.scalar_tensor_tensor(out=net.h[:, n, lo:hi], in0=out(n)[:, lo:hi], scalar=gate_of(net, layer, which, n, m),
                                                        in1=net.h[:, n, lo:hi], op0=ALU.mult, op1=ALU.add)
                mm.then_inc(added, 1)


def gate_up(net, w, tokens):
    nc = net.nc
    TURNS = KF // 2
    wv = w.rearrange("(k p) n -> p k n", p=P)
    hidden = net.big.rearrange("p (n t) -> p n t", n=KF)
    silu = net.work[:, 0:2 * TOK].rearrange("p (s n) -> p s n", s=2)
    out = lambda s: net.ps[:, 2 * s:2 * s + 2, :].rearrange("p b n -> p (b n)")[:, 0:tokens]
    segs = [(lo, min(lo + LAT, tokens)) for lo in range(0, tokens, LAT)]
    names = [f"slab_in{s}" for s in range(RING)] + ["product", "silu_done", "pair_done"]
    with net.stage(*names) as (block, *sems):
        slab_in, (product, silu_done, pair_done) = sems[:RING], sems[RING:]

        @block.sync
        def _(sp):
            column = lambda i, s: (s % 2) * D_FF + (i * 2 + s // 2) * P
            for s in range(RING):
                sp.dma_start(ring_slab(net, s, KD, P), wv[:, :, column(0, s):column(0, s) + P]).then_inc(slab_in[s], 16)
            with sp.Fori(1, TURNS) as i:
                for s in range(RING):
                    sp.wait_ge(product, i * RING + (s + 1 - RING))
                    sp.dma_start(ring_slab(net, s, KD, P), wv[:, :, bass.ds(i * (2 * P) + (s % 2) * D_FF + (s // 2) * P, P)]).then_inc(slab_in[s], 16)

        @block.tensor
        def _(pe):
            with pe.Fori(0, TURNS) as i:
                for s in range(RING):
                    pe.wait_ge(slab_in[s], (i + 1) * 16)
                    pe.wait_ge(pair_done, i * 2 + (s // 2 + 1))
                    slab = ring_slab(net, s, KD, P)
                    for k in range(KD):
                        for lo, hi in segs:
                            mm = nc.tensor.matmul(out(s)[:, lo:hi], slab[:, k, :], net.a[:, k, lo:hi], start=(k == 0), stop=(k == KD - 1))
                    mm.then_inc(product, 1)

        @block.scalar
        def _(act):
            with act.Fori(0, TURNS) as i:
                for p in range(2):
                    act.wait_ge(product, i * RING + (2 * p + 1))
                    act.wait_ge(pair_done, i * 2 + (p + 1))
                    nc.scalar.activation(silu[:, p, 0:tokens], out(2 * p), ACT.Silu).then_inc(silu_done, 1)

        @block.vector
        def _(dve):
            dve.sem_inc(pair_done, 2)
            with dve.Fori(0, TURNS) as i:
                for p in range(2):
                    dve.wait_ge(product, i * RING + (2 * p + 2))
                    dve.wait_ge(silu_done, i * 2 + (p + 1))
                    nc.vector.tensor_tensor(hidden[:, bass.ds(i * 2 + p, 1), 0:tokens], silu[:, p:p + 1, 0:tokens],
                                            out(2 * p + 1).unsqueeze(1), ALU.mult).then_inc(pair_done, 1)


def feed_forward(net, layer, scales, tokens):
    d = net.dram
    modulate(net, layer, 3, scales, tokens)
    gate_up(net, d["w_gate_up"][layer], tokens)
    hidden = net.big.rearrange("p (n t) -> p n t", n=KF)
    project_back(net, d["w_down"][layer], KF, lambda k: hidden[:, k, :], layer, 5, tokens)


def sliding_layer(net):
    nc, d = net.nc, net.dram
    w = d["swa_w_qkv"][0]
    q = net.big[:, 0:KD * TOK].rearrange("p (c t) -> p c t", t=TOK)
    k = net.big[:, KD * TOK:(KD + 4) * TOK].rearrange("p (c t) -> p c t", t=TOK)
    v = net.big[:, (KD + 4) * TOK:(KD + 4) * TOK + 6 * 256].rearrange("p (t n) -> p t n", t=6)
    base = (KD + 4) * TOK + 6 * 256
    gain = lambda n: net.vt[:, 2, V_GAIN + n:V_GAIN + n + 1]
    modulate(net, 0, 0, (0, 1), TOK)
    heads_qk(net, [(w, [(D + n * DH, DH)] * 2, gain(G_SWA_K), k[:, n, :], TOK, True) for n in range(SWA_KV)]
             + [(w, [(n * P, P)], gain(G_SWA_Q), q[:, n, :], TOK, True) for n in range(KD)])
    token_major(net, [(w, [(D + 256, 256)], [(t * P, P, v[:, t, :]) for t in range(6)])], 256)

    buf = net.ring.rearrange("p s n -> p (s n)")
    mask, zero, sinks = buf[:, 0:BAND], buf[:, BAND:BAND + CTX], buf[:, BAND + CTX:BAND + CTX + 16]
    at = BAND + CTX + 16
    keys, sink = buf[:, at:at + TOK], buf[:, at + TOK:at + TOK + 4]
    with net.stage("mask_in", "zeroed") as (block, mask_in, zeroed):
        @block.sync
        def _(sp):
            sp.dma_start(mask, net.extra("swa_mask")).then_inc(mask_in, 16)
            sp.dma_start(sinks, d["swa_sink"].partition_broadcast(P)).then_inc(mask_in, 16)
            sp.wait_ge(mask_in, 32)

        @block.vector
        def _(dve):
            nc.vector.memset(zero, 0.0).then_inc(zeroed, 1)
            dve.wait_ge(zeroed, 1)

    def units(g):
        out = []
        for pair in range(2):
            for qt in range(6):
                for b in range(2):
                    kb = keys[b * DH:(b + 1) * DH, :]
                    value = lambda t: None if g is None else v[:, t, bass.ds(g * DH, DH)]
                    near = [t for t in (qt - 1, qt, qt + 1) if 0 <= t < 4] if qt < 4 else []
                    n, skip = len(near), (P if qt == 0 else 0)
                    ks, biased, blocks = [], [], []
                    if n:
                        lo = LAT - n * P
                        ks.append((lo, n * P, kb[:, near[0] * P:(near[-1] + 1) * P]))
                        biased.append((lo, LAT, mask[:, skip:skip + n * P]))
                        blocks += [(lo + j * P, P, value(t)) for j, t in enumerate(near)]
                    ks.append((LAT, CTX, kb[:, LAT:TOK]))
                    biased.append((LAT, TOK, zero))
                    blocks += [(LAT + j * P, P, value(4 + j)) for j in range(2)]
                    h = 2 * pair + b
                    out.append(Unit(pair, b, qt, ks, biased, blocks, start=sink[:, h:h + 1]))
        return out

    copies = lambda g: [
        lambda: nc.gpsimd.tensor_copy(keys.unsqueeze(1), k[:, bass.ds(g, 1), :]),
        lambda: nc.gpsimd.tensor_copy(sink, sinks[:, bass.ds(g * 4, 4)]),
    ]
    attention(net, SWA_KV, q, copies, lambda g: [], units, buf[:, at + TOK + 4:], net.a)
    project_back(net, d["swa_w_o"][0], KD, lambda k: net.a[:, k, :], 0, 2, TOK)
    feed_forward(net, 0, (2, 3), TOK)


def store_result(net, out):
    nc = net.nc
    rows = net.big[:, 0:4 * D].rearrange("p (t n) -> p t n", t=4)
    with net.stage("turned", "even_out", "odd_out", "stored") as (block, turned, even_out, odd_out, stored):

        @block.tensor
        def _(pe):
            for i in range(8):
                for c in range(4):
                    mm = nc.tensor.transpose(net.ps[:, i, c * P:(c + 1) * P], net.h[:, 4 * (i % 2) + c, (i // 2) * P:(i // 2 + 1) * P], net.c("ident"))
                mm.then_inc(turned, 1)

        @block.scalar
        def _(act):
            for i in range(0, 8, 2):
                act.wait_ge(turned, i + 1)
                nc.scalar.activation(rows[:, i // 2, 0:BANK], net.ps[:, i, :], ACT.Copy).then_inc(even_out, 1)

        @block.vector
        def _(dve):
            for i in range(1, 8, 2):
                dve.wait_ge(turned, i + 1)
                nc.vector.tensor_copy(rows[:, i // 2, BANK:2 * BANK], net.ps[:, i, :]).then_inc(odd_out, 1)

        @block.sync
        def _(sp):
            for t in range(4):
                sp.wait_ge(even_out, t + 1)
                sp.wait_ge(odd_out, t + 1)
                sp.dma_start(out[0, t * P:(t + 1) * P, :], rows[:, t, :]).then_inc(stored, 16)
            sp.wait_ge(stored, 64)


def program(nc, dram, out, upto=9):
    with ExitStack() as ctx:
        net = Net(nc, ctx, dram)
        load_inputs(net)
        modulation(net)
        prepare_biases(net)
        sliding_layer(net)
        if upto > 0:
            neighbour_layer(net)
        if upto > 1:
            second_block(net, upto)
        store_result(net, out)


def prepare_biases(net):
    nc, d = net.nc, net.dram
    na_table = nc.dram_tensor("na_table", (16, 15 * 64), F32, kind="Internal").ap()
    rel_table = nc.dram_tensor("rel_table", (8, 640), F32, kind="Internal").ap()
    net.na_bias = nc.dram_tensor("na_bias", (16, 16, 15 * 48), F32, kind="Internal").ap()
    net.rel_bias = nc.dram_tensor("rel_bias_tiles", (8, P, LAT), F32, kind="Internal").ap()
    raw = net.work[0:16, 0:15 * 31].rearrange("p (r c) -> p r c", c=31)
    wide = net.work[0:16, 512:512 + 15 * 64].rearrange("p (r c) -> p r c", c=64)
    rel = net.work[0:32, 1600:1608]
    rel_far = net.work[0:33, 1608:1616]
    hot = net.work[0:33, 1616:2256]
    rel_rows = net.work[0:8, 2256:2896]
    with net.stage("params_in", "cleared", "scaled", "rel_done", "rel_copied", "table_out", "tiles_out") as (
            block, params_in, cleared, scaled, rel_done, rel_copied, table_out, tiles_out):
        @block.sync
        def _(sp):
            sp.dma_start(raw, d["na_rpb"][0]).then_inc(params_in, 16)
            sp.dma_start(rel, d["rel_bias_2"]).then_inc(params_in, 16)
            sp.dma_start(hot, net.extra("hot_rev", 33)).then_inc(params_in, 16)
            sp.wait_ge(scaled, 2)
            sp.dma_start(na_table, wide.rearrange("p r c -> p (r c)")).then_inc(table_out, 16)
            sp.wait_ge(rel_copied, 2)
            sp.dma_start(rel_table, rel_rows).then_inc(table_out, 16)
            sp.wait_ge(table_out, 32)
            for dr in range(15):
                src = bass.AP(na_table.tensor, dr * 64 + 15, [[960, 16], [-1, 16], [1, 48]])
                sp.dma_start(net.na_bias[:, :, dr * 48:(dr + 1) * 48], src).then_inc(tiles_out, 16)
            src = bass.AP(rel_table.tensor, P - 1, [[640, 8], [-1, P], [1, LAT]])
            sp.dma_start(net.rel_bias, src).then_inc(tiles_out, 16)
            sp.wait_ge(tiles_out, 16 * 16)

        @block.vector
        def _(dve):
            nc.vector.memset(net.work[0:16, 512:512 + 15 * 64], 0.0)
            nc.vector.memset(rel_far, NEG / SCALE).then_inc(cleared, 1)
            dve.wait_ge(cleared, 1)
            dve.wait_ge(params_in, 48)
            nc.vector.tensor_scalar(wide[:, :, 16:47], raw, 1.0 / SCALE, None, ALU.mult).then_inc(scaled, 1)
            nc.vector.tensor_scalar(net.work[0:32, 1608:1616], rel, 1.0 / SCALE, None, ALU.mult).then_inc(scaled, 1)
            for b, (lo, hi) in enumerate(((0, 512), (512, 640))):
                dve.wait_ge(rel_done, b + 1)
                nc.vector.tensor_copy(rel_rows[:, lo:hi], net.ps[0:8, b, 0:hi - lo]).then_inc(rel_copied, 1)

        @block.tensor
        def _(pe):
            pe.wait_ge(scaled, 2)
            for b, (lo, hi) in enumerate(((0, 512), (512, 640))):
                nc.tensor.matmul(net.ps[0:8, b, 0:hi - lo], rel_far, hot[:, lo:hi], start=True, stop=True).then_inc(rel_done, 1)


def neighbour_layer(net):
    nc, d = net.nc, net.dram
    w = d["na_w_qkv"][0]
    q = net.big[:, 0:KD * LAT].rearrange("p (c t) -> p c t", t=LAT)
    k = net.big[:, KD * LAT:KD * (LAT + TOK)].rearrange("p (c t) -> p c t", t=TOK)
    v = net.big[:, KD * (LAT + TOK):KD * (LAT + TOK) + 6 * D].rearrange("p (t n) -> p t n", t=6)
    gain = lambda n: net.vt[:, 2, V_GAIN + n:V_GAIN + n + 1]
    modulate(net, 1, 0, (4, 5), TOK, permute=True)
    heads_qk(net, [(w, [(n * P, P)], gain(G_NA_Q), q[:, n, :], LAT, False) for n in range(KD)]
             + [(w, [(D + n * P, P)], gain(G_NA_K), k[:, n, :], TOK, False) for n in range(KD)])
    token_major(net, [(w, [(2 * D + n * 256, 256)], [(t * P, P, v[:, t, n * 256:(n + 1) * 256]) for t in range(6)])
                      for n in range(4)], 256)

    mask = net.work[:, 0:3 * BAND].rearrange("p (k n) -> p k n", k=3)
    raw = net.work[:, 3 * BAND:7 * BAND].rearrange("p (h n) -> p h n", h=4)
    buf = net.ring.rearrange("p s n -> p (s n)")
    zero = buf[:, 0:CTX]
    keys = buf[:, CTX:CTX + 2 * TOK].rearrange("p (c t) -> p c t", c=2)
    at = CTX + 2 * TOK
    spans = [(0, P, BAND), (2 * P, 0, BAND), (5 * P, 0, 2 * P)]
    width = 7 * P
    bias = buf[:, at:at + 4 * width].rearrange("p (h n) -> p h n", h=4)
    with net.stage("mask_in", "zeroed") as (block, mask_in, zeroed):
        @block.sync
        def _(sp):
            sp.dma_start(mask.rearrange("p k n -> p (k n)"), net.extra("na_mask")).then_inc(mask_in, 16)
            sp.wait_ge(mask_in, 16)

        @block.vector
        def _(dve):
            nc.vector.memset(zero, 0.0).then_inc(zeroed, 1)
            dve.wait_ge(zeroed, 1)

    def copies(g):
        def masked(h, kind):
            to, lo, hi = spans[kind]
            def op():
                view = lambda ap: ap.rearrange("p (d r c) -> p r d c", r=8, c=16)
                src = raw[:, h, :].rearrange("p (r d c) -> p r d c", r=8, c=16)[:, :, lo // P:hi // P, :]
                return nc.gpsimd.tensor_tensor(view(bias[:, h, to:to + hi - lo]), src, view(mask[:, kind, lo:hi]), ALU.add)
            return op
        return ([lambda: nc.gpsimd.tensor_copy(keys, k[:, bass.ds(2 * g, 2), :])]
                + [masked(h, kind) for h in range(4) for kind in range(3)])

    def units(g):
        out = []
        for pair in range(2):
            for qt in range(4):
                for b in range(2):
                    kb = keys[b * DH:(b + 1) * DH, pair, :]
                    h = 2 * pair + b
                    value = lambda t: None if g is None else v[:, t, bass.ds(g * 256 + h * DH, DH)]
                    near = [t for t in (qt - 1, qt, qt + 1) if 0 <= t < 4]
                    n, at = len(near), spans[(0, 1, 1, 2)[qt]][0]
                    lo = LAT - n * P
                    ks = [(lo, n * P, kb[:, near[0] * P:(near[-1] + 1) * P]), (LAT, CTX, kb[:, LAT:TOK])]
                    biased = [(lo, LAT, bias[:, h, at:at + n * P]), (LAT, TOK, zero)]
                    blocks = [(lo + j * P, P, value(t)) for j, t in enumerate(near)] + [(LAT + j * P, P, value(4 + j)) for j in range(2)]
                    out.append(Unit(pair, b, qt, ks, biased, blocks))
        return out

    biases = lambda g: [(raw[r * 16:(r + 1) * 16], net.na_bias[bass.ds(g * 4, 4), :, (7 - r) * 48:(15 - r) * 48].rearrange("h q n -> q h n"))
                        for r in range(8)]
    attention(net, 4, q, copies, biases, units, buf[:, at + 4 * width:], net.a)
    project_back(net, d["na_w_o"][0], KD, lambda k: net.a[:, k, :], 1, 2, LAT, permuted=True)
    feed_forward(net, 1, (6,), LAT)


class Sparse:

    def __init__(self, net):
        big = net.big
        cols = lambda at, *shape: big[:, at:at + int(np.prod(shape))]
        self.ya = cols(0, 4, LAT).rearrange("p (c t) -> p c t", t=LAT)
        self.yb = cols(2048, 4, LAT).rearrange("p (c t) -> p c t", t=LAT)
        self.q = cols(4096, 4, LAT).rearrange("p (c t) -> p c t", t=LAT)
        self.k = cols(6144, 4, LAT).rearrange("p (c t) -> p c t", t=LAT)
        self.v = cols(8192, 4, 256).rearrange("p (t n) -> p t n", t=4)
        self.strips = cols(9216, 4, LAT).rearrange("p (c t) -> p c t", t=LAT)[0:DH]
        self.cmp_bias = cols(11264, 4, N_CMP * 8).rearrange("p (q n h) -> p q n h", q=4, h=8)
        self.gates = cols(12288, 4, 24).rearrange("p (q n) -> p q n", q=4)
        small = lambda n: cols(12384 + 32 * n, 32).rearrange("p (c h) -> p c h", h=4)
        self.beta, self.sums, self.eg, self.el, self.egl, self.g, self.totals = [small(n) for n in range(7)]
        self.small = cols(12384, 160).rearrange("p (n c h) -> p n c h", n=5, h=4)
        self.k_cmp = cols(12700, 2 * N_CMP)
        self.v_cmp = cols(12762, 128)[0:N_CMP]
        self.cmp_hidden = cols(12890, 2, 2, 2 * N_CMP).rearrange("p (i m n) -> p i m n", i=2, m=2)
        self.windows = cols(13600, 32, 2 * N_CMP).rearrange("p (j n) -> p j n", j=32)[0:DH]
        self.hot = cols(15584, 992)[0:33]
        self.rel = cols(16576, 8)
        self.qkv = cols(4096, 12, LAT).rearrange("p (c t) -> p c t", t=LAT)
        self.merged = cols(4096, 8, LAT).rearrange("p (c t) -> p c t", t=LAT)


def gates_and_decays(net, sp_):
    nc, d = net.nc, net.dram
    w = d["w_in_2"][0].rearrange("(k p) n -> p k n", p=P)
    slab = net.ring[:, 0, 0:KD * 40].rearrange("p (k n) -> p k n", k=KD)
    alog, dtb = (net.work[:, 8 * n:8 * n + 8] for n in range(2))
    negexp = net.work[:, 16:20]
    own = lambda ap, par: ap[par * DH:par * DH + DH].rearrange("p (h q) -> p h q", q=2)[:, :, par]
    x, ax, ex, z, z2, poly, pos = (net.work[:, 64 + 32 * n:96 + 32 * n].rearrange("p (c h) -> p c h", h=4) for n in range(7))
    rows = net.work[0:32, 512:640]
    carry = net.work[0:32, 640:648].rearrange("p (q b) -> p q b", q=2)
    wide = lambda ap: ap.unsqueeze(1).to_broadcast([P, 8, 4])
    names = ("weights_in", "consts_in", "gates_raw", "ba_raw", "g_ready", "g_turned", "rows_summed", "sums_turned", "gc_ready",
             "last_done", "gates_sig", "exps", "x_ready", "exp_ready", "room_ready", "link")
    with net.stage(*names) as (block, weights_in, consts_in, gates_raw, ba_raw, g_ready, g_turned, rows_summed, sums_turned,
                               gc_ready, last_done, gates_sig, exps, x_ready, exp_ready, room_ready, link):
        @block.sync
        def _(sp):
            sp.dma_start(slab[:, :, 0:24], w[:, :, IN_GATE:IN_GATE + 24]).then_inc(weights_in, 16)
            sp.dma_start(slab[:, :, 24:40], w[:, :, IN_BETA:IN_BETA + 16]).then_inc(weights_in, 16)
            for dst, src in ((alog, d["dn_a_log_2"]), (dtb, d["dn_dt_bias_2"])):
                sp.dma_start(dst, src[0].partition_broadcast(P)).then_inc(consts_in, 16)

        @block.tensor
        def _(pe):
            pe.wait_ge(weights_in, 32)
            for t in range(4):
                for k in range(KD):
                    mm = nc.tensor.matmul(net.ps[:, 0, t * 24:t * 24 + 24], net.a[:, k, t * P:(t + 1) * P], slab[:, k, 0:24],
                                          start=(k == 0), stop=(k == KD - 1))
            mm.then_inc(gates_raw, 1)
            for par in range(2):
                for c in range(8):
                    for k in range(KD):
                        rhs = slab[:, k, 24:40].rearrange("p (w h q) -> p w h q", w=2, q=2)[:, :, :, par]
                        mm = nc.tensor.matmul(net.ps[par * DH:par * DH + DH, 1 + par, c * 8:c * 8 + 8].rearrange("p (w h) -> p w h", w=2),
                                              net.a[:, k, c * CHUNK:(c + 1) * CHUNK], rhs, start=(k == 0), stop=(k == KD - 1))
            mm.then_inc(ba_raw, 1)
            pe.wait_ge(g_ready, 1)
            nc.tensor.transpose(net.ps[0:32, 3, 0:P], sp_.g.rearrange("p c h -> p (c h)"), net.c("ident")).then_inc(g_turned, 1)
            pe.wait_ge(rows_summed, 1)
            nc.tensor.transpose(net.ps[:, 4, 0:32], rows, net.c("ident")[0:32, 0:32]).then_inc(sums_turned, 1)
            pe.wait_ge(gc_ready, 1)
            nc.tensor.matmul(net.ps[:, 5, 0:32], net.c("last2"), sp_.sums.rearrange("p c h -> p (c h)"), start=True, stop=True).then_inc(last_done, 1)

        @block.scalar
        def _(act):
            act.wait_ge(gates_raw, 1)
            nc.scalar.activation(sp_.gates, net.ps[:, 0, 0:96].rearrange("p (q n) -> p q n", q=4), ACT.Sigmoid).then_inc(gates_sig, 1)
            act.wait_ge(ba_raw, 1)
            for par in range(2):
                rows = slice(par * DH, par * DH + DH)
                raw = net.ps[rows, 1 + par, 0:64].rearrange("p (c w h) -> p c w h", c=8, w=2)
                nc.scalar.activation(sp_.beta[rows], raw[:, :, 0, :], ACT.Sigmoid).then_inc(gates_sig, 1)
            act.wait_ge(consts_in, 32)
            for par in range(2):
                ins = nc.scalar.activation(negexp[par * DH:par * DH + DH], own(alog, par), ACT.Exp)
            act.wait_ge(x_ready, 2)
            nc.scalar.activation(ax, x, ACT.Abs).then_inc(exps, 1)
            act.wait_ge(exps, 1)
            nc.scalar.activation(ex, ax, ACT.Exp, scale=-1.0).then_inc(exp_ready, 1)
            act.wait_ge(room_ready, 1)
            nc.scalar.activation(sp_.eg, sp_.sums, ACT.Exp)
            nc.scalar.activation(sp_.egl, sp_.totals, ACT.Exp)
            nc.scalar.activation(sp_.el, x, ACT.Exp)

        @block.vector
        def _(dve):
            v, links = nc.vector, 0

            def linked(ins):
                nonlocal links
                links += 1
                ins.then_inc(link, 1)
                dve.wait_ge(link, links)

            dve.wait_ge(gates_sig, 3)
            g0 = sp_.gates.rearrange("p q (h b) -> p q h b", b=3)[:, :, :, 0]
            v.tensor_tensor(g0, g0, net.c("cmp_ok").unsqueeze(2).to_broadcast([P, 4, 8]), ALU.mult)
            dve.wait_ge(consts_in, 32)
            for par in range(2):
                half = slice(par * DH, par * DH + DH)
                raw = net.ps[half, 1 + par, 0:64].rearrange("p (c w h) -> p c w h", c=8, w=2)
                v.tensor_tensor(x[half], raw[:, :, 1, :], own(dtb, par).unsqueeze(1).to_broadcast([DH, 8, 4]), ALU.add).then_inc(x_ready, 1)
            dve.wait_ge(x_ready, 2)
            v.tensor_scalar(pos, x, 0.0, None, ALU.max)
            dve.wait_ge(exp_ready, 1)
            linked(v.tensor_scalar(z2, ex, 2.0, None, ALU.add))
            linked(v.reciprocal(z2, z2))
            linked(v.tensor_tensor(z, ex, z2, ALU.mult))
            linked(v.tensor_tensor(z2, z, z, ALU.mult))
            linked(v.tensor_scalar(poly, z2, 1.0 / 17, None, ALU.mult))
            for n in (15, 13, 11, 9, 7, 5, 3):
                linked(v.scalar_tensor_tensor(out=poly, in0=poly, scalar=1.0 / n, in1=z2, op0=ALU.add, op1=ALU.mult))
            linked(v.scalar_tensor_tensor(out=poly, in0=poly, scalar=1.0, in1=z, op0=ALU.add, op1=ALU.mult))
            linked(v.scalar_tensor_tensor(out=pos, in0=poly, scalar=2.0, in1=pos, op0=ALU.mult, op1=ALU.add))
            linked(v.tensor_tensor(pos, pos, wide(negexp), ALU.mult))
            v.tensor_scalar(sp_.g, pos, -1.0, None, ALU.mult).then_inc(g_ready, 1)
            dve.wait_ge(g_turned, 1)
            linked(v.tensor_copy(rows, net.ps[0:32, 3, 0:P]))
            cell = rows.rearrange("p (q b t) -> p q b t", q=2, t=16)
            for n in range(1, 16):
                linked(v.tensor_tensor(cell[:, :, :, n], cell[:, :, :, n], cell[:, :, :, n - 1], ALU.add))
            linked(v.tensor_copy(carry[:, :, 1], cell[:, :, 0, 15]))
            for n in (2, 3):
                linked(v.tensor_tensor(carry[:, :, n], carry[:, :, n - 1], cell[:, :, n - 1, 15], ALU.add))
            v.tensor_tensor(cell[:, :, 1:4, :], cell[:, :, 1:4, :], carry[:, :, 1:4].unsqueeze(3).to_broadcast([32, 2, 3, 16]), ALU.add)\
                .then_inc(rows_summed, 1)
            view = lambda b: net.ps[:, b, 0:32].rearrange("p (c h) -> p c h", h=4)
            dve.wait_ge(sums_turned, 1)
            v.tensor_copy(sp_.sums, view(4)).then_inc(gc_ready, 1)
            dve.wait_ge(last_done, 1)
            dve.wait_ge(gc_ready, 1)
            linked(v.tensor_copy(sp_.totals, view(5)))
            v.tensor_tensor(x, sp_.totals, sp_.sums, ALU.subtract).then_inc(room_ready, 1)


def compress(net, sp_):
    nc, d = net.nc, net.dram
    w = d["w_in_2"][0].rearrange("(k p) n -> p k n", p=P)
    slab = net.work[:, 0:KD * 256].rearrange("p (k n) -> p k n", k=KD)
    sq, ln, rstd, mean, temp = (net.work[:, 2048 + 64 * n:2048 + 64 * n + 62] for n in range(5))
    flat = net.ring.rearrange("p s n -> p (s n)")
    w1 = flat[0:DH, 0:32 * 256].rearrange("p (j n) -> p j n", j=32)
    w2k = flat[:, 8192:8192 + 256].rearrange("p (m n) -> p m n", m=2)
    w2v = flat[:, 8448:8448 + 128].rearrange("p (m n) -> p m n", m=2)
    N = 2 * N_CMP
    names = ("slab_in", "w1_in", "w2_in", "hot_in", "strip_done", "strip_out", "windows_done", "hidden_done", "gelu_done",
             "out_done", "squared", "summed", "mean_done", "newton_step", "ln_done", "rstd_done", "rel_ready", "bias_done", "copied")
    with net.stage(*names) as (block, slab_in, w1_in, w2_in, hot_in, strip_done, strip_out, windows_done, hidden_done, gelu_done,
                               out_done, squared, summed, mean_done, newton_step, ln_done, rstd_done, rel_ready, bias_done, copied):
        @block.sync
        def _(sp):
            sp.dma_start(slab, w[:, :, IN_KV:IN_KV + 256]).then_inc(slab_in, 16)
            sp.dma_start(sp_.rel[0:32], d["rel_bias_2"]).then_inc(hot_in, 16)
            sp.dma_start(sp_.hot, net.extra("hot_fwd", 33)).then_inc(hot_in, 16)
            sp.dma_start(w2v, d["cmp_w2_2"][0, 1].rearrange("(m p) n -> p m n", p=P)).then_inc(w2_in, 16)
            for half in range(2):
                sp.dma_start(w2k[:, :, half * DH:half * DH + DH], d["cmp_w2_2"][0, 0].rearrange("(m p) n -> p m n", p=P)).then_inc(w2_in, 16)
            for i in range(2):
                if i:
                    sp.wait_ge(hidden_done, 2)
                sp.dma_start(w1, d["cmp_w1_2"][0, i].rearrange("(j p) n -> p j n", p=DH)).then_inc(w1_in, 16)

        @block.tensor
        def _(pe):
            pe.wait_ge(slab_in, 16)
            for n in range(4):
                for k in range(KD):
                    mm = nc.tensor.matmul(net.ps[0:DH, n, :], slab[:, k, n * DH:(n + 1) * DH], net.a[:, k, 0:LAT],
                                          start=(k == 0), stop=(k == KD - 1))
                mm.then_inc(strip_done, 1)
            pe.wait_ge(rel_ready, 2)
            for q in range(4):
                for n in range(N_CMP):
                    y = P * q - 16 * n - 31 + 511
                    mm = nc.tensor.matmul(net.ps[:, 4 + q // 2, (q % 2) * 256 + n * 8:(q % 2) * 256 + n * 8 + 8], sp_.hot[:, y:y + P],
                                          sp_.rel[0:33, :], start=True, stop=True)
                mm.then_inc(bias_done, 1)
            for i in range(2):
                pe.wait_ge(w1_in, 16 * (i + 1))
                pe.wait_ge(windows_done, i + 1)
                for m in range(2):
                    if i:
                        pe.wait_ge(gelu_done, m + 1)
                    for j in range(32):
                        mm = nc.tensor.matmul(net.ps[:, 6 + m, 0:N], w1[:, j, m * P:(m + 1) * P], sp_.windows[:, j, :],
                                              start=(j == 0), stop=(j == 31))
                    mm.then_inc(hidden_done, 1)
            pe.wait_ge(w2_in, 48)
            pe.wait_ge(gelu_done, 4)
            pe.wait_ge(strip_out, 4)
            for m in range(2):
                mm = nc.tensor.matmul(net.ps[:, 0, 0:N], w2k[:, m, :], sp_.cmp_hidden[:, 0, m, :], start=(m == 0), stop=(m == 1))
            mm.then_inc(out_done, 1)
            for g in range(2):
                for m in range(2):
                    mm = nc.tensor.matmul(net.ps[0:N_CMP, 1, g * DH:(g + 1) * DH], sp_.cmp_hidden[:, 1, m, g * N_CMP:(g + 1) * N_CMP],
                                          w2v[:, m, :], start=(m == 0), stop=(m == 1))
            mm.then_inc(out_done, 1)
            pe.wait_ge(squared, 1)
            nc.tensor.matmul(net.ps[:, 2, 0:N], net.c("blk64"), sq, start=True, stop=True).then_inc(summed, 1)

        @block.scalar
        def _(act):
            for n in range(4):
                act.wait_ge(strip_done, n + 1)
                nc.scalar.activation(sp_.strips[:, n, :], net.ps[0:DH, n, :], ACT.Copy).then_inc(strip_out, 1)
            for i in range(2):
                for m in range(2):
                    act.wait_ge(hidden_done, 2 * i + m + 1)
                    nc.scalar.activation(sp_.cmp_hidden[:, i, m, :], net.ps[:, 6 + m, 0:N], ACT.Gelu_apprx_tanh).then_inc(gelu_done, 1)
            act.wait_ge(out_done, 1)
            nc.scalar.activation(sq, net.ps[:, 0, 0:N], ACT.Square).then_inc(squared, 1)
            act.wait_ge(mean_done, 1)
            nc.scalar.activation(ln, mean, ACT.Ln).then_inc(ln_done, 1)
            act.wait_ge(ln_done, 1)
            nc.scalar.activation(rstd, ln, ACT.Exp, scale=-0.5).then_inc(rstd_done, 1)

        @block.vector
        def _(dve):
            nc.vector.memset(net.work[0:33, 3000:3008], NEG / SCALE).then_inc(rel_ready, 1)
            dve.wait_ge(rel_ready, 1)
            dve.wait_ge(hot_in, 32)
            nc.vector.tensor_scalar(net.work[0:32, 3000:3008], sp_.rel[0:32], 1.0 / SCALE, None, ALU.mult).then_inc(copied, 1)
            dve.wait_ge(copied, 1)
            nc.vector.tensor_copy(sp_.rel[0:33], net.work[0:33, 3000:3008]).then_inc(rel_ready, 1)
            dve.wait_ge(strip_out, 4)
            part = sp_.strips.ap[0]
            for i in range(2):
                if i:
                    dve.wait_ge(hidden_done, 2)
                strip = sp_.strips[:, 2 * i, 0:1]
                src = bass.AP(strip.tensor, strip.offset, [list(part), [1, 32], [LAT, 2], [16, N_CMP]])
                pos = net.vt[0:DH, 2, V_POS + 32 * i:V_POS + 32 * (i + 1)]
                nc.vector.tensor_tensor(sp_.windows.rearrange("p j (g n) -> p j g n", g=2), src,
                                        pos.unsqueeze(2).unsqueeze(3).to_broadcast([DH, 32, 2, N_CMP]), ALU.add).then_inc(windows_done, 1)
            for q in range(4):
                dve.wait_ge(bias_done, 4)
                nc.vector.tensor_copy(sp_.cmp_bias[:, q], net.ps[:, 4 + q // 2, (q % 2) * 256:(q % 2) * 256 + N_CMP * 8]
                                      .rearrange("p (n h) -> p n h", h=8))
            dve.wait_ge(out_done, 2)
            nc.vector.tensor_copy(sp_.v_cmp, net.ps[0:N_CMP, 1, 0:128])
            dve.wait_ge(summed, 1)
            nc.vector.tensor_scalar(mean, net.ps[:, 2, 0:N], 1.0 / DH, EPS, ALU.mult, ALU.add).then_inc(mean_done, 1)
            dve.wait_ge(rstd_done, 1)
            newton(nc, dve, rstd, mean, temp, newton_step, 0)
            nc.vector.scalar_tensor_tensor(out=sp_.k_cmp, in0=net.ps[:, 0, 0:N], scalar=net.vt[:, 2, V_GAIN + G_QK0 + 1:V_GAIN + G_QK0 + 2],
                                           in1=rstd, op0=ALU.mult, op1=ALU.mult)


def sparse_attention(net, sp_):
    nc, d = net.nc, net.dram
    w = d["w_in_2"][0]
    gain = lambda n: net.vt[:, 2, V_GAIN + G_QK0 + n:V_GAIN + G_QK0 + n + 1]
    kv = lambda i, g: IN_KV + (2 * i + g) * DH
    heads_qk(net, [(w, [(IN_Q + n * P, P)], gain(0), sp_.q[:, n, :], LAT, False) for n in range(4)]
             + [(w, [(kv(i, g), DH)] * 2, gain(i // 2 + 1), sp_.k[:, (i // 2 - 1) * 2 + g, :], LAT, False)
                for i in (2, 4) for g in range(2)])
    token_major(net, [(w, [(kv(3, 0), P), (kv(5, 0), P)], [(t * P, P, sp_.v[:, t, :]) for t in range(4)])], 256)
    gates_and_decays(net, sp_)
    compress(net, sp_)

    buf = net.ring.rearrange("p s n -> p (s n)")
    at = [0]

    def take(n):
        at[0] += n
        return buf[:, at[0] - n:at[0]]

    keys = take(2 * LAT).rearrange("p (w t) -> p w t", w=2)
    k_cmp = take(N_CMP)
    bias_cmp = take(16 * N_CMP).rearrange("p (q h n) -> p q h n", q=4, h=4)
    gates = take(48).rearrange("p (q n) -> p q n", q=4)
    v_cmp = take(DH)[0:N_CMP]
    bias = take(4 * LAT).rearrange("p (h n) -> p h n", h=4)

    def copies(g):
        return ([lambda i=i: nc.gpsimd.tensor_copy(keys[:, i:i + 1, :], sp_.k[:, bass.ds(2 * i + g, 1), :]) for i in range(2)]
                + [lambda: nc.gpsimd.tensor_copy(k_cmp, sp_.k_cmp[:, bass.ds(g * N_CMP, N_CMP)])]
                + [lambda q=q: nc.gpsimd.tensor_copy(bias_cmp[:, q].rearrange("p h n -> p n h"), sp_.cmp_bias[:, q, :, bass.ds(g * 4, 4)])
                   for q in range(4)]
                + [lambda: nc.gpsimd.tensor_copy(gates, sp_.gates[:, :, bass.ds(g * 12, 12)]),
                   lambda: nc.gpsimd.tensor_copy(v_cmp, sp_.v_cmp[:, bass.ds(g * DH, DH)])])

    def units(g):
        out = []
        for pair in range(2):
            for qt in range(4):
                for b in range(2):
                    h, half = 2 * pair + b, slice(b * DH, (b + 1) * DH)
                    gate = lambda n: gates[:, qt, 3 * h + n:3 * h + n + 1]
                    dyn = lambda ap, first: None if g is None else ap[:, bass.ds(g * DH + first, DH)]
                    out.append(Unit(pair, b, qt, [(0, N_CMP, k_cmp[half, :])], [(0, N_CMP, bias_cmp[:, qt, h, :])],
                                    [(0, N_CMP, v_cmp)], gate=gate(0), first=True, last=False))
                    n = (qt + 1) * P
                    for i in range(2):
                        out.append(Unit(pair, b, qt, [(LAT - n, n, keys[half, i, 0:n])], [(LAT - n, LAT, bias[:, h, LAT - n:LAT])],
                                        [(LAT - n + j * P, P, dyn(sp_.v[:, j, :], i * P)) for j in range(qt + 1)],
                                        gate=gate(i + 1), first=False, last=(i == 1)))
        return out

    biases = lambda g: [(bias, net.rel_bias[bass.ds(g * 4, 4)].rearrange("h p n -> p h n"))]
    attention(net, 2, sp_.q, copies, biases, units, buf[:, at[0]:], sp_.ya)


def short_convolution(net, sp_):
    nc, d = net.nc, net.dram
    N, TAPS = 12, 4
    slabs = [slab_loads(d["w_in_2"][0], [(IN_DN + n * P, P)]) for n in range(N)]
    counts = slab_counts(slabs)
    padded = net.work[:, 0:2 * 516].rearrange("p (s n) -> p s n", s=2)
    sums = net.work[:, 1032:1032 + 2 * LAT].rearrange("p (s n) -> p s n", s=2)
    names = [f"slab_in{s}" for s in range(RING)] + ["product", "padded_zero", "copied", "convolved", "silu_done", "tap"]
    with net.stage(*names) as (block, *sems):
        slab_in, (product, padded_zero, copied, convolved, silu_done, tap) = sems[:RING], sems[RING:]

        @block.sync
        def _(sp):
            load_slabs(net, sp, slabs, KD, P, slab_in, product)

        @block.tensor
        def _(pe):
            for n in range(N):
                pe.wait_ge(slab_in[n % RING], counts[n])
                if n >= 4:
                    pe.wait_ge(copied, n - 3)
                for k in range(KD):
                    mm = nc.tensor.matmul(net.ps[:, n % 4, :], ring_slab(net, n % RING, KD, P)[:, k, :], net.a[:, k, 0:LAT],
                                          start=(k == 0), stop=(k == KD - 1))
                mm.then_inc(product, 1)

        @block.scalar
        def _(act):
            act.wait_ge(padded_zero, 1)
            for n in range(N + 1):
                if n < N:
                    act.wait_ge(product, n + 1)
                    if n >= 2:
                        act.wait_ge(convolved, n - 1)
                    nc.scalar.activation(padded[:, n % 2, 3:3 + LAT], net.ps[:, n % 4, :], ACT.Copy).then_inc(copied, 1)
                if n >= 1:
                    act.wait_ge(convolved, n)
                    nc.scalar.activation(sp_.qkv[:, n - 1, :], sums[:, (n - 1) % 2, :], ACT.Silu).then_inc(silu_done, 1)

        @block.vector
        def _(dve):
            nc.vector.memset(padded, 0.0).then_inc(padded_zero, 1)
            for n in range(N):
                dve.wait_ge(copied, n + 1)
                if n >= 2:
                    dve.wait_ge(silu_done, n - 1)
                weight = lambda j: net.vt[:, 2, V_CONV + j * 12 + n:V_CONV + j * 12 + n + 1]
                to = sums[:, n % 2, :]
                nc.vector.tensor_scalar(to, padded[:, n % 2, 3:3 + LAT], weight(3), None, ALU.mult).then_inc(tap, 1)
                for m, j in enumerate((2, 1, 0)):
                    dve.wait_ge(tap, 3 * n + m + 1)
                    nc.vector.scalar_tensor_tensor(out=to, in0=padded[:, n % 2, j:j + LAT], scalar=weight(j), in1=to, op0=ALU.mult,
                                                   op1=ALU.add).then_inc(tap if m < 2 else convolved, 1)

    with net.stage("squared", "summed", "sum_out", "ln_done", "rstd_done", "newton_step", "normed") as (
            block, squared, summed, sum_out, ln_done, rstd_done, newton_step, normed):
        sq = net.work[:, 0:2 * LAT].rearrange("p (s n) -> p s n", s=2)
        ln, rstd = net.work[:, 2 * LAT:3 * LAT], net.work[:, 3 * LAT:5 * LAT].rearrange("p (s n) -> p s n", s=2)
        total, temp = net.work[:, 5 * LAT:6 * LAT], net.work[:, 6 * LAT:7 * LAT]

        @block.scalar
        def _(act):
            for n in range(8):
                if n >= 2:
                    act.wait_ge(summed, n - 1)
                nc.scalar.activation(sq[:, n % 2, :], sp_.qkv[:, n, :], ACT.Square).then_inc(squared, 1)
                act.wait_ge(sum_out, n + 1)
                if n >= 1:
                    act.wait_ge(rstd_done, n)
                nc.scalar.activation(ln, total, ACT.Ln).then_inc(ln_done, 1)
                act.wait_ge(ln_done, n + 1)
                if n >= 2:
                    act.wait_ge(normed, n - 1)
                nc.scalar.activation(rstd[:, n % 2, :], ln, ACT.Exp, scale=-0.5).then_inc(rstd_done, 1)

        @block.tensor
        def _(pe):
            for n in range(8):
                pe.wait_ge(squared, n + 1)
                if n >= 2:
                    pe.wait_ge(sum_out, n - 1)
                nc.tensor.matmul(net.ps[:, n % 2, :], net.c("blk64"), sq[:, n % 2, :], start=True, stop=True).then_inc(summed, 1)

        @block.vector
        def _(dve):
            for n in range(8):
                dve.wait_ge(summed, n + 1)
                nc.vector.tensor_scalar(total, net.ps[:, n % 2, :], 1.0, EPS, ALU.mult, ALU.add).then_inc(sum_out, 1)
                dve.wait_ge(rstd_done, n + 1)
                newton(nc, dve, rstd[:, n % 2, :], total, temp, newton_step, 3 * n)
                nc.vector.scalar_tensor_tensor(out=sp_.qkv[:, n, :], in0=sp_.qkv[:, n, :], scalar=SCALE if n < 4 else 1.0,
                                               in1=rstd[:, n % 2, :], op0=ALU.mult, op1=ALU.mult).then_inc(normed, 1)


def delta_net(net, sp_):
    nc = net.nc
    buf = net.ring.rearrange("p s n -> p (s n)")
    at = [0]

    def take(*shape):
        n = int(np.prod(shape))
        at[0] += n
        ap = buf[:, at[0] - n:at[0]]
        return ap.rearrange("p (h n) -> p h n", h=shape[0]) if len(shape) == 2 else ap

    LEVELS = 6
    k_bd, q_bd, v_bd, low_bd, attn_bd, out_bd = (take(4, P) for _ in range(6))
    state = take(4, CHUNK)
    zeroed_part = buf[:, 0:at[0]]
    lev = take(LEVELS, P)
    kq = take(8, CHUNK)
    kdec_bd, mask_x, inv, inv_t, w2 = (take(4, P) for _ in range(5))
    diag_gc, dist, decay, low_beta, temp, rhs, v_new, mixed = (take(4, CHUNK) for _ in range(8))
    scal = take(5, 4)
    sq = take(4, CHUNK)
    rowsum, ln, rstd, temp4 = take(4), take(4), take(4), take(4)
    beta, gc, eg, el, egl = (scal[:, n, :] for n in range(5))
    bank = lambda n, w=P: net.ps[:, n, 0:4 * w].rearrange("p (h n) -> p h n", h=4)
    kq_ps = net.ps[:, 1, :].rearrange("p (w h n) -> p w h n", w=2, h=4)
    over = lambda ap, w=CHUNK: ap.unsqueeze(2).to_broadcast([P, 4, w])
    pairs = lambda ap, w=CHUNK: ap.unsqueeze(1).to_broadcast([P, 4, w])
    halves = [(slice(0, DH), slice(0, DH)), (slice(DH, P), slice(DH, P))]
    NF, NL = 12, 14
    names = ("tables_in", "zeroed", "fixed", "chunk_free", "diag_ready", "running", "dist_ready", "decayed", "grams", "keys_turned",
             "values_turned", "state_read", "low_ready", "masked", "inverse_ready", "w2_done", "w2_copied", "level_done", "attn_ready",
             "kdec_ready", "rhs_ready", "solved", "v_new_ready", "chunk_products", "sums_ready", "ln_done", "rstd_ready", "out_ready",
             "turned", "out_stored", "link", "dist_abs")
    with net.stage(*names) as (block, tables_in, zeroed, fixed, chunk_free, diag_ready, running, dist_ready, decayed, grams,
                               keys_turned, values_turned, state_read, low_ready, masked, inverse_ready, w2_done, w2_copied,
                               level_done, attn_ready, kdec_ready, rhs_ready, solved, v_new_ready, chunk_products, sums_ready,
                               ln_done, rstd_ready, out_ready, turned, out_stored, link, dist_abs):

        @block.sync
        def _(sp):
            sp.dma_start(lev.rearrange("p h n -> p (h n)"), net.extra("lev")).then_inc(tables_in, 16)

        @block.gpsimd
        def _(pool):
            nc.gpsimd.memset(zeroed_part, 0.0).then_inc(zeroed, 1)
            pool.wait_ge(zeroed, 1)
            with pool.Fori(0, 8) as c:
                pool.wait_ge(chunk_free, c + 1)
                pool.wait_ge(out_stored, c + 1)
                tok = bass.ds(c * CHUNK, CHUNK)
                for rows, cols in halves:
                    for bd, first in ((q_bd, 0), (k_bd, 4), (v_bd, 8)):
                        nc.gpsimd.tensor_copy(bd[rows, :, cols], sp_.qkv[rows, first:first + 4, tok]).then_inc(fixed, 1)
                    nc.gpsimd.tensor_copy(kq[rows, 0:4, :], sp_.qkv[rows, 4:8, tok]).then_inc(fixed, 1)
                    nc.gpsimd.tensor_copy(kq[rows, 4:8, :], sp_.qkv[rows, 0:4, tok]).then_inc(fixed, 1)
                    nc.gpsimd.tensor_copy(scal[rows].unsqueeze(2), sp_.small[rows, :, bass.ds(c, 1), :]).then_inc(fixed, 1)

        @block.tensor
        def _(pe):
            def products(to, lhs, rhs_of, signal):
                for h in range(4):
                    mm = nc.tensor.matmul(to[:, h], lhs[:, h, :], rhs_of(h), start=True, stop=True)
                if signal is not None:
                    mm.then_inc(signal, 1)

            with pe.Fori(0, 8) as c:
                pe.wait_ge(fixed, (c + 1) * NF)
                pair_kq = kq.rearrange("p (w h) n -> p w h n", w=2)
                for h in range(4):
                    mm = nc.tensor.matmul(kq_ps[:, :, h, :], k_bd[:, h, :], pair_kq[:, :, h, :], start=True, stop=True)
                mm.then_inc(grams, 1)
                for h in range(4):
                    mm = nc.tensor.transpose(bank(2)[:, h], k_bd[:, h, :], net.c("ident"))
                mm.then_inc(keys_turned, 1)
                products(bank(3, CHUNK), v_bd, lambda h: net.c("eye2"), values_turned)
                pe.wait_ge(diag_ready, c + 1)
                nc.tensor.matmul(bank(0, CHUNK), net.c("blk64"), diag_gc, start=True, stop=True).then_inc(running, 1)
                products(bank(4, CHUNK), k_bd, lambda h: state[:, h, :], None)
                products(bank(5, CHUNK), q_bd, lambda h: state[:, h, :], state_read)
                for n in range(LEVELS):
                    pe.wait_ge(masked, c * LEVELS + (n + 1))
                    pe.wait_ge(inverse_ready, c * (LEVELS + 1) + (n + 1))
                    products(bank(6), mask_x, lambda h: inv_t[:, h, :], w2_done)
                    pe.wait_ge(w2_copied, c * LEVELS + (n + 1))
                    last = n == LEVELS - 1
                    products(bank(7), inv, lambda h: w2[:, h, :], level_done if last else None)
                    if not last:
                        products(bank(0), w2, lambda h: inv[:, h, :], level_done)
                pe.wait_ge(rhs_ready, c + 1)
                pe.wait_ge(inverse_ready, (c + 1) * (LEVELS + 1))
                products(bank(3, CHUNK), inv_t, lambda h: rhs[:, h, :], solved)
                pe.wait_ge(kdec_ready, c + 1)
                pe.wait_ge(attn_ready, c + 1)
                pe.wait_ge(v_new_ready, c + 1)
                products(bank(2, CHUNK), kdec_bd, lambda h: v_new[:, h, :], None)
                products(bank(4, CHUNK), attn_bd, lambda h: v_new[:, h, :], chunk_products)
                pe.wait_ge(out_ready, c + 1)
                products(bank(1, CHUNK), out_bd, lambda h: net.c("eye2"), turned)

        @block.scalar
        def _(act):
            act.sem_inc(out_stored, 1)
            with act.Fori(0, 8) as c:
                act.wait_ge(dist_ready, c + 1)
                nc.scalar.activation(decay, dist, ACT.Abs).then_inc(dist_abs, 1)
                act.wait_ge(dist_abs, c + 1)
                nc.scalar.activation(decay, decay, ACT.Exp, scale=-1.0).then_inc(decayed, 1)
                for n in range(LEVELS):
                    act.wait_ge(w2_done, c * LEVELS + (n + 1))
                    nc.scalar.activation(w2, bank(6), ACT.Copy).then_inc(w2_copied, 1)
                act.wait_ge(sums_ready, c + 1)
                nc.scalar.activation(ln, rowsum, ACT.Ln).then_inc(ln_done, 1)
                act.wait_ge(ln_done, c + 1)
                nc.scalar.activation(rstd, ln, ACT.Exp, scale=-0.5).then_inc(rstd_ready, 1)
                act.wait_ge(turned, c + 1)
                nc.scalar.activation(sp_.yb[:, :, bass.ds(c * CHUNK, CHUNK)], bank(1, CHUNK), ACT.Copy).then_inc(out_stored, 1)

        @block.vector
        def _(dve):
            dve.sem_inc(chunk_free, 1)
            dve.wait_ge(tables_in, 16)
            dve.wait_ge(zeroed, 1)
            with dve.Fori(0, 8) as c:
                links = 0

                def linked(ins):
                    nonlocal links
                    links += 1
                    ins.then_inc(link, 1)
                    dve.wait_ge(link, c * NL + links)

                v = nc.vector
                dve.wait_ge(fixed, (c + 1) * NF)
                v.tensor_tensor(diag_gc, pairs(net.c("eye2")), over(gc), ALU.mult).then_inc(diag_ready, 1)
                v.tensor_tensor(low_beta, pairs(net.c("low")), over(beta), ALU.mult)
                v.tensor_copy(inv, pairs(net.c("ident"), P))
                v.tensor_copy(inv_t, pairs(net.c("ident"), P)).then_inc(inverse_ready, 1)
                dve.wait_ge(running, c + 1)
                v.tensor_tensor(dist, bank(0, CHUNK), over(gc), ALU.subtract).then_inc(dist_ready, 1)
                dve.wait_ge(grams, c + 1)
                dve.wait_ge(decayed, c + 1)
                linked(v.tensor_tensor(temp, kq_ps[:, 0], decay, ALU.mult))
                for rows, cols in halves:
                    ins = v.tensor_tensor(low_bd[rows, :, cols], temp[rows], low_beta[rows], ALU.mult)
                ins.then_inc(low_ready, 1)
                dve.wait_ge(low_ready, c + 1)
                v.tensor_tensor(mask_x, low_bd, pairs(lev[:, 0, :], P), ALU.mult).then_inc(masked, 1)
                for n in range(LEVELS):
                    if n == 0:
                        linked(v.tensor_tensor(temp, kq_ps[:, 1], decay, ALU.mult))
                        for rows, cols in halves:
                            ins = v.tensor_tensor(attn_bd[rows, :, cols], temp[rows], pairs(net.c("tri"))[rows], ALU.mult)
                        ins.then_inc(attn_ready, 1)
                        dve.wait_ge(attn_ready, c + 1)
                    if n == 1:
                        dve.wait_ge(keys_turned, c + 1)
                        v.tensor_tensor(kdec_bd, bank(2), over(el, P), ALU.mult).then_inc(kdec_ready, 1)
                    if n == 2:
                        dve.wait_ge(state_read, c + 1)
                        linked(v.tensor_tensor(temp, bank(4, CHUNK), over(eg), ALU.mult))
                        dve.wait_ge(values_turned, c + 1)
                        linked(v.tensor_tensor(temp, bank(3, CHUNK), temp, ALU.subtract))
                        v.tensor_tensor(rhs, temp, over(beta), ALU.mult).then_inc(rhs_ready, 1)
                    if n < LEVELS - 1:
                        dve.wait_ge(w2_done, c * LEVELS + (n + 1))
                        v.tensor_tensor(mask_x, low_bd, pairs(lev[:, n + 1, :], P), ALU.mult).then_inc(masked, 1)
                    dve.wait_ge(level_done, c * LEVELS + (n + 1))
                    ins = v.tensor_tensor(inv_t, inv_t, bank(7), ALU.subtract)
                    if n < LEVELS - 1:
                        ins = v.tensor_tensor(inv, inv, bank(0), ALU.subtract)
                    ins.then_inc(inverse_ready, 1)
                    if n < LEVELS - 1:
                        dve.wait_ge(inverse_ready, c * (LEVELS + 1) + (n + 2))
                dve.wait_ge(solved, c + 1)
                v.tensor_copy(v_new, bank(3, CHUNK)).then_inc(v_new_ready, 1)
                linked(v.tensor_tensor(state, state, over(egl), ALU.mult))
                dve.wait_ge(rhs_ready, c + 1)
                linked(v.tensor_tensor(temp, bank(5, CHUNK), over(eg), ALU.mult))
                dve.wait_ge(chunk_products, c + 1)
                v.tensor_tensor(state, state, bank(2, CHUNK), ALU.add)
                linked(v.tensor_tensor(mixed, temp, bank(4, CHUNK), ALU.add))
                linked(v.tensor_tensor(sq, mixed, mixed, ALU.mult))
                linked(v.tensor_reduce(rowsum, sq, AX.X, ALU.add))
                v.tensor_scalar(rowsum, rowsum, 1.0 / DH, EPS, ALU.mult, ALU.add).then_inc(sums_ready, 1)
                dve.wait_ge(rstd_ready, c + 1)
                newton(nc, dve, rstd, rowsum, temp4, link, c * NL + links)
                links += 3
                for rows, cols in halves:
                    ins = v.tensor_tensor(out_bd[rows, :, cols], mixed[rows], over(rstd)[rows], ALU.mult)
                ins.then_inc(out_ready, 1)
                assert links <= NL, links
                dve.wait_ge(out_ready, c + 1)
                if links < NL:
                    dve.sem_inc(link, NL - links)
                dve.sem_inc(chunk_free, 1)


def merge_branches(net, sp_):
    nc, d = net.nc, net.dram
    w = d["w_in_2"][0]
    slabs = [slab_loads(w, [(IN_Z + n * P, P)]) for n in range(4)]
    counts = slab_counts(slabs)
    silu = net.work[:, 0:2 * LAT].rearrange("p (s n) -> p s n", s=2)
    names = [f"slab_in{s}" for s in range(RING)] + ["product", "silu_done", "gated"]
    with net.stage(*names) as (block, *sems):
        slab_in, (product, silu_done, gated) = sems[:RING], sems[RING:]

        @block.sync
        def _(sp):
            load_slabs(net, sp, slabs, KD, P, slab_in, product)

        @block.tensor
        def _(pe):
            for n in range(4):
                pe.wait_ge(slab_in[n], counts[n])
                for k in range(KD):
                    mm = nc.tensor.matmul(net.ps[:, n, :], ring_slab(net, n, KD, P)[:, k, :], net.a[:, k, 0:LAT], start=(k == 0), stop=(k == KD - 1))
                mm.then_inc(product, 1)

        @block.scalar
        def _(act):
            for n in range(4):
                act.wait_ge(product, n + 1)
                if n >= 2:
                    act.wait_ge(gated, n - 1)
                nc.scalar.activation(silu[:, n % 2, :], net.ps[:, n, :], ACT.Silu).then_inc(silu_done, 1)

        @block.vector
        def _(dve):
            for n in range(4):
                dve.wait_ge(silu_done, n + 1)
                nc.vector.scalar_tensor_tensor(out=sp_.yb[:, n, :], in0=sp_.yb[:, n, :], scalar=net.vt[:, 2, V_GAIN + G_DN:V_GAIN + G_DN + 1],
                                               in1=silu[:, n % 2, :], op0=ALU.mult, op1=ALU.mult).then_inc(gated, 1)

    wv = w.rearrange("(k p) n -> p k n", p=P)
    branch = [d[f"w_branch_{x}_2"][0].rearrange("(k p) n -> p k n", p=P) for x in "ab"]
    gate = net.work[:, 0:4 * LAT].rearrange("p (s n) -> p s n", s=4)
    parts = net.work[:, 4 * LAT:6 * LAT].rearrange("p (s n) -> p s n", s=2)
    names = [f"slab_in{s}" for s in range(RING)] + ["product", "sigmoid_done", "weighted", "merged"]
    with net.stage(*names) as (block, *sems):
        slab_in, (product, sigmoid_done, weighted, merged) = sems[:RING], sems[RING:]

        @block.sync
        def _(sp):
            for n in range(KD):
                for s in range(RING):
                    if n:
                        sp.wait_ge(product, 4 * (n - 1) + s + 1)
                    if s < 2:
                        first = IN_MERGE + s * D + n * P
                        sp.dma_start(ring_slab(net, s, KD, P), wv[:, :, first:first + P]).then_inc(slab_in[s], 16)
                    else:
                        sp.dma_start(ring_slab(net, s, 4, P), branch[s - 2][:, :, n * P:(n + 1) * P]).then_inc(slab_in[s], 16)

        @block.tensor
        def _(pe):
            for n in range(KD):
                for s in range(RING):
                    pe.wait_ge(slab_in[s], 16 * (n + 1))
                    if n >= 2:
                        pe.wait_ge(merged, n - 1)
                    depth, src = (KD, net.a) if s < 2 else (4, (sp_.ya, sp_.yb)[s - 2])
                    for k in range(depth):
                        mm = nc.tensor.matmul(net.ps[:, 4 * (n % 2) + s, :], ring_slab(net, s, depth, P)[:, k, :], src[:, k, 0:LAT],
                                              start=(k == 0), stop=(k == depth - 1))
                    mm.then_inc(product, 1)

        @block.scalar
        def _(act):
            for n in range(KD):
                for s in range(2):
                    act.wait_ge(product, 4 * n + s + 1)
                    if n >= 2:
                        act.wait_ge(merged, n - 1)
                    nc.scalar.activation(gate[:, 2 * (n % 2) + s, :], net.ps[:, 4 * (n % 2) + s, :], ACT.Sigmoid).then_inc(sigmoid_done, 1)

        @block.vector
        def _(dve):
            for n in range(KD):
                for s in range(2):
                    dve.wait_ge(product, 4 * n + s + 3)
                    dve.wait_ge(sigmoid_done, 2 * n + s + 1)
                    if n:
                        dve.wait_ge(merged, n)
                    nc.vector.tensor_tensor(parts[:, s, :], gate[:, 2 * (n % 2) + s, :], net.ps[:, 4 * (n % 2) + 2 + s, :], ALU.mult).then_inc(weighted, 1)
                dve.wait_ge(weighted, 2 * n + 2)
                nc.vector.tensor_tensor(sp_.merged[:, n, :], parts[:, 0, :], parts[:, 1, :], ALU.add).then_inc(merged, 1)


def route(net, sp_):
    nc, d = net.nc, net.dram
    net.expert_weights = nc.dram_tensor("expert_weights", (N_EXP, LAT), F32, kind="Internal").ap()
    at = [0]

    def take(*shape):
        n = int(np.prod(shape))
        at[0] += n
        ap = net.work[:, at[0] - n:at[0]]
        return ap.rearrange("p (t n) -> p t n", t=4) if n > 4 else ap

    rw = net.ring[:, 0, 0:KD * N_EXP].rearrange("p (k n) -> p k n", k=KD)
    rb = net.ring[:, 1, 0:N_EXP]
    score, sel, duo, group, best, hit, index, masked, one, two, weight = (
        take(4, N_EXP), take(4, N_EXP), take(4, 24), take(4, 4), take(4), take(4, N_EXP), take(4, N_EXP), take(4, N_EXP),
        take(4, N_EXP), take(4, N_EXP), take(4, N_EXP))
    group_one = take(4, 4)
    rows = net.work[0:N_EXP, 1024:1024 + LAT]
    iota = lambda n: net.c("iota16")[:, 0:n].unsqueeze(1).to_broadcast([P, 4, n])
    wide = lambda ap, n: ap.unsqueeze(2).to_broadcast([P, 4, n])
    with net.stage("weights_in", "logits", "scored", "link", "turned", "rows_done", "stored") as (
            block, weights_in, logits, scored, link, turned, rows_done, stored):
        @block.sync
        def _(sp):
            sp.dma_start(rw, d["router_w_2"].rearrange("(k p) n -> p k n", p=P)).then_inc(weights_in, 16)
            sp.dma_start(rb, d["router_b_2"].partition_broadcast(P)).then_inc(weights_in, 16)
            sp.wait_ge(rows_done, 1)
            sp.dma_start(net.expert_weights, rows).then_inc(stored, 16)
            sp.wait_ge(stored, 16)

        @block.tensor
        def _(pe):
            pe.wait_ge(weights_in, 32)
            for t in range(4):
                for k in range(KD):
                    mm = nc.tensor.matmul(net.ps[:, 0, t * N_EXP:(t + 1) * N_EXP], net.a[:, k, t * P:(t + 1) * P], rw[:, k, :],
                                          start=(k == 0), stop=(k == KD - 1))
            mm.then_inc(logits, 1)
            pe.wait_ge(link, LINKS)
            for t in range(4):
                mm = nc.tensor.transpose(net.ps[0:N_EXP, 1, t * P:(t + 1) * P], weight[:, t, :], net.c("ident"))
            mm.then_inc(turned, 1)

        @block.scalar
        def _(act):
            act.wait_ge(logits, 1)
            nc.scalar.activation(score, net.ps[:, 0, 0:4 * N_EXP].rearrange("p (t n) -> p t n", t=4), ACT.Sigmoid).then_inc(scored, 1)

        @block.vector
        def _(dve):
            v = nc.vector
            links = 0

            def linked(ins):
                nonlocal links
                links += 1
                ins.then_inc(link, 1)
                dve.wait_ge(link, links)

            def first_best(values, n, to):
                linked(v.tensor_reduce(best, values, AX.X, ALU.max))
                linked(v.tensor_tensor(hit[:, :, 0:n], values, wide(best, n), ALU.is_equal))
                linked(v.tensor_scalar(hit[:, :, 0:n], hit[:, :, 0:n], -99.0, 99.0, ALU.mult, ALU.add))
                linked(v.tensor_tensor(index[:, :, 0:n], hit[:, :, 0:n], iota(n), ALU.add))
                linked(v.tensor_reduce(best, index[:, :, 0:n], AX.X, ALU.min))
                linked(v.tensor_tensor(to, iota(n), wide(best, n), ALU.is_equal))

            dve.wait_ge(scored, 1)
            linked(v.tensor_tensor(sel, score, rb.unsqueeze(1).to_broadcast([P, 4, N_EXP]), ALU.add))
            member = sel.rearrange("p t (g e) -> p t g e", g=4)
            sums = duo.rearrange("p t (g s) -> p t g s", g=4)
            for s, (i, j) in enumerate(((0, 1), (0, 2), (0, 3), (1, 2), (1, 3), (2, 3))):
                ins = v.tensor_tensor(sums[:, :, :, s], member[:, :, :, i], member[:, :, :, j], ALU.add)
            linked(ins)
            linked(v.tensor_reduce(group, sums, AX.X, ALU.max))
            first_best(group, 4, group_one)
            spread = masked.rearrange("p t (g e) -> p t g e", g=4)
            chosen = group_one.unsqueeze(3).to_broadcast([P, 4, 4, 4])
            linked(v.tensor_tensor(spread, member, chosen, ALU.mult))
            linked(v.tensor_scalar(group_one, group_one, -1.0, 1e30, ALU.add, ALU.mult))
            linked(v.tensor_tensor(spread, spread, chosen, ALU.add))
            first_best(masked, N_EXP, one)
            linked(v.scalar_tensor_tensor(out=masked, in0=one, scalar=-2e30, in1=masked, op0=ALU.mult, op1=ALU.add))
            first_best(masked, N_EXP, two)
            linked(v.tensor_tensor(one, one, two, ALU.add))
            linked(v.tensor_tensor(weight, one, score, ALU.mult))
            linked(v.tensor_reduce(best, weight, AX.X, ALU.add))
            linked(v.reciprocal(best, best))
            linked(v.tensor_tensor(weight, weight, wide(best, N_EXP), ALU.mult))
            assert links == LINKS, links
            dve.wait_ge(turned, 1)
            v.tensor_copy(rows, net.ps[0:N_EXP, 1, :]).then_inc(rows_done, 1)


LINKS = 30


def experts(net):
    nc, d = net.nc, net.dram
    HC = D_EXP // P
    SIZE = 2 * KD * D_EXP + HC * D
    place = [net.arena[:, n * SIZE:(n + 1) * SIZE] for n in range(2)]
    wg = [p[:, 0:KD * D_EXP].rearrange("p (k n) -> p k n", k=KD) for p in place]
    wu = [p[:, KD * D_EXP:2 * KD * D_EXP].rearrange("p (k n) -> p k n", k=KD) for p in place]
    wd = [p[:, 2 * KD * D_EXP:].rearrange("p (k n) -> p k n", k=HC) for p in place]
    rest = net.arena[:, 2 * SIZE:]
    hidden = rest[:, 0:HC * LAT].rearrange("p (k n) -> p k n", k=HC)
    weight = rest[:, HC * LAT:HC * LAT + 2 * LAT].rearrange("p (s n) -> p s n", s=2)
    silu = net.work[:, 0:2 * LAT].rearrange("p (s n) -> p s n", s=2)
    up = net.work[:, 2 * LAT:4 * LAT].rearrange("p (s n) -> p s n", s=2)
    mats = [d[n][0].rearrange("e (k p) n -> e p k n", p=P) for n in ("moe_w_gate_2", "moe_w_up_2", "moe_w_down_2")]
    TURNS = N_EXP // 2
    names = ("expert_in0", "expert_in1", "up_done", "silu_done", "weighted", "hidden_done", "down_done", "added", "expert_done")
    with net.stage(*names) as (block, in0, in1, up_done, silu_done, weighted, hidden_done, down_done, added, expert_done):
        expert_in = (in0, in1)

        @block.sync
        def _(sp):
            with sp.Fori(0, TURNS) as i:
                for s in range(2):
                    sp.wait_ge(expert_done, i * 2 + (s + 1))
                    e = bass.ds(i * 2 + s, 1)
                    for dst, src in zip((wg[s], wu[s], wd[s]), mats):
                        sp.dma_start(dst.unsqueeze(1), src[e].rearrange("e p k n -> p e k n")).then_inc(expert_in[s], 16)
                    sp.dma_start(weight[:, s, :].unsqueeze(1), net.expert_weights[e].partition_broadcast(P)).then_inc(expert_in[s], 16)

        @block.tensor
        def _(pe):
            with pe.Fori(0, TURNS) as i:
                for s in range(2):
                    pe.wait_ge(expert_in[s], (i + 1) * 64)
                    for f in range(HC):
                        pe.wait_ge(hidden_done, i * (2 * HC) + (s * HC + f + 1))
                        for b, w in enumerate((wg[s], wu[s])):
                            for k in range(KD):
                                mm = nc.tensor.matmul(net.ps[:, 2 * (f % 2) + b, :], w[:, k, f * P:(f + 1) * P], net.a[:, k, 0:LAT],
                                                      start=(k == 0), stop=(k == KD - 1))
                            mm.then_inc(up_done, 1)
                    pe.wait_ge(hidden_done, i * (2 * HC) + (s * HC + HC + 2))
                    for n in range(KD):
                        pe.wait_ge(added, i * (2 * KD) + (s * KD + n + 1))
                        for k in range(HC):
                            mm = nc.tensor.matmul(net.ps[:, 4 + n % 4, :], wd[s][:, k, n * P:(n + 1) * P], hidden[:, k, :],
                                                  start=(k == 0), stop=(k == HC - 1))
                        mm.then_inc(down_done, 1)

        @block.scalar
        def _(act):
            with act.Fori(0, TURNS) as i:
                for s in range(2):
                    for f in range(HC):
                        act.wait_ge(up_done, i * (4 * HC) + (s * 2 * HC + 2 * f + 1))
                        act.wait_ge(hidden_done, i * (2 * HC) + (s * HC + f + 1))
                        nc.scalar.activation(silu[:, f % 2, :], net.ps[:, 2 * (f % 2), :], ACT.Silu).then_inc(silu_done, 1)

        @block.vector
        def _(dve):
            dve.sem_inc(hidden_done, 2)
            dve.sem_inc(added, 4)
            dve.sem_inc(expert_done, 2)
            with dve.Fori(0, TURNS) as i:
                for s in range(2):
                    dve.wait_ge(expert_in[s], (i + 1) * 64)
                    for f in range(HC):
                        n = s * HC + f
                        dve.wait_ge(silu_done, i * (2 * HC) + (n + 1))
                        nc.vector.tensor_tensor(up[:, f % 2, :], silu[:, f % 2, :], weight[:, s, :], ALU.mult).then_inc(weighted, 1)
                        dve.wait_ge(weighted, i * (2 * HC) + (n + 1))
                        dve.wait_ge(up_done, i * (4 * HC) + (2 * n + 2))
                        nc.vector.tensor_tensor(hidden[:, f, :], up[:, f % 2, :], net.ps[:, 2 * (f % 2) + 1, :], ALU.mult).then_inc(hidden_done, 1)
                    for n in range(KD):
                        dve.wait_ge(down_done, i * (2 * KD) + (s * KD + n + 1))
                        if n == 0:
                            dve.wait_ge(added, i * (2 * KD) + (s * KD + 4))
                        nc.vector.scalar_tensor_tensor(out=net.h[:, n, 0:LAT], in0=net.ps[:, 4 + n % 4, :], scalar=gate_of(net, 2, 5, n, 0),
                                                       in1=net.h[:, n, 0:LAT], op0=ALU.mult, op1=ALU.add).then_inc(added, 1)
                    dve.wait_ge(added, i * (2 * KD) + (s * KD + KD + 4))
                    dve.sem_inc(expert_done, 1)


def second_block(net, upto=9):
    d, sp_ = net.dram, Sparse(net)
    modulate(net, 2, 0, (7,), LAT)
    sparse_attention(net, sp_)
    short_convolution(net, sp_)
    delta_net(net, sp_)
    merge_branches(net, sp_)
    project_back(net, d["w_out_2"][0], KD, lambda k: sp_.merged[:, k, :], 2, 2, LAT)
    if upto > 2:
        modulate(net, 2, 3, (8,), LAT)
        route(net, sp_)
        experts(net)

INPUTS = ["x", "c", "ctx", "c_ctx", "w_ada", "b_ada", "g_mix", "g_ffn", "w_gate_up", "w_down", "swa_w_qkv", "swa_g_q", "swa_g_k",
          "swa_sink", "swa_w_o", "na_w_qkv", "na_g_q", "na_g_k", "na_rpb", "na_w_o", "c_2", "rel_bias_2", "router_w_2",
          "router_b_2", "ada_w_2", "ada_b_2", "norm1_g_2", "norm2_g_2", "w_in_2", "qk_norm_g_2", "cmp_pos_2", "cmp_w1_2",
          "cmp_w2_2", "dn_conv_w_2", "dn_a_log_2", "dn_dt_bias_2", "dn_norm_g_2", "w_branch_a_2", "w_branch_b_2", "w_out_2",
          "moe_w_gate_2", "moe_w_up_2", "moe_w_down_2"]


def kernel(**inputs):
    import concourse.bacc as bacc
    from concourse.bass_utils import run_bass_kernel_spmd

    nc = bacc.Bacc("TRN2", target_bir_lowering=False, num_devices=1)
    t = tables()
    arrays = {f"in_{name}": np.ascontiguousarray(inputs[name]) for name in INPUTS}
    arrays["in_tables"] = np.concatenate([t[n] for n in RESIDENT], 1)
    arrays["in_more_tables"] = np.concatenate([t[n] for n in LOADED], 1)
    dram = {name[3:]: nc.dram_tensor(name, a.shape, F32, kind="ExternalInput").ap() for name, a in arrays.items()}
    out = nc.dram_tensor("out_x", (1, LAT, D), F32, kind="ExternalOutput").ap()
    program(nc, dram, out)
    got = run_bass_kernel_spmd(nc, [arrays], core_ids=[0])
    return got.results[0]["out_x"]
```

```python
from contextlib import ExitStack, contextmanager

import numpy as np

import concourse.bass as bass
from concourse import mybir

ALU = mybir.AluOpType
ACT = mybir.ActivationFunctionType
AX = mybir.AxisListType
F32 = mybir.dt.float32
I32 = mybir.dt.int32

P = 128
D = 1024
KD = D // P
LAT = 512
CTX = 256
TOK = LAT + CTX
D_FF = 2816
KF = D_FF // P
DH = 64
SCALE = DH ** -0.5
EPS = 1e-6
NEG = -1e30
GRID_W = 64
SWA_KV = 4
BAND = 3 * P
RING = 4
SLAB = KF * P
BANK = 512
N_EXP = 16
D_EXP = 512
BLOCKS = 2 * LAT // P + N_EXP
CHUNK = 64
N_CMP = LAT // 16 - 1
GDN_H = 8

IN_Q, IN_KV, IN_GATE, IN_DN, IN_BETA, IN_Z, IN_MERGE = 0, 512, 1280, 1304, 2840, 2856, 3368


def bucket(dist):
    exact = 16
    far = np.maximum(dist, exact).astype(np.float32)
    large = exact + (np.log(far / np.float32(exact)) / np.float32(np.log(1024 / exact)) * np.float32(32 - exact)).astype(np.int32)
    return np.where(dist < exact, np.maximum(dist, 0), np.minimum(large, 31))


def tables():
    out = {}
    out["ident"] = np.eye(P)
    out["ones"] = np.ones((P, P))
    i = np.arange(P)
    out["blk64"] = (i[:, None] // DH == i[None, :] // DH)
    rot = np.zeros((P, P))
    for m in range(P):
        if m % 32 < 16:
            rot[m + 16, m] = -1.0
        else:
            rot[m - 16, m] = 1.0
    out["rot"] = rot
    t = np.arange(LAT)
    freqs = np.float32(10000.0) ** (-np.arange(16, dtype=np.float32) / np.float32(16))
    pos = np.where((i[:, None] % DH) < 32, t[None, :] // GRID_W, t[None, :] % GRID_W).astype(np.float32)
    ang = (pos * freqs[i % 16][:, None]).astype(np.float32)
    out["cos"], out["sin"] = np.cos(ang), np.sin(ang)
    j = np.arange(BAND)
    out["swa_mask"] = np.where(np.abs(i[:, None] + P - j[None, :]) <= P, 0.0, NEG / SCALE)
    na = np.zeros((P, 3, BAND))
    for kind, cb in enumerate((0, 1, 3)):
        qc = 16 * cb + i % 16
        start = np.clip(qc - 8, 0, GRID_W - 16)
        kc = 16 * (cb + j // P - 1) + j % 16
        ok = (kc[None, :] >= start[:, None]) & (kc[None, :] < start[:, None] + 16)
        na[:, kind] = np.where(ok, 0.0, NEG / SCALE)
    out["na_mask"] = na.reshape(P, 3 * BAND)
    a = i % CHUNK
    same = i[:, None] // CHUNK == i[None, :] // CHUNK
    lev = np.zeros((P, 6, P))
    for n in range(6):
        s = 1 << n
        lev[:, n] = same & (a[:, None] // (2 * s) == a[None, :] // (2 * s)) & (a[:, None] // s % 2 == 1) & (a[None, :] // s % 2 == 0)
    out["lev"] = lev.reshape(P, -1)
    half = np.arange(CHUNK)
    out["tri"] = a[:, None] <= half[None, :]
    out["low"] = a[:, None] > half[None, :]
    out["eye2"] = a[:, None] == half[None, :]
    out["last2"] = same & (a[:, None] == CHUNK - 1)
    out["cmp_ok"] = (np.arange(4)[None, :] * P + i[:, None] >= 31)
    out["eps"] = np.full((P, 1), EPS)
    out["iota16"] = np.arange(16) + np.zeros((P, 1))
    out["upper"] = i[:, None] < i[None, :]
    out["blocks"] = np.arange(BLOCKS) + np.zeros((P, 1))
    out["tokens"] = np.arange(4)[None, :] * P + i[:, None]
    def hot(dist):
        o = np.zeros((P, dist.size))
        o[:32] = (bucket(dist)[None, :] == np.arange(32)[:, None]) & (dist >= 0)[None, :]
        o[32] = dist < 0
        return o
    out["hot_rev"] = hot(511 - np.arange(640))
    out["hot_fwd"] = hot(np.arange(992) - 511)
    return {k: np.ascontiguousarray(v, np.float32) for k, v in out.items()}


RESIDENT = ["ident", "ones", "blk64", "rot", "cos", "sin", "tri", "low", "eye2", "last2", "cmp_ok", "iota16", "eps"]
LOADED = ["upper", "blocks", "tokens", "lev", "swa_mask", "na_mask", "hot_rev", "hot_fwd"]


def pack(names):
    t = tables()
    at, where = 0, {}
    for n in names:
        where[n] = (at, t[n].shape[1])
        at += t[n].shape[1]
    return where, at


class Net:

    def __init__(self, nc, ctx, dram):
        self.nc, self.dram, self.stages, self.used = nc, dram, 0, []
        sb = lambda name, shape: ctx.enter_context(nc.sbuf_tensor(name, shape, F32))
        self.h = sb("residual", [P, KD, TOK])
        self.a = sb("normed", [P, KD, TOK])
        self.arena = sb("arena", [P, RING * SLAB + KF * TOK])
        self.ring = self.arena[:, 0:RING * SLAB].rearrange("p (s n) -> p s n", s=RING)
        self.big = self.arena[:, RING * SLAB:]
        self.where, n = pack(RESIDENT)
        self.extras, _ = pack(LOADED)
        self.const = sb("const", [P, n])
        self.vt = sb("vectors", [P, 3, P])
        self.mod = sb("mods", [P, 3, 48, 2])
        self.vec = sb("scales", [P, 9, KD])
        self.cond = sb("cond", [P, 3, KD, 2])
        self.work = sb("work", [P, 3840])
        self.share = sb("shares", [P, 4, 2])
        self.slot_tokens = sb("slot_tokens", [P, BLOCKS + 2])
        integers = lambda name, shape: ctx.enter_context(nc.sbuf_tensor(name, shape, I32))
        self.slots = integers("slots", [P, 8])
        self.block_expert = integers("block_expert", [P, BLOCKS])
        self.rows_wanted = integers("rows_wanted", [P, 2])
        self.ps = ctx.enter_context(nc.psum_tensor("ps", [P, 8, BANK], F32))

    def c(self, name, rows=P):
        at, n = self.where[name]
        return self.const[0:rows, at:at + n]

    def extra(self, name, rows=P):
        at, n = self.extras[name]
        return self.dram["more_tables"][0:rows, at:at + n]

    @contextmanager
    def stage(self, *names):
        self.stages += 1
        sems = [self.nc.alloc_semaphore(f"{n}_{self.stages}") for n in names]
        if self.used:
            self.nc.clear_and_free_semaphores(self.used)
        with self.nc.Block() as block:
            yield (block, *sems)
        self.used = sems


def newton(nc, dve, rstd, mean, temp, step, at):
    nc.vector.tensor_tensor(temp, rstd, rstd, ALU.mult).then_inc(step, 1)
    dve.wait_ge(step, at + 1)
    nc.vector.scalar_tensor_tensor(out=temp, in0=temp, scalar=-0.5, in1=mean, op0=ALU.mult, op1=ALU.mult).then_inc(step, 1)
    dve.wait_ge(step, at + 2)
    nc.vector.scalar_tensor_tensor(out=rstd, in0=temp, scalar=1.5, in1=rstd, op0=ALU.add, op1=ALU.mult).then_inc(step, 1)
    dve.wait_ge(step, at + 3)


V_BADA, V_GMIX, V_GFFN = 0, 96, 112
V_ADA2, V_N1, V_N2, V_C, V_CC, V_C2 = 0, 48, 56, 64, 72, 80
V_CONV, V_GAIN, V_POS = 0, 48, 57
G_SWA_Q, G_SWA_K, G_NA_Q, G_NA_K, G_QK0, G_DN = 0, 1, 2, 3, 4, 8


def load_inputs(net):
    nc, d = net.nc, net.dram
    rows = net.work[:, 0:3 * P].rearrange("p (s n) -> p s n", s=3)
    xin = net.big[:, 0:4 * D].rearrange("p (t n) -> p t n", t=4)
    cin = net.big[:, 4 * D:6 * D].rearrange("p (t n) -> p t n", t=2)
    names = ("tables_in", "rows_in", "tokens_in", "rows_zero", "turned", "copied", "vecs_done", "silu_done")
    with net.stage(*names) as (block, tables_in, rows_in, tokens_in, rows_zero, turned, copied, vecs_done, silu_done):
        fold = lambda ap: ap.rearrange("(r n) -> r n", n=P)
        loads = [
            (rows[0:96, 0, :], d["b_ada"].rearrange("l (r n) -> (l r) n", n=P)),
            (rows[96:112, 0, :], d["g_mix"].rearrange("l (r n) -> (l r) n", n=P)),
            (rows[112:128, 0, :], d["g_ffn"].rearrange("l (r n) -> (l r) n", n=P)),
            (rows[0:48, 1, :], fold(d["ada_b_2"][0])),
            (rows[48:56, 1, :], fold(d["norm1_g_2"][0])),
            (rows[56:64, 1, :], fold(d["norm2_g_2"][0])),
            (rows[64:72, 1, :], fold(d["c"][0])),
            (rows[72:80, 1, :], fold(d["c_ctx"])),
            (rows[80:88, 1, :], fold(d["c_2"][0])),
            (rows[0:48, 2, :], d["dn_conv_w_2"][0].rearrange("j (r n) -> (j r) n", n=P)),
            (rows[57:121, 2, 0:DH], d["cmp_pos_2"][0].rearrange("i j n -> (i j) n")),
        ]
        for half in range(2):
            cols = slice(half * DH, half * DH + DH)
            loads += [
                (rows[48:49, 2, cols], d["swa_g_q"]),
                (rows[49:50, 2, cols], d["swa_g_k"]),
                (rows[50:51, 2, cols], d["na_g_q"]),
                (rows[51:52, 2, cols], d["na_g_k"]),
                (rows[52:56, 2, cols], d["qk_norm_g_2"][0]),
                (rows[56:57, 2, cols], d["dn_norm_g_2"]),
            ]

        @block.sync
        def _(sp):
            sp.dma_start(net.const[:], d["tables"]).then_inc(tables_in, 16)
            sp.dma_start(xin, d["x"][0].rearrange("(t p) n -> p t n", p=P)).then_inc(tokens_in, 16)
            sp.dma_start(cin, d["ctx"][0].rearrange("(t p) n -> p t n", p=P)).then_inc(tokens_in, 16)

        @block.gpsimd
        def _(pool):
            nc.gpsimd.memset(rows[:], 0.0).then_inc(rows_zero, 1)

        @block.scalar
        def _(act):
            act.wait_ge(rows_zero, 1)
            for dst, src in loads:
                act.dma_start(dst, src).then_inc(rows_in, 16)
            for g in range(1, 16, 2):
                act.wait_ge(turned, 3 + g + 1)
                n = 4 if g < 8 else 2
                dst = net.h[:, g % 8, 0:LAT] if g < 8 else net.h[:, g % 8, LAT:TOK]
                nc.scalar.activation(dst, net.ps[:, g % 8, 0:n * P], ACT.Copy).then_inc(copied, 1)
            act.wait_ge(vecs_done, 3)
            for n, at in enumerate((V_C, V_CC, V_C2, V_C2)):
                l = 2 if n >= 2 else 0
                for ll in ((0, 1) if n < 2 else (2,)):
                    nc.scalar.activation(net.cond[:, ll, :, n % 2], net.vt[:, 1, at:at + KD], ACT.Silu).then_inc(silu_done, 1)

        @block.tensor
        def _(pe):
            pe.wait_ge(tables_in, 16)
            pe.wait_ge(rows_in, 16 * len(loads))
            for s in range(3):
                nc.tensor.transpose(net.ps[:, s, 0:P], rows[:, s, :], net.c("ident")).then_inc(turned, 1)
            pe.wait_ge(tokens_in, 32)
            for g in range(16):
                if g < 3:
                    pe.wait_ge(vecs_done, g + 1)
                if g >= 8:
                    pe.wait_ge(copied, 8)
                src, n = (xin, 4) if g < 8 else (cin, 2)
                for t in range(n):
                    mm = nc.tensor.transpose(net.ps[:, g % 8, t * P:(t + 1) * P], src[:, t, (g % 8) * P:(g % 8 + 1) * P], net.c("ident"))
                mm.then_inc(turned, 1)

        @block.vector
        def _(dve):
            for s in range(3):
                dve.wait_ge(turned, s + 1)
                nc.vector.tensor_copy(net.vt[:, s, :], net.ps[:, s, 0:P]).then_inc(vecs_done, 1)
            for g in range(0, 16, 2):
                dve.wait_ge(turned, 3 + g + 1)
                n = 4 if g < 8 else 2
                dst = net.h[:, g % 8, 0:LAT] if g < 8 else net.h[:, g % 8, LAT:TOK]
                nc.vector.tensor_copy(dst, net.ps[:, g % 8, 0:n * P]).then_inc(copied, 1)


class Biases:

    NAMES = ("params_in", "cleared", "scaled", "rel_done", "rel_copied", "table_out", "tiles_out")

    def __init__(self, net):
        nc, self.net = net.nc, net
        self.na_table = nc.dram_tensor("na_table", (16, 15 * 64), F32, kind="Internal").ap()
        self.rel_table = nc.dram_tensor("rel_table", (8, 640), F32, kind="Internal").ap()
        net.na_bias = nc.dram_tensor("na_bias", (16, 16, 15 * 48), F32, kind="Internal").ap()
        net.rel_bias = nc.dram_tensor("rel_bias_tiles", (8, P, LAT), F32, kind="Internal").ap()
        self.raw = net.work[0:16, 0:15 * 31].rearrange("p (r c) -> p r c", c=31)
        self.wide = net.work[0:16, 512:512 + 15 * 64].rearrange("p (r c) -> p r c", c=64)
        self.rel = net.work[0:32, 1600:1608]
        self.rel_far = net.work[0:33, 1608:1616]
        self.hot = net.work[0:33, 1616:2256]
        self.rel_rows = net.work[0:8, 2256:2896]
        self.parts = ((0, 512), (512, 640))

    def transfers(self, act, params_in, scaled, rel_copied, table_out, tiles_out):
        net = self.net
        act.dma_start(self.raw, net.dram["na_rpb"][0]).then_inc(params_in, 16)
        act.dma_start(self.rel, net.dram["rel_bias_2"]).then_inc(params_in, 16)
        act.dma_start(self.hot, net.extra("hot_rev", 33)).then_inc(params_in, 16)
        act.wait_ge(scaled, 2)
        act.dma_start(self.na_table, self.wide.rearrange("p r c -> p (r c)")).then_inc(table_out, 16)
        act.wait_ge(rel_copied, 2)
        act.dma_start(self.rel_table, self.rel_rows).then_inc(table_out, 16)
        act.wait_ge(table_out, 32)
        for dr in range(15):
            src = bass.AP(self.na_table.tensor, dr * 64 + 15, [[960, 16], [-1, 16], [1, 48]])
            act.dma_start(net.na_bias[:, :, dr * 48:(dr + 1) * 48], src).then_inc(tiles_out, 16)
        src = bass.AP(self.rel_table.tensor, P - 1, [[640, 8], [-1, P], [1, LAT]])
        act.dma_start(net.rel_bias, src).then_inc(tiles_out, 16)
        act.wait_ge(tiles_out, 16 * 16)

    def scale(self, dve, cleared, params_in, scaled):
        net, v = self.net, self.net.nc.vector
        v.memset(net.work[0:16, 512:512 + 15 * 64], 0.0)
        v.memset(self.rel_far, NEG / SCALE).then_inc(cleared, 1)
        dve.wait_ge(cleared, 1)
        dve.wait_ge(params_in, 48)
        v.tensor_scalar(self.wide[:, :, 16:47], self.raw, 1.0 / SCALE, None, ALU.mult).then_inc(scaled, 1)
        v.tensor_scalar(self.rel_far[0:32], self.rel, 1.0 / SCALE, None, ALU.mult).then_inc(scaled, 1)

    def rows(self, dve, rel_done, rel_copied):
        net, v = self.net, self.net.nc.vector
        for n, (lo, hi) in enumerate(self.parts):
            dve.wait_ge(rel_done, n + 1)
            v.tensor_copy(self.rel_rows[:, lo:hi], net.ps[0:8, 7, 0:hi - lo]).then_inc(rel_copied, 1)

    def products(self, pe, scaled, rel_done, rel_copied):
        net = self.net
        pe.wait_ge(scaled, 2)
        for n, (lo, hi) in enumerate(self.parts):
            if n:
                pe.wait_ge(rel_copied, n)
            net.nc.tensor.matmul(net.ps[0:8, 7, 0:hi - lo], self.rel_far, self.hot[:, lo:hi], start=True, stop=True).then_inc(rel_done, 1)


def modulation(net):
    nc, d = net.nc, net.dram
    WIDE = 256
    STEPS = 6 * D // WIDE // RING
    GROUPS = STEPS * RING
    mats = [d["w_ada"][0], d["w_ada"][1], d["ada_w_2"][0]]
    slab = lambda s: net.ring[:, s, 0:KD * WIDE].rearrange("p (k n) -> p k n", k=KD)
    rows = [net.big[0:2, n * 6 * D:(n + 1) * 6 * D] for n in range(2)]
    biases = Biases(net)
    with net.stage(*[f"ada_in{s}" for s in range(RING)], "slab_used", "row_copied", "rows_turned", "mod_done",
                   *Biases.NAMES) as (block, *sems):
        ada_in, (slab_used, row_copied, rows_turned, mod_done) = sems[:RING], sems[RING:RING + 4]
        params_in, cleared, scaled, rel_done, rel_copied, table_out, tiles_out = sems[RING + 4:]

        @block.sync
        def _(sp):
            for l, w in enumerate(mats):
                wv = w.rearrange("(k p) n -> p k n", p=P)
                for s in range(RING):
                    if l:
                        sp.wait_ge(slab_used, (l * STEPS - 1) * RING + s + 1)
                    sp.dma_start(slab(s), wv[:, :, s * WIDE:(s + 1) * WIDE]).then_inc(ada_in[s], 16)
                with sp.Fori(1, STEPS) as i:
                    for s in range(RING):
                        sp.wait_ge(slab_used, (i + (l * STEPS - 1)) * RING + s + 1)
                        sp.dma_start(slab(s), wv[:, :, bass.ds((i * RING + s) * WIDE, WIDE)]).then_inc(ada_in[s], 16)

        @block.scalar
        def _(act):
            biases.transfers(act, params_in, scaled, rel_copied, table_out, tiles_out)

        @block.tensor
        def _(pe):
            for l in range(3):
                with pe.Fori(0, STEPS) as i:
                    for s in range(RING):
                        pe.wait_ge(ada_in[s], (i + (l * STEPS + 1)) * 16)
                        pe.wait_ge(row_copied, (i + l * STEPS) * RING + (s + 1))
                        for n, k in enumerate((1, 3, 5, 7, 0, 2, 4, 6)):
                            mm = nc.tensor.matmul(net.ps[0:2, s, 0:WIDE], net.cond[:, l, k, :], slab(s)[:, k, :],
                                                  start=(n == 0), stop=(n == KD - 1))
                        mm.then_inc(slab_used, 1)
                if l == 0:
                    biases.products(pe, scaled, rel_done, rel_copied)
                pe.wait_ge(row_copied, (l + 1) * GROUPS + RING)
                for n in range(6 * KD):
                    mm = nc.tensor.transpose(net.ps[:, 4 + l, 2 * n:2 * n + 2], rows[l % 2][:, n * P:(n + 1) * P], net.c("ident")[0:2, 0:2])
                mm.then_inc(rows_turned, 1)

        @block.vector
        def _(dve):
            dve.sem_inc(row_copied, RING)
            biases.scale(dve, cleared, params_in, scaled)
            for l in range(3):
                if l >= 2:
                    dve.wait_ge(rows_turned, l - 1)
                with dve.Fori(0, STEPS) as i:
                    for s in range(RING):
                        dve.wait_ge(slab_used, (i + l * STEPS) * RING + (s + 1))
                        nc.vector.tensor_scalar(rows[l % 2][:, bass.ds((i * RING + s) * WIDE, WIDE)], net.ps[0:2, s, 0:WIDE],
                                                1.0, None, ALU.mult).then_inc(row_copied, 1)
                if l == 0:
                    biases.rows(dve, rel_done, rel_copied)
            for l in range(3):
                dve.wait_ge(rows_turned, l + 1)
                bias = net.vt[:, 0, l * 48:(l + 1) * 48] if l < 2 else net.vt[:, 1, V_ADA2:V_ADA2 + 48]
                for w in range(2):
                    nc.vector.tensor_tensor(net.mod[:, l, :, w], net.ps[:, 4 + l, 0:96].rearrange("p (n w) -> p n w", w=2)[:, :, w],
                                            bias, ALU.add).then_inc(mod_done, 1)
            dve.wait_ge(mod_done, 6)
            for n, (l, w, j, gain) in enumerate(SCALES):
                g = net.vt[:, gain[0], gain[1]:gain[1] + KD]
                nc.vector.scalar_tensor_tensor(out=net.vec[:, n, :], in0=net.mod[:, l, j * KD:(j + 1) * KD, w],
                                               scalar=1.0, in1=g, op0=ALU.add, op1=ALU.mult)


SCALES = [
    (0, 0, 1, (0, V_GMIX)), (0, 1, 1, (0, V_GMIX)), (0, 0, 4, (0, V_GFFN)), (0, 1, 4, (0, V_GFFN)),
    (1, 0, 1, (0, V_GMIX + KD)), (1, 1, 1, (0, V_GMIX + KD)), (1, 0, 4, (0, V_GFFN + KD)),
    (2, 0, 1, (1, V_N1)), (2, 0, 4, (1, V_N2)),
]


def by_column_block(ap):
    return ap.rearrange("p (r b c) -> p r b c", b=4, c=16)


def modulate(net, layer, shift, scales, tokens, permute=False):
    nc = net.nc
    sq = net.work[:, 0:2 * TOK].rearrange("p (s n) -> p s n", s=2)
    ln, rstd, mean = (net.work[:, n * TOK:n * TOK + tokens] for n in (2, 3, 4))
    segs = [(0, LAT)] + ([(LAT, TOK)] if tokens > LAT else [])
    with net.stage("squared", "summed", "mean_done", "ln_done", "rstd_done", "newton_step", "scaled") as (
            block, squared, summed, mean_done, ln_done, rstd_done, newton_step, scaled):
        sums = net.ps[:, 0:2, :].rearrange("p b n -> p (b n)")[:, 0:tokens]

        @block.scalar
        def _(act):
            for c in range(KD):
                if c >= 2:
                    act.wait_ge(summed, c - 1)
                nc.scalar.activation(sq[:, c % 2, 0:tokens], net.h[:, c, 0:tokens], ACT.Square).then_inc(squared, 1)
            act.wait_ge(mean_done, 1)
            nc.scalar.activation(ln, mean, ACT.Ln).then_inc(ln_done, 1)
            act.wait_ge(ln_done, 1)
            nc.scalar.activation(rstd, ln, ACT.Exp, scale=-0.5).then_inc(rstd_done, 1)
            for c in range(KD):
                act.wait_ge(scaled, c + 1)
                for n, (lo, hi) in enumerate(segs):
                    nc.scalar.activation(net.a[:, c, lo:hi], net.a[:, c, lo:hi], ACT.Identity,
                                         scale=net.vec[:, scales[n], c:c + 1],
                                         bias=net.mod[:, layer, shift * KD + c, n:n + 1])

        @block.tensor
        def _(pe):
            for c in range(KD):
                pe.wait_ge(squared, c + 1)
                for lo, hi in segs:
                    mm = nc.tensor.matmul(sums[:, lo:hi], net.c("ones"), sq[:, c % 2, lo:hi], start=(c == 0), stop=(c == KD - 1))
                mm.then_inc(summed, 1)

        @block.vector
        def _(dve):
            dve.wait_ge(summed, KD)
            nc.vector.tensor_scalar(mean, sums, 1.0 / D, EPS, ALU.mult, ALU.add).then_inc(mean_done, 1)
            dve.wait_ge(rstd_done, 1)
            newton(nc, dve, rstd, mean, sq[:, 0, 0:tokens], newton_step, 0)
            for c in range(KD):
                if permute:
                    dst = net.a[:, c, 0:LAT].rearrange("p (b r c) -> p r b c", r=8, c=16)
                    mm = nc.vector.tensor_tensor(dst, by_column_block(net.h[:, c, 0:LAT]), by_column_block(rstd[:, 0:LAT]), ALU.mult)
                    if tokens > LAT:
                        mm = nc.vector.tensor_tensor(net.a[:, c, LAT:TOK], net.h[:, c, LAT:TOK], rstd[:, LAT:TOK], ALU.mult)
                else:
                    mm = nc.vector.tensor_tensor(net.a[:, c, 0:tokens], net.h[:, c, 0:tokens], rstd[:, 0:tokens], ALU.mult)
                mm.then_inc(scaled, 1)


def slab_loads(w, columns):
    wv = w.rearrange("(k p) n -> p k n", p=P)
    out, at = [], 0
    for first, count in columns:
        out.append((at, count, wv[:, :, first:first + count]))
        at += count
    return out


def ring_slab(net, slot, k, n):
    return net.ring[:, slot, 0:k * n].rearrange("p (k n) -> p k n", k=k)


def load_slabs(net, sp, slabs, k, width, loaded, slab_used):
    for n, loads in enumerate(slabs):
        if n >= RING:
            sp.wait_ge(slab_used, n - RING + 1)
        for at, count, src in loads:
            sp.dma_start(ring_slab(net, n % RING, k, width)[:, :, at:at + count], src).then_inc(loaded[n % RING], 16)


def slab_counts(slabs):
    total, out = [0] * RING, []
    for n, loads in enumerate(slabs):
        total[n % RING] += 16 * len(loads)
        out.append(total[n % RING])
    return out


def heads_qk(net, jobs):
    nc = net.nc
    N = len(jobs)
    slabs = [slab_loads(w, cols) for w, cols, *_ in jobs]
    counts = slab_counts(slabs)
    sq = net.work[:, 0:2 * TOK].rearrange("p (s n) -> p s n", s=2)
    ln = net.work[:, 2 * TOK:3 * TOK]
    rstd = net.work[:, 3 * TOK:5 * TOK].rearrange("p (s n) -> p s n", s=2)
    scaled = net.ring[:, 0, KD * P:KD * P + 2 * LAT].rearrange("p (s n) -> p s n", s=2)
    by_cos = net.ring[:, 1, KD * P:KD * P + LAT]
    by_sin = net.ring[:, 1, KD * P + LAT:KD * P + 2 * LAT]
    proj = lambda n: net.ps[:, 2 * (n % 2):2 * (n % 2) + 2, :].rearrange("p b n -> p (b n)")
    sums = net.ps[:, 4:6, :].rearrange("p b n -> p (b n)")
    turned = net.ps[:, 6, :]
    mean, temp = (net.ring[:, s, KD * P:KD * P + TOK] for s in (2, 3))
    names = [f"slab_in{s}" for s in range(RING)] + ["slab_used", "squared", "summed", "mean_done", "ln_done", "rstd_done",
                                                    "newton_step", "normed", "rotated", "sin_done", "cos_done", "roped"]
    rope_before = [sum(j[5] for j in jobs[:n]) for n in range(N + 1)]
    with net.stage(*names) as (block, *sems):
        slab_in, (slab_used, squared, summed, mean_done, ln_done, rstd_done, newton_step, normed, rotated, sin_done, cos_done, roped) = sems[:RING], sems[RING:]

        @block.sync
        def _(sp):
            load_slabs(net, sp, slabs, KD, P, slab_in, slab_used)

        @block.tensor
        def _(pe):
            def sum_and_turn(n):
                if 1 <= n <= N:
                    m, t = n - 1, jobs[n - 1][4]
                    pe.wait_ge(squared, m + 1)
                    if m >= 1:
                        pe.wait_ge(mean_done, m)
                    for lo in range(0, t, LAT):
                        hi = min(lo + LAT, t)
                        mm = nc.tensor.matmul(sums[:, lo:hi], net.c("blk64"), sq[:, m % 2, lo:hi], start=True, stop=True)
                    mm.then_inc(summed, 1)
                if n >= 2 and jobs[n - 2][5]:
                    m = n - 2
                    pe.wait_ge(normed, m + 1)
                    if rope_before[m]:
                        pe.wait_ge(sin_done, rope_before[m])
                    nc.tensor.matmul(turned, net.c("rot"), scaled[:, m % 2, :], start=True, stop=True).then_inc(rotated, 1)

            for n in range(N):
                pe.wait_ge(slab_in[n % RING], counts[n])
                if n >= 2:
                    pe.wait_ge(normed, n - 1)
                w, t = ring_slab(net, n % RING, KD, P), jobs[n][4]
                for k in range(KD):
                    if k == 2:
                        sum_and_turn(n)
                    for lo in range(0, t, LAT):
                        hi = min(lo + LAT, t)
                        mm = nc.tensor.matmul(proj(n)[:, lo:hi], w[:, k, :], net.a[:, k, lo:hi], start=(k == 0), stop=(k == KD - 1))
                mm.then_inc(slab_used, 1)
            sum_and_turn(N)
            sum_and_turn(N + 1)

        @block.scalar
        def _(act):
            def square(n):
                act.wait_ge(slab_used, n + 1)
                if n >= 2:
                    act.wait_ge(summed, n - 1)
                t = jobs[n][4]
                nc.scalar.activation(sq[:, n % 2, 0:t], proj(n)[:, 0:t], ACT.Square).then_inc(squared, 1)

            square(0)
            for n in range(N):
                t = jobs[n][4]
                act.wait_ge(mean_done, n + 1)
                if n >= 1:
                    act.wait_ge(rstd_done, n)
                nc.scalar.activation(ln[:, 0:t], mean[:, 0:t], ACT.Ln).then_inc(ln_done, 1)
                act.wait_ge(ln_done, n + 1)
                if n >= 2:
                    act.wait_ge(normed, n - 1)
                nc.scalar.activation(rstd[:, n % 2, 0:t], ln[:, 0:t], ACT.Exp, scale=-0.5).then_inc(rstd_done, 1)
                if n + 1 < N:
                    square(n + 1)

        @block.vector
        def _(dve):
            def by_sine(m):
                dve.wait_ge(rotated, rope_before[m] + 1)
                if rope_before[m]:
                    dve.wait_ge(roped, rope_before[m])
                nc.vector.tensor_tensor(by_sin, turned, net.c("sin"), ALU.mult).then_inc(sin_done, 1)

            for n in range(N):
                _, _, gain, dst, t, rope = jobs[n]
                dve.wait_ge(summed, n + 1)
                nc.vector.tensor_scalar(mean[:, 0:t], sums[:, 0:t], 1.0 / DH, EPS, ALU.mult, ALU.add).then_inc(mean_done, 1)
                dve.wait_ge(rstd_done, n + 1)
                newton(nc, dve, rstd[:, n % 2, 0:t], mean[:, 0:t], temp[:, 0:t], newton_step, 3 * n)
                if rope and rope_before[n] >= 2:
                    dve.wait_ge(cos_done, rope_before[n] - 1)
                    dve.wait_ge(rotated, rope_before[n] - 1)
                spans = [(0, LAT, scaled[:, n % 2, :])] if rope else [(0, LAT, dst[:, 0:LAT])]
                if t > LAT:
                    spans.append((LAT, t, dst[:, LAT:t]))
                for lo, hi, to in spans:
                    mm = nc.vector.scalar_tensor_tensor(out=to, in0=proj(n)[:, lo:hi], scalar=gain, in1=rstd[:, n % 2, lo:hi],
                                                        op0=ALU.mult, op1=ALU.mult)
                mm.then_inc(normed, 1)
                if n >= 1 and jobs[n - 1][5]:
                    by_sine(n - 1)
            if jobs[N - 1][5]:
                by_sine(N - 1)

        @block.gpsimd
        def _(pool):
            for n in range(N):
                if jobs[n][5]:
                    pool.wait_ge(normed, n + 1)
                    if rope_before[n]:
                        pool.wait_ge(roped, rope_before[n])
                    nc.gpsimd.tensor_tensor(by_cos, scaled[:, n % 2, :], net.c("cos"), ALU.mult).then_inc(cos_done, 1)
                    pool.wait_ge(cos_done, rope_before[n] + 1)
                    pool.wait_ge(sin_done, rope_before[n] + 1)
                    nc.gpsimd.tensor_tensor(jobs[n][3][:, 0:LAT], by_cos, by_sin, ALU.add).then_inc(roped, 1)


def token_major(net, jobs, width, func=ACT.Copy):
    nc = net.nc
    slabs = [slab_loads(w, cols) for w, cols, _ in jobs]
    counts = slab_counts(slabs)
    names = [f"slab_in{s}" for s in range(RING)] + ["slab_used", "tile_done", "even_out", "odd_out"]
    with net.stage(*names) as (block, *sems):
        slab_in, (slab_used, tile_done, even_out, odd_out) = sems[:RING], sems[RING:]
        tiles = [(n, t, m, dst) for n, (_, _, ts) in enumerate(jobs) for t, m, dst in ts]
        n_cols = [sum(c for _, c in cols) for _, cols, _ in jobs]

        @block.sync
        def _(sp):
            load_slabs(net, sp, slabs, KD, width, slab_in, slab_used)

        @block.tensor
        def _(pe):
            for i, (n, t, m, _) in enumerate(tiles):
                if i == 0 or tiles[i - 1][0] != n:
                    pe.wait_ge(slab_in[n % RING], counts[n])
                if i >= 8:
                    pe.wait_ge(even_out if i % 2 == 0 else odd_out, (i - 8) // 2 + 1)
                for k in range(KD):
                    mm = nc.tensor.matmul(net.ps[0:m, i % 8, 0:n_cols[n]], net.a[:, k, t:t + m],
                                          ring_slab(net, n % RING, KD, width)[:, k, 0:n_cols[n]], start=(k == 0), stop=(k == KD - 1))
                mm.then_inc(tile_done, 1)
                if i + 1 == len(tiles) or tiles[i + 1][0] != n:
                    pe.wait_ge(tile_done, i + 1)
                    pe.sem_inc(slab_used, 1)

        @block.scalar
        def _(act):
            for i in range(0, len(tiles), 2):
                n, _, m, dst = tiles[i]
                act.wait_ge(tile_done, i + 1)
                nc.scalar.activation(dst, net.ps[0:m, i % 8, 0:n_cols[n]], func).then_inc(even_out, 1)

        @block.vector
        def _(dve):
            for i in range(1, len(tiles), 2):
                n, _, m, dst = tiles[i]
                dve.wait_ge(tile_done, i + 1)
                nc.vector.tensor_copy(dst, net.ps[0:m, i % 8, 0:n_cols[n]]).then_inc(odd_out, 1)


class Unit:

    def __init__(self, pair, b, qt, keys, biased, blocks, start=None, gate=None, first=True, last=True, ready=None):
        self.pair, self.b, self.qt, self.keys, self.biased, self.blocks = pair, b, qt, keys, biased, blocks
        self.start, self.gate, self.first, self.last = start, gate, first, last
        self.ready = ready
        self.lo, self.hi = keys[0][0], keys[-1][0] + keys[-1][1]
        self.steps = 2 + (start is not None) + (gate is not None)


def attention(net, groups, q_in, copies, biases, make_units, buf, out, early):
    nc = net.nc
    at = [0]

    def take(*shape):
        n = int(np.prod(shape))
        ap = buf[:, at[0]:at[0] + n]
        at[0] += n
        return ap if len(shape) == 1 else ap.rearrange("p (s n) -> p s n", s=shape[0])

    qs = take(2, q_in.shape[2])
    probs, turned_probs = take(2, TOK), take(2, 5 * P)
    mixed_heads = take(2, P)
    stats = take(4, 10)
    units = make_units(None)
    NU = len(units)
    NS = sum(u.steps for u in units)
    ends = [n for n, u in enumerate(units) if u.b == 1 and u.last]
    NE = len(ends)
    NC = len(copies(0)) + 1
    NB = len(biases(0))
    scores = lambda n: net.ps[:, 2 * (n % 2):2 * (n % 2) + 2, :].rearrange("p b n -> p (b n)")
    turn = net.ps[:, 4:6, :].rearrange("p b n -> p (b n)")
    mix, back = net.ps[:, 6, 0:DH], net.ps[:, 7, 0:P]
    gated = any(u.gate is not None for u in units)
    names = ("fixed_ready", "bias_free", "bias_in", "products_free", "vector_free", "scalar_free", "scored", "maxed", "exped", "probs_turned", "probs_copied",
             "mixed", "step", "head_scaled", "heads_turned", "heads_out")
    with net.stage(*names) as (block, fixed_ready, bias_free, bias_in, products_free, vector_free, scalar_free, scored, maxed, exped, probs_turned,
                               probs_copied, mixed, step, head_scaled, heads_turned, heads_out):

        @block.sync
        def _(sp):
            if NB:
                with sp.Fori(0, groups) as g:
                    sp.wait_ge(bias_free, g + 1)
                    for dst, src in biases(g):
                        sp.dma_start(dst, src).then_inc(bias_in, 16)

        @block.gpsimd
        def _(pool):
            if NB and not gated:
                pool.sem_inc(bias_free, 1)
            with pool.Fori(0, groups) as g:
                pool.wait_ge(products_free, g + 1)
                if gated:
                    pool.wait_ge(vector_free, g + 1)
                    pool.wait_ge(scalar_free, g + 1)
                    pool.wait_ge(bias_in, (g + 1) * 16 * NB)
                nc.gpsimd.tensor_copy(qs, q_in[:, bass.ds(2 * g, 2), :]).then_inc(fixed_ready, 1)
                ops = copies(g)
                for op in ops[0:early - 1]:
                    op().then_inc(fixed_ready, 1)
                if not gated:
                    pool.wait_ge(vector_free, g + 1)
                    pool.wait_ge(scalar_free, g + 1)
                if NB and not gated:
                    pool.wait_ge(bias_in, (g + 1) * 16 * NB)
                for op in ops[early - 1:]:
                    op().then_inc(fixed_ready, 1)
                if NB and not gated:
                    pool.wait_ge(fixed_ready, (g + 1) * NC)
                    pool.sem_inc(bias_free, 1)

        @block.tensor
        def _(pe):
            pe.sem_inc(products_free, 1)
            with pe.Fori(0, groups) as g:
                valued = make_units(g)
                pe.wait_ge(fixed_ready, g * NC + early)
                for s in range(NU + 3):
                    if s < NU:
                        u = units[s]
                        if s >= 2:
                            pe.wait_ge(maxed, g * NU + (s - 1))
                        for lo, n, key in u.keys:
                            mm = nc.tensor.matmul(scores(s)[:, lo:lo + n], qs[u.b * DH:(u.b + 1) * DH, u.pair, u.qt * P:(u.qt + 1) * P],
                                                  key, start=True, stop=True)
                        mm.then_inc(scored, 1)
                    if 1 <= s <= NU:
                        n, u = s - 1, units[s - 1]
                        pe.wait_ge(exped, g * NU + (n + 1))
                        if s == NU and not gated:
                            pe.sem_inc(products_free, 1)
                        if n >= 1:
                            pe.wait_ge(probs_copied, g * NU + n)
                        for j, (lo, w, _) in enumerate(u.blocks):
                            mm = nc.tensor.transpose(turn[0:w, j * P:(j + 1) * P], probs[:, n % 2, lo:lo + w], net.c("ident"))
                        mm.then_inc(probs_turned, 1)
                    if 2 <= s <= NU + 1:
                        n, u = s - 2, units[s - 2]
                        values = valued[n].blocks
                        pe.wait_ge(probs_copied, g * NU + (n + 1))
                        if n >= 1:
                            pe.wait_ge(head_scaled, g * NU + n)
                        for j, (_, w, value) in enumerate(values):
                            mm = nc.tensor.matmul(mix, turned_probs[0:w, n % 2, j * P:(j + 1) * P], value,
                                                  start=(j == 0), stop=(j == len(values) - 1))
                        mm.then_inc(mixed, 1)
                    if s >= 3 and s - 3 in ends:
                        e = ends.index(s - 3)
                        pe.wait_ge(head_scaled, g * NU + (s - 2))
                        if e >= 1:
                            pe.wait_ge(heads_out, g * NE + e)
                        nc.tensor.transpose(back, mixed_heads[:, e % 2, :], net.c("ident")).then_inc(heads_turned, 1)
                if gated:
                    pe.sem_inc(products_free, 1)

        @block.scalar
        def _(act):
            act.sem_inc(scalar_free, 1)
            with act.Fori(0, groups) as g:
                for s in range(NU + 3):
                    if 1 <= s <= NU:
                        n, u = s - 1, units[s - 1]
                        act.wait_ge(probs_turned, g * NU + (n + 1))
                        if n >= 2:
                            act.wait_ge(mixed, g * NU + (n - 1))
                        w = min(u.blocks[0][1], P)
                        nc.scalar.activation(turned_probs[0:w, n % 2, 0:len(u.blocks) * P], turn[0:w, 0:len(u.blocks) * P],
                                             ACT.Copy).then_inc(probs_copied, 1)
                    if s < NU:
                        u, st = units[s], stats[:, s % 4, :]
                        act.wait_ge(maxed, g * NU + (s + 1))
                        if u.start is not None:
                            nc.scalar.activation(st[:, 8:9], u.start, ACT.Exp, bias=st[:, 1:2])
                        nc.scalar.activation(probs[:, s % 2, u.lo:u.hi], probs[:, s % 2, u.lo:u.hi], ACT.Exp, bias=st[:, 1:2],
                                             accum_out=st[:, 2:3]).then_inc(exped, 1)
                    if s == NU - 1:
                        act.wait_ge(exped, g * NU + NU)
                        act.sem_inc(scalar_free, 1)
                    if s >= 3 and s - 3 in ends:
                        e, u = ends.index(s - 3), units[s - 3]
                        act.wait_ge(heads_turned, g * NE + (e + 1))
                        nc.scalar.activation(out[:, bass.ds(2 * g + u.pair, 1), u.qt * P:(u.qt + 1) * P],
                                             back.unsqueeze(1), ACT.Copy).then_inc(heads_out, 1)
                act.wait_ge(heads_out, g * NE + NE)

        @block.vector
        def _(dve):
            dve.sem_inc(vector_free, 1)
            if NB and gated:
                dve.sem_inc(bias_free, 1)
            with dve.Fori(0, groups) as g:
                done, ready = 0, 0
                for s in range(NU + 2):
                    if s < NU:
                        u, st = units[s], stats[:, s % 4, :]
                        if (u.ready or NC) > ready:
                            ready = u.ready or NC
                            dve.wait_ge(fixed_ready, g * NC + ready)
                        dve.wait_ge(scored, g * NU + (s + 1))
                        if s >= 2:
                            dve.wait_ge(probs_turned, g * NU + (s - 1))
                        if u.start is not None:
                            nc.vector.tensor_copy(st[:, 3:4], u.start)
                        else:
                            nc.vector.memset(st[:, 3:4], -3.0e38)
                        for n, (lo, hi, bias) in enumerate(u.biased):
                            mm = nc.vector.tensor_tensor_reduce(probs[:, s % 2, lo:hi], scores(s)[:, lo:hi], bias, SCALE, -3.0e38,
                                                                ALU.add, ALU.max, st[:, 4 + n:5 + n])
                        mm.then_inc(step, 1)
                        done += 1
                        dve.wait_ge(step, g * NS + done)
                        nc.vector.tensor_reduce(st[:, 1:2], st[:, 3:4 + len(u.biased)], AX.X, ALU.max, negate=True).then_inc(maxed, 1)
                        if s == NU - 1 and not gated:
                            dve.sem_inc(vector_free, 1)
                    if s >= 2:
                        n, u = s - 2, units[s - 2]
                        st, e = stats[:, n % 4, :], sum(x < n for x in ends)
                        total = st[:, 2:3]
                        dve.wait_ge(exped, g * NU + (n + 1))
                        if u.start is not None:
                            nc.vector.tensor_tensor(st[:, 7:8], total, st[:, 8:9], ALU.add).then_inc(step, 1)
                            done += 1
                            dve.wait_ge(step, g * NS + done)
                            total = st[:, 7:8]
                        nc.vector.reciprocal(st[:, 0:1], total).then_inc(step, 1)
                        done += 1
                        dve.wait_ge(step, g * NS + done)
                        share = st[:, 0:1]
                        if u.gate is not None:
                            nc.vector.tensor_tensor(st[:, 6:7], share, u.gate, ALU.mult).then_inc(step, 1)
                            done += 1
                            dve.wait_ge(step, g * NS + done)
                            share = st[:, 6:7]
                        dve.wait_ge(mixed, g * NU + (n + 1))
                        to = mixed_heads[:, e % 2, u.b * DH:(u.b + 1) * DH]
                        if u.first:
                            if e >= 2:
                                dve.wait_ge(heads_turned, g * NE + (e - 1))
                            nc.vector.tensor_scalar(to, mix, share, None, ALU.mult).then_inc(head_scaled, 1)
                        else:
                            dve.wait_ge(head_scaled, g * NU + n)
                            nc.vector.scalar_tensor_tensor(out=to, in0=mix, scalar=share, in1=to, op0=ALU.mult,
                                                           op1=ALU.add).then_inc(head_scaled, 1)
                assert done == NS
                dve.wait_ge(head_scaled, g * NU + NU)
                if gated:
                    dve.sem_inc(vector_free, 1)
                    dve.sem_inc(bias_free, 1)


def gate_of(net, layer, which, n, w):
    return net.mod[:, layer, which * KD + n, w:w + 1]


def project_back(net, w, k_chunks, source, layer, which, tokens, permuted=False):
    nc = net.nc
    slabs = [slab_loads(w, [(n * P, P)]) for n in range(KD)]
    counts = slab_counts(slabs)
    segs = [(0, LAT)] + ([(LAT, tokens)] if tokens > LAT else [])
    temp = net.work[:, 0:2 * LAT].rearrange("p (s n) -> p s n", s=2)
    out = lambda n: net.ps[:, 2 * (n % 4):2 * (n % 4) + 2, :].rearrange("p b n -> p (b n)")
    names = [f"slab_in{s}" for s in range(RING)] + ["product", "added", "gated"]
    with net.stage(*names) as (block, *sems):
        slab_in, (product, added, gated) = sems[:RING], sems[RING:]

        @block.sync
        def _(sp):
            load_slabs(net, sp, slabs, k_chunks, P, slab_in, product)

        @block.tensor
        def _(pe):
            for n in range(KD):
                pe.wait_ge(slab_in[n % RING], counts[n])
                if n >= 4:
                    pe.wait_ge(added, n - 3)
                slab = ring_slab(net, n % RING, k_chunks, P)
                for k in range(k_chunks):
                    for lo, hi in segs:
                        mm = nc.tensor.matmul(out(n)[:, lo:hi], slab[:, k, :], source(k)[:, lo:hi], start=(k == 0), stop=(k == k_chunks - 1))
                mm.then_inc(product, 1)

        @block.vector
        def _(dve):
            for n in range(KD):
                dve.wait_ge(product, n + 1)
                if permuted:
                    nc.vector.tensor_scalar(temp[:, n % 2, :], out(n)[:, 0:LAT], gate_of(net, layer, which, n, 0), None,
                                            ALU.mult).then_inc(gated, 1)
                    dve.wait_ge(gated, n + 1)
                    grid = by_column_block(net.h[:, n, 0:LAT])
                    nc.vector.tensor_tensor(grid, grid, temp[:, n % 2, :].rearrange("p (b r c) -> p r b c", r=8, c=16),
                                            ALU.add).then_inc(added, 1)
                    continue
                for m, (lo, hi) in enumerate(segs):
                    mm = nc.vector.scalar_tensor_tensor(out=net.h[:, n, lo:hi], in0=out(n)[:, lo:hi], scalar=gate_of(net, layer, which, n, m),
                                                        in1=net.h[:, n, lo:hi], op0=ALU.mult, op1=ALU.add)
                mm.then_inc(added, 1)


def gate_up(net, w, tokens):
    nc = net.nc
    TURNS = KF // 2
    wv = w.rearrange("(k p) n -> p k n", p=P)
    hidden = net.big.rearrange("p (n t) -> p n t", n=KF)
    silu = net.work[:, 0:2 * TOK].rearrange("p (s n) -> p s n", s=2)
    out = lambda s: net.ps[:, 2 * s:2 * s + 2, :].rearrange("p b n -> p (b n)")[:, 0:tokens]
    segs = [(lo, min(lo + LAT, tokens)) for lo in range(0, tokens, LAT)]
    names = [f"slab_in{s}" for s in range(RING)] + ["product", "silu_done", "pair_done"]
    with net.stage(*names) as (block, *sems):
        slab_in, (product, silu_done, pair_done) = sems[:RING], sems[RING:]

        @block.sync
        def _(sp):
            column = lambda i, s: (s % 2) * D_FF + (i * 2 + s // 2) * P
            for s in range(RING):
                sp.dma_start(ring_slab(net, s, KD, P), wv[:, :, column(0, s):column(0, s) + P]).then_inc(slab_in[s], 16)
            with sp.Fori(1, TURNS) as i:
                for s in range(RING):
                    sp.wait_ge(product, i * RING + (s + 1 - RING))
                    sp.dma_start(ring_slab(net, s, KD, P), wv[:, :, bass.ds(i * (2 * P) + (s % 2) * D_FF + (s // 2) * P, P)]).then_inc(slab_in[s], 16)

        @block.tensor
        def _(pe):
            with pe.Fori(0, TURNS) as i:
                for s in range(RING):
                    pe.wait_ge(slab_in[s], (i + 1) * 16)
                    pe.wait_ge(pair_done, i * 2 + (s // 2 + 1))
                    slab = ring_slab(net, s, KD, P)
                    for k in range(KD):
                        for lo, hi in segs:
                            mm = nc.tensor.matmul(out(s)[:, lo:hi], slab[:, k, :], net.a[:, k, lo:hi], start=(k == 0), stop=(k == KD - 1))
                    mm.then_inc(product, 1)

        @block.scalar
        def _(act):
            with act.Fori(0, TURNS) as i:
                for p in range(2):
                    act.wait_ge(product, i * RING + (2 * p + 1))
                    act.wait_ge(pair_done, i * 2 + (p + 1))
                    nc.scalar.activation(silu[:, p, 0:tokens], out(2 * p), ACT.Silu).then_inc(silu_done, 1)

        @block.vector
        def _(dve):
            dve.sem_inc(pair_done, 2)
            with dve.Fori(0, TURNS) as i:
                for p in range(2):
                    dve.wait_ge(product, i * RING + (2 * p + 2))
                    dve.wait_ge(silu_done, i * 2 + (p + 1))
                    nc.vector.tensor_tensor(hidden[:, bass.ds(i * 2 + p, 1), 0:tokens], silu[:, p:p + 1, 0:tokens],
                                            out(2 * p + 1).unsqueeze(1), ALU.mult).then_inc(pair_done, 1)


def feed_forward(net, layer, scales, tokens):
    d = net.dram
    modulate(net, layer, 3, scales, tokens)
    gate_up(net, d["w_gate_up"][layer], tokens)
    hidden = net.big.rearrange("p (n t) -> p n t", n=KF)
    project_back(net, d["w_down"][layer], KF, lambda k: hidden[:, k, :], layer, 5, tokens)


def sliding_layer(net):
    nc, d = net.nc, net.dram
    w = d["swa_w_qkv"][0]
    q = net.big[:, 0:KD * TOK].rearrange("p (c t) -> p c t", t=TOK)
    k = net.big[:, KD * TOK:(KD + 4) * TOK].rearrange("p (c t) -> p c t", t=TOK)
    v = net.big[:, (KD + 4) * TOK:(KD + 4) * TOK + 6 * 256].rearrange("p (t n) -> p t n", t=6)
    base = (KD + 4) * TOK + 6 * 256
    gain = lambda n: net.vt[:, 2, V_GAIN + n:V_GAIN + n + 1]
    modulate(net, 0, 0, (0, 1), TOK)
    heads_qk(net, [(w, [(D + n * DH, DH)] * 2, gain(G_SWA_K), k[:, n, :], TOK, True) for n in range(SWA_KV)]
             + [(w, [(n * P, P)], gain(G_SWA_Q), q[:, n, :], TOK, True) for n in range(KD)])
    token_major(net, [(w, [(D + 256, 256)], [(t * P, P, v[:, t, :]) for t in range(6)])], 256)

    buf = net.ring.rearrange("p s n -> p (s n)")
    mask, zero, sinks = buf[:, 0:BAND], buf[:, BAND:BAND + CTX], buf[:, BAND + CTX:BAND + CTX + 16]
    at = BAND + CTX + 16
    keys, sink = buf[:, at:at + TOK], buf[:, at + TOK:at + TOK + 4]
    with net.stage("mask_in", "zeroed") as (block, mask_in, zeroed):
        @block.sync
        def _(sp):
            sp.dma_start(mask, net.extra("swa_mask")).then_inc(mask_in, 16)
            sp.dma_start(sinks, d["swa_sink"].partition_broadcast(P)).then_inc(mask_in, 16)
            sp.wait_ge(mask_in, 32)

        @block.vector
        def _(dve):
            nc.vector.memset(zero, 0.0).then_inc(zeroed, 1)
            dve.wait_ge(zeroed, 1)

    def units(g):
        out = []
        for pair in range(2):
            for qt in range(6):
                for b in range(2):
                    kb = keys[b * DH:(b + 1) * DH, :]
                    value = lambda t: None if g is None else v[:, t, bass.ds(g * DH, DH)]
                    near = [t for t in (qt - 1, qt, qt + 1) if 0 <= t < 4] if qt < 4 else []
                    n, skip = len(near), (P if qt == 0 else 0)
                    ks, biased, blocks = [], [], []
                    if n:
                        lo = LAT - n * P
                        ks.append((lo, n * P, kb[:, near[0] * P:(near[-1] + 1) * P]))
                        biased.append((lo, LAT, mask[:, skip:skip + n * P]))
                        blocks += [(lo + j * P, P, value(t)) for j, t in enumerate(near)]
                    ks.append((LAT, CTX, kb[:, LAT:TOK]))
                    biased.append((LAT, TOK, zero))
                    blocks += [(LAT + j * P, P, value(4 + j)) for j in range(2)]
                    h = 2 * pair + b
                    out.append(Unit(pair, b, qt, ks, biased, blocks, start=sink[:, h:h + 1]))
        return out

    copies = lambda g: [
        lambda: nc.gpsimd.tensor_copy(keys.unsqueeze(1), k[:, bass.ds(g, 1), :]),
        lambda: nc.gpsimd.tensor_copy(sink, sinks[:, bass.ds(g * 4, 4)]),
    ]
    attention(net, SWA_KV, q, copies, lambda g: [], units, buf[:, at + TOK + 4:], net.a, 2)
    project_back(net, d["swa_w_o"][0], KD, lambda k: net.a[:, k, :], 0, 2, TOK)
    feed_forward(net, 0, (2, 3), TOK)


def store_result(net, out):
    nc = net.nc
    rows = net.big[:, 0:4 * D].rearrange("p (t n) -> p t n", t=4)
    with net.stage("turned", "even_out", "odd_out", "stored") as (block, turned, even_out, odd_out, stored):

        @block.tensor
        def _(pe):
            for i in range(8):
                for c in range(4):
                    mm = nc.tensor.transpose(net.ps[:, i, c * P:(c + 1) * P], net.h[:, 4 * (i % 2) + c, (i // 2) * P:(i // 2 + 1) * P], net.c("ident"))
                mm.then_inc(turned, 1)

        @block.scalar
        def _(act):
            for i in range(0, 8, 2):
                act.wait_ge(turned, i + 1)
                nc.scalar.activation(rows[:, i // 2, 0:BANK], net.ps[:, i, :], ACT.Copy).then_inc(even_out, 1)

        @block.vector
        def _(dve):
            for i in range(1, 8, 2):
                dve.wait_ge(turned, i + 1)
                nc.vector.tensor_copy(rows[:, i // 2, BANK:2 * BANK], net.ps[:, i, :]).then_inc(odd_out, 1)

        @block.sync
        def _(sp):
            for t in range(4):
                sp.wait_ge(even_out, t + 1)
                sp.wait_ge(odd_out, t + 1)
                sp.dma_start(out[0, t * P:(t + 1) * P, :], rows[:, t, :]).then_inc(stored, 16)
            sp.wait_ge(stored, 64)


def program(nc, dram, out):
    with ExitStack() as ctx:
        net = Net(nc, ctx, dram)
        load_inputs(net)
        modulation(net)
        sliding_layer(net)
        neighbour_layer(net)
        second_block(net)
        store_result(net, out)


def neighbour_layer(net):
    nc, d = net.nc, net.dram
    w = d["na_w_qkv"][0]
    q = net.big[:, 0:KD * LAT].rearrange("p (c t) -> p c t", t=LAT)
    k = net.big[:, KD * LAT:KD * (LAT + TOK)].rearrange("p (c t) -> p c t", t=TOK)
    v = net.big[:, KD * (LAT + TOK):KD * (LAT + TOK) + 6 * D].rearrange("p (t n) -> p t n", t=6)
    gain = lambda n: net.vt[:, 2, V_GAIN + n:V_GAIN + n + 1]
    modulate(net, 1, 0, (4, 5), TOK, permute=True)
    heads_qk(net, [(w, [(n * P, P)], gain(G_NA_Q), q[:, n, :], LAT, False) for n in range(KD)]
             + [(w, [(D + n * P, P)], gain(G_NA_K), k[:, n, :], TOK, False) for n in range(KD)])
    token_major(net, [(w, [(2 * D + n * 256, 256)], [(t * P, P, v[:, t, n * 256:(n + 1) * 256]) for t in range(6)])
                      for n in range(4)], 256)

    mask = net.work[:, 0:3 * BAND].rearrange("p (k n) -> p k n", k=3)
    raw = net.work[:, 3 * BAND:7 * BAND].rearrange("p (h n) -> p h n", h=4)
    buf = net.ring.rearrange("p s n -> p (s n)")
    zero = buf[:, 0:CTX]
    keys = buf[:, CTX:CTX + 2 * TOK].rearrange("p (c t) -> p c t", c=2)
    at = CTX + 2 * TOK
    spans = [(0, P, BAND), (2 * P, 0, BAND), (5 * P, 0, 2 * P)]
    width = 7 * P
    bias = buf[:, at:at + 4 * width].rearrange("p (h n) -> p h n", h=4)
    with net.stage("mask_in", "zeroed") as (block, mask_in, zeroed):
        @block.sync
        def _(sp):
            sp.dma_start(mask.rearrange("p k n -> p (k n)"), net.extra("na_mask")).then_inc(mask_in, 16)
            sp.wait_ge(mask_in, 16)

        @block.vector
        def _(dve):
            nc.vector.memset(zero, 0.0).then_inc(zeroed, 1)
            dve.wait_ge(zeroed, 1)

    def copies(g):
        def masked(h, kind):
            to, lo, hi = spans[kind]
            def op():
                view = lambda ap: ap.rearrange("p (d r c) -> p r d c", r=8, c=16)
                src = raw[:, h, :].rearrange("p (r d c) -> p r d c", r=8, c=16)[:, :, lo // P:hi // P, :]
                return nc.gpsimd.tensor_tensor(view(bias[:, h, to:to + hi - lo]), src, view(mask[:, kind, lo:hi]), ALU.add)
            return op
        return ([lambda: nc.gpsimd.tensor_copy(keys, k[:, bass.ds(2 * g, 2), :])]
                + [masked(2 * pair + b, kind) for pair in range(2) for kind in range(3) for b in range(2)])

    def units(g):
        out = []
        for pair in range(2):
            for qt in range(4):
                for b in range(2):
                    kb = keys[b * DH:(b + 1) * DH, pair, :]
                    h = 2 * pair + b
                    value = lambda t: None if g is None else v[:, t, bass.ds(g * 256 + h * DH, DH)]
                    near = [t for t in (qt - 1, qt, qt + 1) if 0 <= t < 4]
                    n, at = len(near), spans[(0, 1, 1, 2)[qt]][0]
                    lo = LAT - n * P
                    ks = [(lo, n * P, kb[:, near[0] * P:(near[-1] + 1) * P]), (LAT, CTX, kb[:, LAT:TOK])]
                    biased = [(lo, LAT, bias[:, h, at:at + n * P]), (LAT, TOK, zero)]
                    blocks = [(lo + j * P, P, value(t)) for j, t in enumerate(near)] + [(LAT + j * P, P, value(4 + j)) for j in range(2)]
                    kind = (0, 1, 1, 2)[qt]
                    out.append(Unit(pair, b, qt, ks, biased, blocks, ready=2 + 6 * pair + 2 * kind + b + 1))
        return out

    biases = lambda g: [(raw[r * 16:(r + 1) * 16], net.na_bias[bass.ds(g * 4, 4), :, (7 - r) * 48:(15 - r) * 48].rearrange("h q n -> q h n"))
                        for r in range(8)]
    attention(net, 4, q, copies, biases, units, buf[:, at + 4 * width:], net.a, 2)
    project_back(net, d["na_w_o"][0], KD, lambda k: net.a[:, k, :], 1, 2, LAT, permuted=True)
    feed_forward(net, 1, (6,), LAT)


class Sparse:

    def __init__(self, net):
        big = net.big
        cols = lambda at, *shape: big[:, at:at + int(np.prod(shape))]
        self.ya = cols(0, 4, LAT).rearrange("p (c t) -> p c t", t=LAT)
        self.yb = cols(2048, 4, LAT).rearrange("p (c t) -> p c t", t=LAT)
        self.q = cols(4096, 4, LAT).rearrange("p (c t) -> p c t", t=LAT)
        self.k = cols(6144, 4, LAT).rearrange("p (c t) -> p c t", t=LAT)
        self.v = cols(8192, 4, 256).rearrange("p (t n) -> p t n", t=4)
        self.strips = cols(9216, 4, LAT).rearrange("p (c t) -> p c t", t=LAT)[0:DH]
        self.cmp_bias = cols(11264, 4, N_CMP * 8).rearrange("p (q n h) -> p q n h", q=4, h=8)
        self.gates = cols(12288, 4, 24).rearrange("p (q n) -> p q n", q=4)
        small = lambda n: cols(12384 + 32 * n, 32).rearrange("p (c h) -> p c h", h=4)
        self.beta, self.sums, self.eg, self.el, self.egl, self.g, self.totals = [small(n) for n in range(7)]
        self.small = cols(12384, 160).rearrange("p (n c h) -> p n c h", n=5, h=4)
        self.k_cmp = cols(12700, 2 * N_CMP)
        self.v_cmp = cols(12762, 128)[0:N_CMP]
        self.cmp_hidden = cols(12890, 2, 2, 2 * N_CMP).rearrange("p (i m n) -> p i m n", i=2, m=2)
        self.windows = cols(13600, 32, 2 * N_CMP).rearrange("p (j n) -> p j n", j=32)[0:DH]
        self.hot = cols(15584, 992)[0:33]
        self.rel = cols(16576, 8)
        self.qkv = cols(4096, 12, LAT).rearrange("p (c t) -> p c t", t=LAT)
        self.merged = cols(4096, 8, LAT).rearrange("p (c t) -> p c t", t=LAT)


def gates_and_decays(net, sp_):
    nc, d = net.nc, net.dram
    w = d["w_in_2"][0].rearrange("(k p) n -> p k n", p=P)
    slab = net.ring[:, 0, 0:KD * 40].rearrange("p (k n) -> p k n", k=KD)
    alog, dtb = (net.work[:, 8 * n:8 * n + 8] for n in range(2))
    negexp = net.work[:, 16:20]
    own = lambda ap, par: ap[par * DH:par * DH + DH].rearrange("p (h q) -> p h q", q=2)[:, :, par]
    x, ax, ex, z, z2, poly, pos = (net.work[:, 64 + 32 * n:96 + 32 * n].rearrange("p (c h) -> p c h", h=4) for n in range(7))
    rows = net.work[0:32, 512:640]
    carry = net.work[0:32, 640:648].rearrange("p (q b) -> p q b", q=2)
    wide = lambda ap: ap.unsqueeze(1).to_broadcast([P, 8, 4])
    names = ("weights_in", "consts_in", "gates_raw", "ba_raw", "g_ready", "g_turned", "rows_summed", "sums_turned", "gc_ready",
             "last_done", "gates_sig", "exps", "x_ready", "exp_ready", "room_ready", "link")
    with net.stage(*names) as (block, weights_in, consts_in, gates_raw, ba_raw, g_ready, g_turned, rows_summed, sums_turned,
                               gc_ready, last_done, gates_sig, exps, x_ready, exp_ready, room_ready, link):
        @block.sync
        def _(sp):
            sp.dma_start(slab[:, :, 0:24], w[:, :, IN_GATE:IN_GATE + 24]).then_inc(weights_in, 16)
            sp.dma_start(slab[:, :, 24:40], w[:, :, IN_BETA:IN_BETA + 16]).then_inc(weights_in, 16)
            for dst, src in ((alog, d["dn_a_log_2"]), (dtb, d["dn_dt_bias_2"])):
                sp.dma_start(dst, src[0].partition_broadcast(P)).then_inc(consts_in, 16)

        @block.tensor
        def _(pe):
            pe.wait_ge(weights_in, 32)
            for t in range(4):
                for k in range(KD):
                    mm = nc.tensor.matmul(net.ps[:, 0, t * 24:t * 24 + 24], net.a[:, k, t * P:(t + 1) * P], slab[:, k, 0:24],
                                          start=(k == 0), stop=(k == KD - 1))
            mm.then_inc(gates_raw, 1)
            for par in range(2):
                for c in range(8):
                    for k in range(KD):
                        rhs = slab[:, k, 24:40].rearrange("p (w h q) -> p w h q", w=2, q=2)[:, :, :, par]
                        mm = nc.tensor.matmul(net.ps[par * DH:par * DH + DH, 1 + par, c * 8:c * 8 + 8].rearrange("p (w h) -> p w h", w=2),
                                              net.a[:, k, c * CHUNK:(c + 1) * CHUNK], rhs, start=(k == 0), stop=(k == KD - 1))
            mm.then_inc(ba_raw, 1)
            pe.wait_ge(g_ready, 1)
            nc.tensor.transpose(net.ps[0:32, 3, 0:P], sp_.g.rearrange("p c h -> p (c h)"), net.c("ident")).then_inc(g_turned, 1)
            pe.wait_ge(rows_summed, 1)
            nc.tensor.transpose(net.ps[:, 4, 0:32], rows, net.c("ident")[0:32, 0:32]).then_inc(sums_turned, 1)
            pe.wait_ge(gc_ready, 1)
            nc.tensor.matmul(net.ps[:, 5, 0:32], net.c("last2"), sp_.sums.rearrange("p c h -> p (c h)"), start=True, stop=True).then_inc(last_done, 1)

        @block.scalar
        def _(act):
            act.wait_ge(gates_raw, 1)
            nc.scalar.activation(sp_.gates, net.ps[:, 0, 0:96].rearrange("p (q n) -> p q n", q=4), ACT.Sigmoid).then_inc(gates_sig, 1)
            act.wait_ge(ba_raw, 1)
            for par in range(2):
                rows = slice(par * DH, par * DH + DH)
                raw = net.ps[rows, 1 + par, 0:64].rearrange("p (c w h) -> p c w h", c=8, w=2)
                nc.scalar.activation(sp_.beta[rows], raw[:, :, 0, :], ACT.Sigmoid).then_inc(gates_sig, 1)
            act.wait_ge(consts_in, 32)
            for par in range(2):
                ins = nc.scalar.activation(negexp[par * DH:par * DH + DH], own(alog, par), ACT.Exp)
            act.wait_ge(x_ready, 2)
            nc.scalar.activation(ax, x, ACT.Abs).then_inc(exps, 1)
            act.wait_ge(exps, 1)
            nc.scalar.activation(ex, ax, ACT.Exp, scale=-1.0).then_inc(exp_ready, 1)
            act.wait_ge(room_ready, 1)
            nc.scalar.activation(sp_.eg, sp_.sums, ACT.Exp)
            nc.scalar.activation(sp_.egl, sp_.totals, ACT.Exp)
            nc.scalar.activation(sp_.el, x, ACT.Exp)

        @block.vector
        def _(dve):
            v, links = nc.vector, 0

            def linked(ins):
                nonlocal links
                links += 1
                ins.then_inc(link, 1)
                dve.wait_ge(link, links)

            dve.wait_ge(gates_sig, 3)
            g0 = sp_.gates.rearrange("p q (h b) -> p q h b", b=3)[:, :, :, 0]
            v.tensor_tensor(g0, g0, net.c("cmp_ok").unsqueeze(2).to_broadcast([P, 4, 8]), ALU.mult)
            dve.wait_ge(consts_in, 32)
            for par in range(2):
                half = slice(par * DH, par * DH + DH)
                raw = net.ps[half, 1 + par, 0:64].rearrange("p (c w h) -> p c w h", c=8, w=2)
                v.tensor_tensor(x[half], raw[:, :, 1, :], own(dtb, par).unsqueeze(1).to_broadcast([DH, 8, 4]), ALU.add).then_inc(x_ready, 1)
            dve.wait_ge(x_ready, 2)
            v.tensor_scalar(pos, x, 0.0, None, ALU.max)
            dve.wait_ge(exp_ready, 1)
            linked(v.tensor_scalar(z2, ex, 2.0, None, ALU.add))
            linked(v.reciprocal(z2, z2))
            linked(v.tensor_tensor(z, ex, z2, ALU.mult))
            linked(v.tensor_tensor(z2, z, z, ALU.mult))
            linked(v.tensor_scalar(poly, z2, 1.0 / 17, None, ALU.mult))
            for n in (15, 13, 11, 9, 7, 5, 3):
                linked(v.scalar_tensor_tensor(out=poly, in0=poly, scalar=1.0 / n, in1=z2, op0=ALU.add, op1=ALU.mult))
            linked(v.scalar_tensor_tensor(out=poly, in0=poly, scalar=1.0, in1=z, op0=ALU.add, op1=ALU.mult))
            linked(v.scalar_tensor_tensor(out=pos, in0=poly, scalar=2.0, in1=pos, op0=ALU.mult, op1=ALU.add))
            linked(v.tensor_tensor(pos, pos, wide(negexp), ALU.mult))
            v.tensor_scalar(sp_.g, pos, -1.0, None, ALU.mult).then_inc(g_ready, 1)
            dve.wait_ge(g_turned, 1)
            linked(v.tensor_copy(rows, net.ps[0:32, 3, 0:P]))
            cell = rows.rearrange("p (q b t) -> p q b t", q=2, t=16)
            for n in range(1, 16):
                linked(v.tensor_tensor(cell[:, :, :, n], cell[:, :, :, n], cell[:, :, :, n - 1], ALU.add))
            linked(v.tensor_copy(carry[:, :, 1], cell[:, :, 0, 15]))
            for n in (2, 3):
                linked(v.tensor_tensor(carry[:, :, n], carry[:, :, n - 1], cell[:, :, n - 1, 15], ALU.add))
            v.tensor_tensor(cell[:, :, 1:4, :], cell[:, :, 1:4, :], carry[:, :, 1:4].unsqueeze(3).to_broadcast([32, 2, 3, 16]), ALU.add)\
                .then_inc(rows_summed, 1)
            view = lambda b: net.ps[:, b, 0:32].rearrange("p (c h) -> p c h", h=4)
            dve.wait_ge(sums_turned, 1)
            v.tensor_copy(sp_.sums, view(4)).then_inc(gc_ready, 1)
            dve.wait_ge(last_done, 1)
            dve.wait_ge(gc_ready, 1)
            linked(v.tensor_copy(sp_.totals, view(5)))
            v.tensor_tensor(x, sp_.totals, sp_.sums, ALU.subtract).then_inc(room_ready, 1)


def compress(net, sp_):
    nc, d = net.nc, net.dram
    w = d["w_in_2"][0].rearrange("(k p) n -> p k n", p=P)
    slab = net.work[:, 0:KD * 256].rearrange("p (k n) -> p k n", k=KD)
    sq, ln, rstd, mean, temp = (net.work[:, 2048 + 64 * n:2048 + 64 * n + 62] for n in range(5))
    flat = net.ring.rearrange("p s n -> p (s n)")
    w1 = flat[0:DH, 0:32 * 256].rearrange("p (j n) -> p j n", j=32)
    w2k = flat[:, 8192:8192 + 256].rearrange("p (m n) -> p m n", m=2)
    w2v = flat[:, 8448:8448 + 128].rearrange("p (m n) -> p m n", m=2)
    N = 2 * N_CMP
    names = ("slab_in", "w1_in", "w2_in", "hot_in", "strip_done", "strip_out", "windows_done", "hidden_done", "gelu_done",
             "out_done", "squared", "summed", "mean_done", "newton_step", "ln_done", "rstd_done", "rel_ready", "bias_done", "copied")
    with net.stage(*names) as (block, slab_in, w1_in, w2_in, hot_in, strip_done, strip_out, windows_done, hidden_done, gelu_done,
                               out_done, squared, summed, mean_done, newton_step, ln_done, rstd_done, rel_ready, bias_done, copied):
        @block.sync
        def _(sp):
            sp.dma_start(slab, w[:, :, IN_KV:IN_KV + 256]).then_inc(slab_in, 16)
            sp.dma_start(sp_.rel[0:32], d["rel_bias_2"]).then_inc(hot_in, 16)
            sp.dma_start(sp_.hot, net.extra("hot_fwd", 33)).then_inc(hot_in, 16)
            sp.dma_start(w2v, d["cmp_w2_2"][0, 1].rearrange("(m p) n -> p m n", p=P)).then_inc(w2_in, 16)
            for half in range(2):
                sp.dma_start(w2k[:, :, half * DH:half * DH + DH], d["cmp_w2_2"][0, 0].rearrange("(m p) n -> p m n", p=P)).then_inc(w2_in, 16)
            for i in range(2):
                if i:
                    sp.wait_ge(hidden_done, 2)
                sp.dma_start(w1, d["cmp_w1_2"][0, i].rearrange("(j p) n -> p j n", p=DH)).then_inc(w1_in, 16)

        @block.tensor
        def _(pe):
            pe.wait_ge(slab_in, 16)
            for n in range(4):
                for k in range(KD):
                    mm = nc.tensor.matmul(net.ps[0:DH, n, :], slab[:, k, n * DH:(n + 1) * DH], net.a[:, k, 0:LAT],
                                          start=(k == 0), stop=(k == KD - 1))
                mm.then_inc(strip_done, 1)
            pe.wait_ge(rel_ready, 2)
            for q in range(4):
                for n in range(N_CMP):
                    y = P * q - 16 * n - 31 + 511
                    mm = nc.tensor.matmul(net.ps[:, 4 + q // 2, (q % 2) * 256 + n * 8:(q % 2) * 256 + n * 8 + 8], sp_.hot[:, y:y + P],
                                          sp_.rel[0:33, :], start=True, stop=True)
                mm.then_inc(bias_done, 1)
            for i in range(2):
                pe.wait_ge(w1_in, 16 * (i + 1))
                pe.wait_ge(windows_done, i + 1)
                for m in range(2):
                    if i:
                        pe.wait_ge(gelu_done, m + 1)
                    for j in range(32):
                        mm = nc.tensor.matmul(net.ps[:, 6 + m, 0:N], w1[:, j, m * P:(m + 1) * P], sp_.windows[:, j, :],
                                              start=(j == 0), stop=(j == 31))
                    mm.then_inc(hidden_done, 1)
            pe.wait_ge(w2_in, 48)
            pe.wait_ge(gelu_done, 4)
            pe.wait_ge(strip_out, 4)
            for m in range(2):
                mm = nc.tensor.matmul(net.ps[:, 0, 0:N], w2k[:, m, :], sp_.cmp_hidden[:, 0, m, :], start=(m == 0), stop=(m == 1))
            mm.then_inc(out_done, 1)
            for g in range(2):
                for m in range(2):
                    mm = nc.tensor.matmul(net.ps[0:N_CMP, 1, g * DH:(g + 1) * DH], sp_.cmp_hidden[:, 1, m, g * N_CMP:(g + 1) * N_CMP],
                                          w2v[:, m, :], start=(m == 0), stop=(m == 1))
            mm.then_inc(out_done, 1)
            pe.wait_ge(squared, 1)
            nc.tensor.matmul(net.ps[:, 2, 0:N], net.c("blk64"), sq, start=True, stop=True).then_inc(summed, 1)

        @block.scalar
        def _(act):
            for n in range(4):
                act.wait_ge(strip_done, n + 1)
                nc.scalar.activation(sp_.strips[:, n, :], net.ps[0:DH, n, :], ACT.Copy).then_inc(strip_out, 1)
            for i in range(2):
                for m in range(2):
                    act.wait_ge(hidden_done, 2 * i + m + 1)
                    nc.scalar.activation(sp_.cmp_hidden[:, i, m, :], net.ps[:, 6 + m, 0:N], ACT.Gelu_apprx_tanh).then_inc(gelu_done, 1)
            act.wait_ge(out_done, 1)
            nc.scalar.activation(sq, net.ps[:, 0, 0:N], ACT.Square).then_inc(squared, 1)
            act.wait_ge(mean_done, 1)
            nc.scalar.activation(ln, mean, ACT.Ln).then_inc(ln_done, 1)
            act.wait_ge(ln_done, 1)
            nc.scalar.activation(rstd, ln, ACT.Exp, scale=-0.5).then_inc(rstd_done, 1)

        @block.vector
        def _(dve):
            nc.vector.memset(net.work[0:33, 3000:3008], NEG / SCALE).then_inc(rel_ready, 1)
            dve.wait_ge(rel_ready, 1)
            dve.wait_ge(hot_in, 32)
            nc.vector.tensor_scalar(net.work[0:32, 3000:3008], sp_.rel[0:32], 1.0 / SCALE, None, ALU.mult).then_inc(copied, 1)
            dve.wait_ge(copied, 1)
            nc.vector.tensor_copy(sp_.rel[0:33], net.work[0:33, 3000:3008]).then_inc(rel_ready, 1)
            dve.wait_ge(strip_out, 4)
            part = sp_.strips.ap[0]
            for i in range(2):
                if i:
                    dve.wait_ge(hidden_done, 2)
                strip = sp_.strips[:, 2 * i, 0:1]
                src = bass.AP(strip.tensor, strip.offset, [list(part), [1, 32], [LAT, 2], [16, N_CMP]])
                pos = net.vt[0:DH, 2, V_POS + 32 * i:V_POS + 32 * (i + 1)]
                nc.vector.tensor_tensor(sp_.windows.rearrange("p j (g n) -> p j g n", g=2), src,
                                        pos.unsqueeze(2).unsqueeze(3).to_broadcast([DH, 32, 2, N_CMP]), ALU.add).then_inc(windows_done, 1)
            for q in range(4):
                dve.wait_ge(bias_done, 4)
                nc.vector.tensor_copy(sp_.cmp_bias[:, q], net.ps[:, 4 + q // 2, (q % 2) * 256:(q % 2) * 256 + N_CMP * 8]
                                      .rearrange("p (n h) -> p n h", h=8))
            dve.wait_ge(out_done, 2)
            nc.vector.tensor_copy(sp_.v_cmp, net.ps[0:N_CMP, 1, 0:128])
            dve.wait_ge(summed, 1)
            nc.vector.tensor_scalar(mean, net.ps[:, 2, 0:N], 1.0 / DH, EPS, ALU.mult, ALU.add).then_inc(mean_done, 1)
            dve.wait_ge(rstd_done, 1)
            newton(nc, dve, rstd, mean, temp, newton_step, 0)
            nc.vector.scalar_tensor_tensor(out=sp_.k_cmp, in0=net.ps[:, 0, 0:N], scalar=net.vt[:, 2, V_GAIN + G_QK0 + 1:V_GAIN + G_QK0 + 2],
                                           in1=rstd, op0=ALU.mult, op1=ALU.mult)


def sparse_attention(net, sp_):
    nc, d = net.nc, net.dram
    w = d["w_in_2"][0]
    gain = lambda n: net.vt[:, 2, V_GAIN + G_QK0 + n:V_GAIN + G_QK0 + n + 1]
    kv = lambda i, g: IN_KV + (2 * i + g) * DH
    heads_qk(net, [(w, [(IN_Q + n * P, P)], gain(0), sp_.q[:, n, :], LAT, False) for n in range(4)]
             + [(w, [(kv(i, g), DH)] * 2, gain(i // 2 + 1), sp_.k[:, (i // 2 - 1) * 2 + g, :], LAT, False)
                for i in (2, 4) for g in range(2)])
    token_major(net, [(w, [(kv(3, 0), P), (kv(5, 0), P)], [(t * P, P, sp_.v[:, t, :]) for t in range(4)])], 256)
    gates_and_decays(net, sp_)
    compress(net, sp_)

    buf = net.ring.rearrange("p s n -> p (s n)")
    at = [0]

    def take(n):
        at[0] += n
        return buf[:, at[0] - n:at[0]]

    keys = take(2 * LAT).rearrange("p (w t) -> p w t", w=2)
    k_cmp = take(N_CMP)
    bias_cmp = take(16 * N_CMP).rearrange("p (q h n) -> p q h n", q=4, h=4)
    gates = take(48).rearrange("p (q n) -> p q n", q=4)
    v_cmp = take(DH)[0:N_CMP]
    bias = take(4 * LAT).rearrange("p (h n) -> p h n", h=4)

    def copies(g):
        return ([lambda i=i: nc.gpsimd.tensor_copy(keys[:, i:i + 1, :], sp_.k[:, bass.ds(2 * i + g, 1), :]) for i in range(2)]
                + [lambda: nc.gpsimd.tensor_copy(k_cmp, sp_.k_cmp[:, bass.ds(g * N_CMP, N_CMP)])]
                + [lambda q=q: nc.gpsimd.tensor_copy(bias_cmp[:, q].rearrange("p h n -> p n h"), sp_.cmp_bias[:, q, :, bass.ds(g * 4, 4)])
                   for q in range(4)]
                + [lambda: nc.gpsimd.tensor_copy(gates, sp_.gates[:, :, bass.ds(g * 12, 12)]),
                   lambda: nc.gpsimd.tensor_copy(v_cmp, sp_.v_cmp[:, bass.ds(g * DH, DH)])])

    def units(g):
        out = []
        for pair in range(2):
            for qt in range(4):
                for b in range(2):
                    h, half = 2 * pair + b, slice(b * DH, (b + 1) * DH)
                    gate = lambda n: gates[:, qt, 3 * h + n:3 * h + n + 1]
                    dyn = lambda ap, first: None if g is None else ap[:, bass.ds(g * DH + first, DH)]
                    out.append(Unit(pair, b, qt, [(0, N_CMP, k_cmp[half, :])], [(0, N_CMP, bias_cmp[:, qt, h, :])],
                                    [(0, N_CMP, v_cmp)], gate=gate(0), first=True, last=False))
                    n = (qt + 1) * P
                    for i in range(2):
                        out.append(Unit(pair, b, qt, [(LAT - n, n, keys[half, i, 0:n])], [(LAT - n, LAT, bias[:, h, LAT - n:LAT])],
                                        [(LAT - n + j * P, P, dyn(sp_.v[:, j, :], i * P)) for j in range(qt + 1)],
                                        gate=gate(i + 1), first=False, last=(i == 1)))
        return out

    biases = lambda g: [(bias, net.rel_bias[bass.ds(g * 4, 4)].rearrange("h p n -> p h n"))]
    attention(net, 2, sp_.q, copies, biases, units, buf[:, at[0]:], sp_.ya, len(copies(0)) + 1)


def short_convolution(net, sp_):
    nc, d = net.nc, net.dram
    N, TAPS = 12, 4
    slabs = [slab_loads(d["w_in_2"][0], [(IN_DN + n * P, P)]) for n in range(N)]
    counts = slab_counts(slabs)
    padded = net.work[:, 0:2 * 516].rearrange("p (s n) -> p s n", s=2)
    sums = net.work[:, 1032:1032 + 2 * LAT].rearrange("p (s n) -> p s n", s=2)
    names = [f"slab_in{s}" for s in range(RING)] + ["product", "padded_zero", "copied", "convolved", "silu_done", "tap"]
    with net.stage(*names) as (block, *sems):
        slab_in, (product, padded_zero, copied, convolved, silu_done, tap) = sems[:RING], sems[RING:]

        @block.sync
        def _(sp):
            load_slabs(net, sp, slabs, KD, P, slab_in, product)

        @block.tensor
        def _(pe):
            for n in range(N):
                pe.wait_ge(slab_in[n % RING], counts[n])
                if n >= 4:
                    pe.wait_ge(copied, n - 3)
                for k in range(KD):
                    mm = nc.tensor.matmul(net.ps[:, n % 4, :], ring_slab(net, n % RING, KD, P)[:, k, :], net.a[:, k, 0:LAT],
                                          start=(k == 0), stop=(k == KD - 1))
                mm.then_inc(product, 1)

        @block.scalar
        def _(act):
            act.wait_ge(padded_zero, 1)
            for n in range(N + 1):
                if n < N:
                    act.wait_ge(product, n + 1)
                    if n >= 2:
                        act.wait_ge(convolved, n - 1)
                    nc.scalar.activation(padded[:, n % 2, 3:3 + LAT], net.ps[:, n % 4, :], ACT.Copy).then_inc(copied, 1)
                if n >= 1:
                    act.wait_ge(convolved, n)
                    nc.scalar.activation(sp_.qkv[:, n - 1, :], sums[:, (n - 1) % 2, :], ACT.Silu).then_inc(silu_done, 1)

        @block.vector
        def _(dve):
            nc.vector.memset(padded, 0.0).then_inc(padded_zero, 1)
            for n in range(N):
                dve.wait_ge(copied, n + 1)
                if n >= 2:
                    dve.wait_ge(silu_done, n - 1)
                weight = lambda j: net.vt[:, 2, V_CONV + j * 12 + n:V_CONV + j * 12 + n + 1]
                to = sums[:, n % 2, :]
                nc.vector.tensor_scalar(to, padded[:, n % 2, 3:3 + LAT], weight(3), None, ALU.mult).then_inc(tap, 1)
                for m, j in enumerate((2, 1, 0)):
                    dve.wait_ge(tap, 3 * n + m + 1)
                    nc.vector.scalar_tensor_tensor(out=to, in0=padded[:, n % 2, j:j + LAT], scalar=weight(j), in1=to, op0=ALU.mult,
                                                   op1=ALU.add).then_inc(tap if m < 2 else convolved, 1)

    head_norms(net, [(sp_.qkv[:, n, :], 1.0, SCALE if n < 4 else 1.0) for n in range(8)])


def head_norms(net, chunks):
    nc = net.nc
    with net.stage("squared", "summed", "sum_out", "ln_done", "rstd_done", "newton_step", "normed") as (
            block, squared, summed, sum_out, ln_done, rstd_done, newton_step, normed):
        sq = net.work[:, 0:2 * LAT].rearrange("p (s n) -> p s n", s=2)
        ln, rstd = net.work[:, 2 * LAT:3 * LAT], net.work[:, 3 * LAT:5 * LAT].rearrange("p (s n) -> p s n", s=2)
        total, temp = net.work[:, 5 * LAT:6 * LAT], net.work[:, 6 * LAT:7 * LAT]

        @block.scalar
        def _(act):
            for n, (x, _, _) in enumerate(chunks):
                if n >= 2:
                    act.wait_ge(summed, n - 1)
                nc.scalar.activation(sq[:, n % 2, :], x, ACT.Square).then_inc(squared, 1)
                act.wait_ge(sum_out, n + 1)
                if n >= 1:
                    act.wait_ge(rstd_done, n)
                nc.scalar.activation(ln, total, ACT.Ln).then_inc(ln_done, 1)
                act.wait_ge(ln_done, n + 1)
                if n >= 2:
                    act.wait_ge(normed, n - 1)
                nc.scalar.activation(rstd[:, n % 2, :], ln, ACT.Exp, scale=-0.5).then_inc(rstd_done, 1)

        @block.tensor
        def _(pe):
            for n in range(len(chunks)):
                pe.wait_ge(squared, n + 1)
                if n >= 2:
                    pe.wait_ge(sum_out, n - 1)
                nc.tensor.matmul(net.ps[:, n % 2, :], net.c("blk64"), sq[:, n % 2, :], start=True, stop=True).then_inc(summed, 1)

        @block.vector
        def _(dve):
            for n, (x, share, factor) in enumerate(chunks):
                dve.wait_ge(summed, n + 1)
                nc.vector.tensor_scalar(total, net.ps[:, n % 2, :], share, EPS, ALU.mult, ALU.add).then_inc(sum_out, 1)
                dve.wait_ge(rstd_done, n + 1)
                newton(nc, dve, rstd[:, n % 2, :], total, temp, newton_step, 3 * n)
                nc.vector.scalar_tensor_tensor(out=x, in0=x, scalar=factor, in1=rstd[:, n % 2, :], op0=ALU.mult, op1=ALU.mult).then_inc(normed, 1)


def delta_net(net, sp_):
    nc = net.nc
    buf = net.ring.rearrange("p s n -> p (s n)")
    at = [0]

    def take(*shape):
        n = int(np.prod(shape))
        at[0] += n
        ap = buf[:, at[0] - n:at[0]]
        return ap.rearrange("p (h n) -> p h n", h=shape[0]) if len(shape) == 2 else ap

    LEVELS = 6
    k_bd, q_bd, v_bd, low_bd, attn_bd, out_bd = (take(4, P) for _ in range(6))
    state = take(4, CHUNK)
    zeroed_part = buf[:, 0:at[0]]
    lev = take(LEVELS, P)
    kq = take(8, CHUNK)
    kdec_bd, mask_x, inv, inv_t, w2 = (take(4, P) for _ in range(5))
    diag_gc, dist, decay, low_beta, temp, rhs, v_new = (take(4, CHUNK) for _ in range(7))
    scal = take(5, 4)
    beta, gc, eg, el, egl = (scal[:, n, :] for n in range(5))
    bank = lambda n, w=P: net.ps[:, n, 0:4 * w].rearrange("p (h n) -> p h n", h=4)
    kq_ps = net.ps[:, 1, :].rearrange("p (w h n) -> p w h n", w=2, h=4)
    over = lambda ap, w=CHUNK: ap.unsqueeze(2).to_broadcast([P, 4, w])
    pairs = lambda ap, w=CHUNK: ap.unsqueeze(1).to_broadcast([P, 4, w])
    halves = [(slice(0, DH), slice(0, DH)), (slice(DH, P), slice(DH, P))]
    NF, NL = 12, 6
    names = ("tables_in", "zeroed", "fixed", "operands_free", "chunk_free", "diag_ready", "running", "dist_ready", "decayed", "grams", "keys_turned",
             "values_turned", "state_read", "low_ready", "masked", "inv_ready", "inv_t_ready", "w2_done", "w2_copied", "level_done",
             "level_t_done", "attn_ready", "kdec_ready", "rhs_ready", "solved", "v_new_ready", "chunk_products", "out_ready",
             "turned", "out_stored", "link", "dist_abs")
    with net.stage(*names) as (block, tables_in, zeroed, fixed, operands_free, chunk_free, diag_ready, running, dist_ready, decayed, grams,
                               keys_turned, values_turned, state_read, low_ready, masked, inv_ready, inv_t_ready, w2_done, w2_copied,
                               level_done, level_t_done, attn_ready, kdec_ready, rhs_ready, solved, v_new_ready, chunk_products,
                               out_ready, turned, out_stored, link, dist_abs):

        @block.sync
        def _(sp):
            sp.dma_start(lev.rearrange("p h n -> p (h n)"), net.extra("lev")).then_inc(tables_in, 16)

        @block.gpsimd
        def _(pool):
            nc.gpsimd.memset(zeroed_part, 0.0).then_inc(zeroed, 1)
            pool.wait_ge(zeroed, 1)
            with pool.Fori(0, 8) as c:
                pool.wait_ge(operands_free, c + 1)
                tok = bass.ds(c * CHUNK, CHUNK)
                for rows, cols in halves:
                    for bd, first in ((q_bd, 0), (k_bd, 4), (v_bd, 8)):
                        nc.gpsimd.tensor_copy(bd[rows, :, cols], sp_.qkv[rows, first:first + 4, tok]).then_inc(fixed, 1)
                    nc.gpsimd.tensor_copy(kq[rows, 0:4, :], sp_.qkv[rows, 4:8, tok]).then_inc(fixed, 1)
                    nc.gpsimd.tensor_copy(kq[rows, 4:8, :], sp_.qkv[rows, 0:4, tok]).then_inc(fixed, 1)
                pool.wait_ge(chunk_free, c + 1)
                pool.wait_ge(out_stored, c + 1)
                for rows, _ in halves:
                    nc.gpsimd.tensor_copy(scal[rows].unsqueeze(2), sp_.small[rows, :, bass.ds(c, 1), :]).then_inc(fixed, 1)

        @block.tensor
        def _(pe):
            def products(to, lhs, rhs_of, signal):
                for h in range(4):
                    mm = nc.tensor.matmul(to[:, h], lhs[:, h, :], rhs_of(h), start=True, stop=True)
                if signal is not None:
                    mm.then_inc(signal, 1)

            pe.sem_inc(operands_free, 1)
            with pe.Fori(0, 8) as c:
                pe.wait_ge(fixed, (c + 1) * NF)
                pair_kq = kq.rearrange("p (w h) n -> p w h n", w=2)
                for h in range(4):
                    mm = nc.tensor.matmul(kq_ps[:, :, h, :], k_bd[:, h, :], pair_kq[:, :, h, :], start=True, stop=True)
                mm.then_inc(grams, 1)
                for h in range(4):
                    mm = nc.tensor.transpose(bank(2)[:, h], k_bd[:, h, :], net.c("ident"))
                mm.then_inc(keys_turned, 1)
                products(bank(3, CHUNK), v_bd, lambda h: net.c("eye2"), values_turned)
                pe.wait_ge(diag_ready, c + 1)
                nc.tensor.matmul(bank(0, CHUNK), net.c("blk64"), diag_gc, start=True, stop=True).then_inc(running, 1)
                products(bank(4, CHUNK), k_bd, lambda h: state[:, h, :], None)
                products(bank(5, CHUNK), q_bd, lambda h: state[:, h, :], state_read)
                pe.wait_ge(masked, c * LEVELS + 1)
                products(bank(6), mask_x, lambda h: net.c("ident"), w2_done)
                for n in range(1, LEVELS):
                    pe.wait_ge(masked, c * LEVELS + (n + 1))
                    pe.wait_ge(inv_t_ready, c * LEVELS + n)
                    products(bank(6), mask_x, lambda h: inv_t[:, h, :], w2_done)
                    pe.wait_ge(w2_copied, c * (LEVELS - 1) + n)
                    if n == 1:
                        pe.sem_inc(operands_free, 1)
                    pe.wait_ge(inv_ready, c * (LEVELS - 1) + n)
                    products(bank(7), inv, lambda h: w2[:, h, :], level_t_done)
                    if n < LEVELS - 1:
                        products(bank(0), w2, lambda h: inv[:, h, :], level_done)
                pe.wait_ge(rhs_ready, c + 1)
                pe.wait_ge(inv_t_ready, (c + 1) * LEVELS)
                products(bank(3, CHUNK), inv_t, lambda h: rhs[:, h, :], solved)
                pe.wait_ge(kdec_ready, c + 1)
                pe.wait_ge(attn_ready, c + 1)
                pe.wait_ge(v_new_ready, c + 1)
                products(bank(2, CHUNK), kdec_bd, lambda h: v_new[:, h, :], None)
                products(bank(4, CHUNK), attn_bd, lambda h: v_new[:, h, :], chunk_products)
                pe.wait_ge(out_ready, c + 1)
                products(bank(1, CHUNK), out_bd, lambda h: net.c("eye2"), turned)

        @block.scalar
        def _(act):
            act.sem_inc(out_stored, 1)
            with act.Fori(0, 8) as c:
                act.wait_ge(dist_ready, c + 1)
                nc.scalar.activation(decay, dist, ACT.Abs).then_inc(dist_abs, 1)
                act.wait_ge(dist_abs, c + 1)
                nc.scalar.activation(decay, decay, ACT.Exp, scale=-1.0).then_inc(decayed, 1)
                for n in range(1, LEVELS):
                    act.wait_ge(w2_done, c * LEVELS + (n + 1))
                    nc.scalar.activation(w2, bank(6), ACT.Copy).then_inc(w2_copied, 1)
                act.wait_ge(turned, c + 1)
                nc.scalar.activation(sp_.yb[:, :, bass.ds(c * CHUNK, CHUNK)], bank(1, CHUNK), ACT.Copy).then_inc(out_stored, 1)

        @block.vector
        def _(dve):
            dve.sem_inc(chunk_free, 1)
            dve.wait_ge(tables_in, 16)
            dve.wait_ge(zeroed, 1)
            with dve.Fori(0, 8) as c:
                links = 0

                def linked(ins):
                    nonlocal links
                    links += 1
                    ins.then_inc(link, 1)
                    dve.wait_ge(link, c * NL + links)

                v = nc.vector
                dve.wait_ge(fixed, (c + 1) * NF)
                v.tensor_tensor(diag_gc, pairs(net.c("eye2")), over(gc), ALU.mult).then_inc(diag_ready, 1)
                v.tensor_tensor(low_beta, pairs(net.c("low")), over(beta), ALU.mult)
                dve.wait_ge(running, c + 1)
                v.tensor_tensor(dist, bank(0, CHUNK), over(gc), ALU.subtract).then_inc(dist_ready, 1)
                dve.wait_ge(grams, c + 1)
                dve.wait_ge(decayed, c + 1)
                linked(v.tensor_tensor(temp, kq_ps[:, 0], decay, ALU.mult))
                for rows, cols in halves:
                    ins = v.tensor_tensor(low_bd[rows, :, cols], temp[rows], low_beta[rows], ALU.mult)
                ins.then_inc(low_ready, 1)
                dve.wait_ge(low_ready, c + 1)
                v.tensor_tensor(mask_x, low_bd, pairs(lev[:, 0, :], P), ALU.mult).then_inc(masked, 1)
                dve.wait_ge(masked, c * LEVELS + 1)
                v.tensor_tensor(inv, pairs(net.c("ident"), P), mask_x, ALU.subtract).then_inc(inv_ready, 1)
                dve.wait_ge(w2_done, c * LEVELS + 1)
                dve.wait_ge(inv_ready, c * (LEVELS - 1) + 1)
                v.tensor_tensor(mask_x, low_bd, pairs(lev[:, 1, :], P), ALU.mult).then_inc(masked, 1)
                v.tensor_tensor(inv_t, pairs(net.c("ident"), P), bank(6), ALU.subtract).then_inc(inv_t_ready, 1)
                for n in range(1, LEVELS):
                    if n == 1:
                        linked(v.tensor_tensor(temp, kq_ps[:, 1], decay, ALU.mult))
                        for rows, cols in halves:
                            ins = v.tensor_tensor(attn_bd[rows, :, cols], temp[rows], pairs(net.c("tri"))[rows], ALU.mult)
                        ins.then_inc(attn_ready, 1)
                        dve.wait_ge(attn_ready, c + 1)
                    if n == 2:
                        dve.wait_ge(keys_turned, c + 1)
                        v.tensor_tensor(kdec_bd, bank(2), over(el, P), ALU.mult).then_inc(kdec_ready, 1)
                    if n == 3:
                        dve.wait_ge(state_read, c + 1)
                        linked(v.tensor_tensor(temp, bank(4, CHUNK), over(eg), ALU.mult))
                        dve.wait_ge(values_turned, c + 1)
                        linked(v.tensor_tensor(temp, bank(3, CHUNK), temp, ALU.subtract))
                        v.tensor_tensor(rhs, temp, over(beta), ALU.mult).then_inc(rhs_ready, 1)
                    if n < LEVELS - 1:
                        dve.wait_ge(w2_done, c * LEVELS + (n + 1))
                        v.tensor_tensor(mask_x, low_bd, pairs(lev[:, n + 1, :], P), ALU.mult).then_inc(masked, 1)
                    dve.wait_ge(level_t_done, c * (LEVELS - 1) + n)
                    dve.wait_ge(inv_t_ready, c * LEVELS + n)
                    v.tensor_tensor(inv_t, inv_t, bank(7), ALU.subtract).then_inc(inv_t_ready, 1)
                    if n < LEVELS - 1:
                        dve.wait_ge(level_done, c * (LEVELS - 2) + n)
                        dve.wait_ge(inv_ready, c * (LEVELS - 1) + n)
                        v.tensor_tensor(inv, inv, bank(0), ALU.subtract).then_inc(inv_ready, 1)
                dve.wait_ge(solved, c + 1)
                v.tensor_copy(v_new, bank(3, CHUNK)).then_inc(v_new_ready, 1)
                linked(v.tensor_tensor(state, state, over(egl), ALU.mult))
                dve.wait_ge(rhs_ready, c + 1)
                linked(v.tensor_tensor(temp, bank(5, CHUNK), over(eg), ALU.mult))
                dve.wait_ge(chunk_products, c + 1)
                v.tensor_tensor(state, state, bank(2, CHUNK), ALU.add)
                for rows, cols in halves:
                    ins = v.tensor_tensor(out_bd[rows, :, cols], temp[rows], bank(4, CHUNK)[rows], ALU.add)
                ins.then_inc(out_ready, 1)
                assert links == NL, links
                dve.wait_ge(out_ready, c + 1)
                dve.sem_inc(chunk_free, 1)


def merge_branches(net, sp_):
    nc, d = net.nc, net.dram
    w = d["w_in_2"][0]
    slabs = [slab_loads(w, [(IN_Z + n * P, P)]) for n in range(4)]
    counts = slab_counts(slabs)
    silu = net.work[:, 0:2 * LAT].rearrange("p (s n) -> p s n", s=2)
    names = [f"slab_in{s}" for s in range(RING)] + ["product", "silu_done", "gated"]
    with net.stage(*names) as (block, *sems):
        slab_in, (product, silu_done, gated) = sems[:RING], sems[RING:]

        @block.sync
        def _(sp):
            load_slabs(net, sp, slabs, KD, P, slab_in, product)

        @block.tensor
        def _(pe):
            for n in range(4):
                pe.wait_ge(slab_in[n], counts[n])
                for k in range(KD):
                    mm = nc.tensor.matmul(net.ps[:, n, :], ring_slab(net, n, KD, P)[:, k, :], net.a[:, k, 0:LAT], start=(k == 0), stop=(k == KD - 1))
                mm.then_inc(product, 1)

        @block.scalar
        def _(act):
            for n in range(4):
                act.wait_ge(product, n + 1)
                if n >= 2:
                    act.wait_ge(gated, n - 1)
                nc.scalar.activation(silu[:, n % 2, :], net.ps[:, n, :], ACT.Silu).then_inc(silu_done, 1)

        @block.vector
        def _(dve):
            for n in range(4):
                dve.wait_ge(silu_done, n + 1)
                nc.vector.scalar_tensor_tensor(out=sp_.yb[:, n, :], in0=sp_.yb[:, n, :], scalar=net.vt[:, 2, V_GAIN + G_DN:V_GAIN + G_DN + 1],
                                               in1=silu[:, n % 2, :], op0=ALU.mult, op1=ALU.mult).then_inc(gated, 1)

    wv = w.rearrange("(k p) n -> p k n", p=P)
    branch = [d[f"w_branch_{x}_2"][0].rearrange("(k p) n -> p k n", p=P) for x in "ab"]
    gate = net.work[:, 0:4 * LAT].rearrange("p (s n) -> p s n", s=4)
    parts = net.work[:, 4 * LAT:6 * LAT].rearrange("p (s n) -> p s n", s=2)
    names = [f"slab_in{s}" for s in range(RING)] + ["product", "sigmoid_done", "weighted", "merged"]
    with net.stage(*names) as (block, *sems):
        slab_in, (product, sigmoid_done, weighted, merged) = sems[:RING], sems[RING:]

        @block.sync
        def _(sp):
            for n in range(KD):
                for s in range(RING):
                    if n:
                        sp.wait_ge(product, 4 * (n - 1) + s + 1)
                    if s < 2:
                        first = IN_MERGE + s * D + n * P
                        sp.dma_start(ring_slab(net, s, KD, P), wv[:, :, first:first + P]).then_inc(slab_in[s], 16)
                    else:
                        sp.dma_start(ring_slab(net, s, 4, P), branch[s - 2][:, :, n * P:(n + 1) * P]).then_inc(slab_in[s], 16)

        @block.tensor
        def _(pe):
            for n in range(KD):
                for s in range(RING):
                    pe.wait_ge(slab_in[s], 16 * (n + 1))
                    if n >= 2:
                        pe.wait_ge(merged, n - 1)
                    depth, src = (KD, net.a) if s < 2 else (4, (sp_.ya, sp_.yb)[s - 2])
                    for k in range(depth):
                        mm = nc.tensor.matmul(net.ps[:, 4 * (n % 2) + s, :], ring_slab(net, s, depth, P)[:, k, :], src[:, k, 0:LAT],
                                              start=(k == 0), stop=(k == depth - 1))
                    mm.then_inc(product, 1)

        @block.scalar
        def _(act):
            for n in range(KD):
                for s in range(2):
                    act.wait_ge(product, 4 * n + s + 1)
                    if n >= 2:
                        act.wait_ge(merged, n - 1)
                    nc.scalar.activation(gate[:, 2 * (n % 2) + s, :], net.ps[:, 4 * (n % 2) + s, :], ACT.Sigmoid).then_inc(sigmoid_done, 1)

        @block.vector
        def _(dve):
            for n in range(KD):
                for s in range(2):
                    dve.wait_ge(product, 4 * n + s + 3)
                    dve.wait_ge(sigmoid_done, 2 * n + s + 1)
                    if n:
                        dve.wait_ge(merged, n)
                    nc.vector.tensor_tensor(parts[:, s, :], gate[:, 2 * (n % 2) + s, :], net.ps[:, 4 * (n % 2) + 2 + s, :], ALU.mult).then_inc(weighted, 1)
                dve.wait_ge(weighted, 2 * n + 2)
                nc.vector.tensor_tensor(sp_.merged[:, n, :], parts[:, 0, :], parts[:, 1, :], ALU.add).then_inc(merged, 1)


def route(net):
    nc, d = net.nc, net.dram
    net.token_rows = nc.dram_tensor("token_rows", (LAT, D), F32, kind="Internal").ap()
    slot_table = nc.dram_tensor("slot_table", ((BLOCKS + 2) * P, 1), F32, kind="Internal").ap()
    at = [0]

    def take(*shape):
        n = int(np.prod(shape))
        at[0] += n
        ap = net.work[:, at[0] - n:at[0]]
        return ap.rearrange("p (t n) -> p t n", t=4) if len(shape) == 2 else ap

    rw = net.ring[:, 0, 0:KD * N_EXP].rearrange("p (k n) -> p k n", k=KD)
    rb = net.ring[:, 1, 0:N_EXP]
    tabs = net.ring[:, 2, 0:P + BLOCKS + 4]
    upper, block_no, token_no = tabs[:, 0:P], tabs[:, P:P + BLOCKS], tabs[:, P + BLOCKS:]
    table = net.ring[0:BLOCKS + 2, 3, 0:P]
    score, sel, duo, group, best, hit, index, masked, one, two, both = (
        take(4, N_EXP), take(4, N_EXP), take(4, 24), take(4, 4), take(4), take(4, N_EXP), take(4, N_EXP), take(4, N_EXP),
        take(4, N_EXP), take(4, N_EXP), take(4, N_EXP))
    group_one = take(4, 4)
    ends, ends_b, used = take(N_EXP), take(N_EXP), take(N_EXP)
    place, slot = take(4, N_EXP), take(4, 2)
    reached, expert = take(BLOCKS * N_EXP), take(BLOCKS)
    rows = net.big[:, 0:4 * D].rearrange("p (t n) -> p t n", t=4)
    iota = lambda n: net.c("iota16")[:, 0:n].unsqueeze(1).to_broadcast([P, 4, n])
    wide = lambda ap, n: ap.unsqueeze(2).to_broadcast([P, 4, n])
    names = ("weights_in", "tables_in", "logits", "scored", "link", "both_ready", "counted", "rows_turned", "rows_copied",
             "rows_stored", "table_zero", "table_clear", "slots_ready", "scattered", "table_in", "table_turned")
    with net.stage(*names) as (block, weights_in, tables_in, logits, scored, link, both_ready, counted, rows_turned, rows_copied,
                               rows_stored, table_zero, table_clear, slots_ready, scattered, table_in, table_turned):
        @block.sync
        def _(sp):
            sp.dma_start(rw, d["router_w_2"].rearrange("(k p) n -> p k n", p=P)).then_inc(weights_in, 16)
            sp.dma_start(rb, d["router_b_2"].partition_broadcast(P)).then_inc(weights_in, 16)
            first = net.extras["upper"][0]
            sp.dma_start(tabs, d["more_tables"][:, first:first + P + BLOCKS + 4]).then_inc(tables_in, 16)
            sp.wait_ge(table_zero, 1)
            by_block = slot_table.rearrange("(j p) o -> j (p o)", p=P)
            sp.dma_start(by_block, table).then_inc(table_clear, 16)
            for t in range(4):
                sp.wait_ge(rows_copied, 2 * t + 2)
                sp.dma_start(net.token_rows[t * P:(t + 1) * P], rows[:, t, :]).then_inc(rows_stored, 16)
            sp.wait_ge(scattered, 8 * 16)
            sp.dma_start(table, by_block).then_inc(table_in, 16)
            sp.wait_ge(rows_stored, 4 * 16)

        @block.gpsimd
        def _(pool):
            nc.gpsimd.memset(table, 0.0).then_inc(table_zero, 1)
            pool.wait_ge(tables_in, 16)
            pool.wait_ge(table_clear, 16)
            pool.wait_ge(slots_ready, 1)
            for t in range(4):
                for w in range(2):
                    nc.gpsimd.indirect_dma_start(slot_table, bass.IndirectOffsetOnAxis(net.slots[:, 2 * t + w:2 * t + w + 1], 0),
                                                 token_no[:, t:t + 1], None).then_inc(scattered, 16)

        @block.tensor
        def _(pe):
            pe.wait_ge(weights_in, 32)
            for t in range(4):
                for k in range(KD):
                    mm = nc.tensor.matmul(net.ps[:, 0, t * N_EXP:(t + 1) * N_EXP], net.a[:, k, t * P:(t + 1) * P], rw[:, k, :],
                                          start=(k == 0), stop=(k == KD - 1))
            mm.then_inc(logits, 1)
            for n in range(8):
                if n >= 4:
                    pe.wait_ge(rows_copied, n - 3)
                for k in range(4):
                    mm = nc.tensor.transpose(net.ps[:, 4 + n % 4, k * P:(k + 1) * P],
                                             net.a[:, n % 2 * 4 + k, n // 2 * P:(n // 2 + 1) * P], net.c("ident"))
                mm.then_inc(rows_turned, 1)
            pe.wait_ge(tables_in, 16)
            pe.wait_ge(both_ready, 1)
            for t in range(4):
                for s in range(t + 1):
                    nc.tensor.matmul(net.ps[:, 1, t * N_EXP:(t + 1) * N_EXP], upper if s == t else net.c("ones"), both[:, s, :],
                                     start=(s == 0), stop=(s == t))
            for s in range(4):
                mm = nc.tensor.matmul(net.ps[:, 2, 0:N_EXP], net.c("ones"), both[:, s, :], start=(s == 0), stop=(s == 3))
            mm.then_inc(counted, 1)
            pe.wait_ge(table_in, 16)
            nc.tensor.transpose(net.ps[:, 3, 0:BLOCKS + 2], table, net.c("ident")[0:BLOCKS + 2, 0:BLOCKS + 2]).then_inc(table_turned, 1)

        @block.scalar
        def _(act):
            act.wait_ge(logits, 1)
            nc.scalar.activation(score, net.ps[:, 0, 0:4 * N_EXP].rearrange("p (t n) -> p t n", t=4), ACT.Sigmoid).then_inc(scored, 1)
            for n in range(8):
                act.wait_ge(rows_turned, n + 1)
                nc.scalar.activation(rows[:, n // 2, n % 2 * BANK:(n % 2 + 1) * BANK], net.ps[:, 4 + n % 4, :], ACT.Copy).then_inc(rows_copied, 1)

        @block.vector
        def _(dve):
            v = nc.vector
            links = 0

            def linked(ins):
                nonlocal links
                links += 1
                ins.then_inc(link, 1)
                dve.wait_ge(link, links)

            def first_best(values, n, to):
                linked(v.tensor_reduce(best, values, AX.X, ALU.max))
                linked(v.tensor_tensor(hit[:, :, 0:n], values, wide(best, n), ALU.is_equal))
                linked(v.tensor_scalar(hit[:, :, 0:n], hit[:, :, 0:n], -99.0, 99.0, ALU.mult, ALU.add))
                linked(v.tensor_tensor(index[:, :, 0:n], hit[:, :, 0:n], iota(n), ALU.add))
                linked(v.tensor_reduce(best, index[:, :, 0:n], AX.X, ALU.min))
                linked(v.tensor_tensor(to, iota(n), wide(best, n), ALU.is_equal))

            dve.wait_ge(scored, 1)
            linked(v.tensor_tensor(sel, score, rb.unsqueeze(1).to_broadcast([P, 4, N_EXP]), ALU.add))
            member = sel.rearrange("p t (g e) -> p t g e", g=4)
            sums = duo.rearrange("p t (g s) -> p t g s", g=4)
            for s, (i, j) in enumerate(((0, 1), (0, 2), (0, 3), (1, 2), (1, 3), (2, 3))):
                ins = v.tensor_tensor(sums[:, :, :, s], member[:, :, :, i], member[:, :, :, j], ALU.add)
            linked(ins)
            linked(v.tensor_reduce(group, sums, AX.X, ALU.max))
            first_best(group, 4, group_one)
            spread = masked.rearrange("p t (g e) -> p t g e", g=4)
            chosen = group_one.unsqueeze(3).to_broadcast([P, 4, 4, 4])
            linked(v.tensor_tensor(spread, member, chosen, ALU.mult))
            linked(v.tensor_scalar(group_one, group_one, -1.0, 1e30, ALU.add, ALU.mult))
            linked(v.tensor_tensor(spread, spread, chosen, ALU.add))
            first_best(masked, N_EXP, one)
            linked(v.scalar_tensor_tensor(out=masked, in0=one, scalar=-2e30, in1=masked, op0=ALU.mult, op1=ALU.add))
            first_best(masked, N_EXP, two)
            v.tensor_tensor(both, one, two, ALU.add).then_inc(both_ready, 1)
            linked(v.tensor_tensor(masked, one, score, ALU.mult))
            linked(v.tensor_reduce(net.share[:, :, 0], masked, AX.X, ALU.add))
            linked(v.tensor_tensor(masked, two, score, ALU.mult))
            linked(v.tensor_reduce(net.share[:, :, 1], masked, AX.X, ALU.add))
            linked(v.tensor_tensor(best, net.share[:, :, 0], net.share[:, :, 1], ALU.add))
            linked(v.reciprocal(best, best))
            linked(v.tensor_tensor(net.share[:], net.share[:], wide(best, 2), ALU.mult))
            dve.wait_ge(counted, 1)
            count = net.ps[:, 2, 0:N_EXP]
            linked(v.tensor_scalar(used, count, 0.0, None, ALU.is_gt))
            for m in range(1, 4):
                linked(v.scalar_tensor_tensor(out=used, in0=count, scalar=float(m * P), in1=used, op0=ALU.is_gt, op1=ALU.add))
            src, dst = used, ends
            for step in (1, 2, 4, 8):
                v.tensor_copy(dst[:, 0:step], src[:, 0:step])
                linked(v.tensor_tensor(dst[:, step:], src[:, step:], src[:, 0:N_EXP - step], ALU.add))
                src, dst = dst, (ends_b if dst is ends else ends)
            total, start = src, dst
            linked(v.tensor_tensor(start, total, used, ALU.subtract))
            linked(v.scalar_tensor_tensor(out=place, in0=start.unsqueeze(1).to_broadcast([P, 4, N_EXP]), scalar=float(P),
                                          in1=net.ps[:, 1, 0:4 * N_EXP].rearrange("p (t n) -> p t n", t=4), op0=ALU.mult, op1=ALU.add))
            linked(v.tensor_tensor(one, one, place, ALU.mult))
            linked(v.tensor_tensor(two, two, place, ALU.mult))
            v.tensor_reduce(slot[:, :, 0], one, AX.X, ALU.add)
            linked(v.tensor_reduce(slot[:, :, 1], two, AX.X, ALU.add))
            v.tensor_copy(net.slots[:].rearrange("p (t w) -> p t w", w=2), slot).then_inc(slots_ready, 1)
            grid = reached.rearrange("p (j e) -> p j e", e=N_EXP)
            linked(v.tensor_tensor(grid, total.unsqueeze(1).to_broadcast([P, BLOCKS, N_EXP]),
                                   block_no.unsqueeze(2).to_broadcast([P, BLOCKS, N_EXP]), ALU.is_le))
            linked(v.tensor_reduce(expert, grid, AX.X, ALU.add))
            v.tensor_scalar(net.block_expert[:], expert, float(N_EXP - 1), None, ALU.min)
            dve.wait_ge(table_turned, 1)
            v.tensor_copy(net.slot_tokens[:], net.ps[:, 3, 0:BLOCKS + 2])


def experts(net):
    nc, d = net.nc, net.dram
    net.slot_rows = nc.dram_tensor("slot_rows", (BLOCKS * P, D), F32, kind="Internal").ap()
    HC = D_EXP // P
    SIZE = 2 * KD * D_EXP + HC * D
    place = [net.arena[:, n * SIZE:(n + 1) * SIZE] for n in range(2)]
    wg = [p[:, 0:KD * D_EXP].rearrange("p (k n) -> p k n", k=KD) for p in place]
    wu = [p[:, KD * D_EXP:2 * KD * D_EXP].rearrange("p (k n) -> p k n", k=KD) for p in place]
    wd = [p[:, 2 * KD * D_EXP:].rearrange("p (k n) -> p k n", k=HC) for p in place]
    spare = net.a.rearrange("p k t -> p (k t)")
    gathered = net.work[:, 0:2 * D].rearrange("p (s n) -> p s n", s=2)
    silu, hidden = net.work[:, 2 * D:2 * D + BANK], net.work[:, 2 * D + BANK:2 * D + 2 * BANK]
    x = spare[:, 0:2 * D].rearrange("p (s n) -> p s n", s=2)
    y = spare[:, 2 * D:4 * D].rearrange("p (s n) -> p s n", s=2)
    bank2 = lambda n: net.ps[:, n:n + 2, :].rearrange("p b n -> p (b n)")
    mats = [d[n][0].rearrange("e (k p) n -> e p k n", p=P) for n in ("moe_w_gate_2", "moe_w_up_2", "moe_w_down_2")]
    TURNS = BLOCKS // 2
    names = ("gate_in0", "gate_in1", "up_in0", "up_in1", "down_in0", "down_in1", "wanted", "gather_go", "gathered_in0", "gathered_in1", "turned", "x_copied", "gate_done", "up_done",
             "silu_done", "hidden_done", "down_done", "y_copied", "stored0", "stored1")
    with net.stage(*names) as (block, gate_in0, gate_in1, up_in0, up_in1, down_in0, down_in1, wanted, gather_go, gathered0, gathered1, turned, x_copied, gate_done, up_done,
                               silu_done, hidden_done, down_done, y_copied, stored0, stored1):
        gate_in, up_in, down_in = (gate_in0, gate_in1), (up_in0, up_in1), (down_in0, down_in1)
        gathered_in, stored = (gathered0, gathered1), (stored0, stored1)

        @block.sync
        def _(sp):
            with sp.Fori(0, TURNS) as i:
                for s in range(2):
                    e = bass.ds(sp.value_load(net.block_expert[0:1, bass.ds(i * 2 + s, 1)], min_val=0, max_val=N_EXP - 1), 1)
                    for dst, src, used, landed in ((wg[s], mats[0], up_done, gate_in[s]), (wu[s], mats[1], None, up_in[s]),
                                                   (wd[s], mats[2], down_done, down_in[s])):
                        if used is not None:
                            sp.wait_ge(used, i * 2 + (s + 1))
                        sp.dma_start(dst.unsqueeze(1), src[e].rearrange("e p k n -> p e k n")).then_inc(landed, 16)

        @block.gpsimd
        def _(pool):
            def gather(s):
                nc.gpsimd.indirect_dma_start(gathered[:, s, :], None, net.token_rows,
                                             bass.IndirectOffsetOnAxis(net.rows_wanted[:, s:s + 1], 0)).then_inc(gathered_in[s], 16)

            with pool.Fori(0, TURNS) as i:
                for s in range(2):
                    pool.wait_ge(wanted, i * 2 + (s + 1))
                    pool.wait_ge(turned, i * 2 + (s + 1))
                    pool.sem_inc(gather_go, 1)
                    gather(s)
            pool.wait_ge(wanted, BLOCKS + 1)
            pool.wait_ge(turned, BLOCKS + 1)
            gather(0)

        @block.tensor
        def _(pe):
            def turn(s):
                for k in range(KD):
                    mm = nc.tensor.transpose(bank2(0)[:, k * P:(k + 1) * P], gathered[:, s, k * P:(k + 1) * P], net.c("ident"))
                mm.then_inc(turned, 1)

            pe.sem_inc(turned, 2)
            pe.sem_inc(up_done, 2)
            pe.sem_inc(down_done, 2)
            pe.wait_ge(gathered_in[0], 16)
            turn(0)
            with pe.Fori(0, TURNS) as i:
                for s in range(2):
                    pe.wait_ge(x_copied, i * 2 + (s + 1))
                    pe.wait_ge(hidden_done, i * 2 + (s + 1))
                    for bank, w, landed, done in ((2, wg[s], gate_in[s], gate_done), (3, wu[s], up_in[s], up_done)):
                        pe.wait_ge(landed, (i + 1) * 16)
                        for f in range(HC):
                            for k in range(KD):
                                mm = nc.tensor.matmul(net.ps[:, bank, f * P:(f + 1) * P], w[:, k, f * P:(f + 1) * P],
                                                      x[:, s, k * P:(k + 1) * P], start=(k == 0), stop=(k == KD - 1))
                        mm.then_inc(done, 1)
                    pe.wait_ge(gathered_in[1 - s], (i + (s + 1)) * 16)
                    turn(1 - s)
                    pe.wait_ge(hidden_done, i * 2 + (s + 2))
                    pe.wait_ge(y_copied, i * 2 + (s + 1))
                    pe.wait_ge(down_in[s], (i + 1) * 16)
                    for half in range(2):
                        for k in range(HC):
                            mm = nc.tensor.matmul(net.ps[:, 4 + 2 * s + half, :], hidden[:, k * P:(k + 1) * P],
                                                  wd[s][:, k, half * BANK:(half + 1) * BANK], start=(k == 0), stop=(k == HC - 1))
                    mm.then_inc(down_done, 1)

        @block.scalar
        def _(act):
            act.sem_inc(stored0, 16)
            act.sem_inc(stored1, 16)
            act.wait_ge(turned, 3)
            nc.scalar.activation(x[:, 0, :], bank2(0), ACT.Copy).then_inc(x_copied, 1)
            with act.Fori(0, TURNS) as i:
                for s in range(2):
                    act.wait_ge(gate_done, i * 2 + (s + 1))
                    act.wait_ge(hidden_done, i * 2 + (s + 1))
                    nc.scalar.activation(silu, net.ps[:, 2, :], ACT.Silu).then_inc(silu_done, 1)
                    act.wait_ge(turned, i * 2 + (s + 4))
                    nc.scalar.activation(x[:, 1 - s, :], bank2(0), ACT.Copy).then_inc(x_copied, 1)
                    act.wait_ge(y_copied, i * 2 + (s + 3))
                    act.dma_start(net.slot_rows[bass.ds((i * 2 + s) * P, P)], y[:, s, :]).then_inc(stored[s], 16)
            for s in range(2):
                act.wait_ge(stored[s], (TURNS + 1) * 16)

        @block.vector
        def _(dve):
            def want(s, block_no):
                nc.vector.tensor_scalar(net.rows_wanted[:, s:s + 1], net.slot_tokens[:, block_no], 1.0, None, ALU.mult).then_inc(wanted, 1)

            dve.sem_inc(hidden_done, 1)
            dve.sem_inc(y_copied, 2)
            want(0, slice(0, 1))
            want(1, slice(1, 2))
            with dve.Fori(0, TURNS) as i:
                for s in range(2):
                    dve.wait_ge(gathered_in[s], (i + 1) * 16)
                    want(s, bass.ds(i * 2 + (s + 2), 1))
                    dve.wait_ge(silu_done, i * 2 + (s + 1))
                    dve.wait_ge(up_done, i * 2 + (s + 3))
                    nc.vector.tensor_tensor(hidden, silu, net.ps[:, 3, :], ALU.mult).then_inc(hidden_done, 1)
                    dve.wait_ge(down_done, i * 2 + (s + 3))
                    dve.wait_ge(stored[s], (i + 1) * 16)
                    nc.vector.tensor_copy(y[:, s, :], bank2(4 + 2 * s)).then_inc(y_copied, 1)


def combine(net):
    nc = net.nc
    rows = net.arena[:, 0:8 * D].rearrange("p (n m) -> p n m", n=8)
    with net.stage("rows_in", "first_done", "summed", "turned") as (block, rows_in, first_done, summed, turned):
        @block.gpsimd
        def _(pool):
            for n in range(8):
                nc.gpsimd.indirect_dma_start(rows[:, n, :], None, net.slot_rows,
                                             bass.IndirectOffsetOnAxis(net.slots[:, n:n + 1], 0)).then_inc(rows_in, 16)

        @block.tensor
        def _(pe):
            for t in range(4):
                pe.wait_ge(summed, t + 1)
                for k in range(KD):
                    mm = nc.tensor.transpose(net.ps[:, 2 * t + k // 4, k % 4 * P:(k % 4 + 1) * P], rows[:, 2 * t, k * P:(k + 1) * P], net.c("ident"))
                mm.then_inc(turned, 1)

        @block.vector
        def _(dve):
            def add(t):
                for k in range(KD):
                    to = net.h[:, k, t * P:(t + 1) * P]
                    nc.vector.scalar_tensor_tensor(out=to, in0=net.ps[:, 2 * t + k // 4, k % 4 * P:(k % 4 + 1) * P],
                                                   scalar=gate_of(net, 2, 5, k, 0), in1=to, op0=ALU.mult, op1=ALU.add)

            dve.wait_ge(rows_in, 8 * 16)
            for t in range(4):
                one, two = rows[:, 2 * t, :], rows[:, 2 * t + 1, :]
                nc.vector.tensor_scalar(one, one, net.share[:, t, 0:1], None, ALU.mult).then_inc(first_done, 1)
                dve.wait_ge(first_done, t + 1)
                nc.vector.scalar_tensor_tensor(out=one, in0=two, scalar=net.share[:, t, 1:2], in1=one, op0=ALU.mult,
                                               op1=ALU.add).then_inc(summed, 1)
                if t >= 1:
                    dve.wait_ge(turned, t)
                    add(t - 1)
            dve.wait_ge(turned, 4)
            add(3)


def second_block(net):
    d, sp_ = net.dram, Sparse(net)
    modulate(net, 2, 0, (7,), LAT)
    sparse_attention(net, sp_)
    short_convolution(net, sp_)
    delta_net(net, sp_)
    head_norms(net, [(sp_.yb[:, n, :], 1.0 / DH, 1.0) for n in range(4)])
    merge_branches(net, sp_)
    project_back(net, d["w_out_2"][0], KD, lambda k: sp_.merged[:, k, :], 2, 2, LAT)
    modulate(net, 2, 3, (8,), LAT)
    route(net)
    experts(net)
    combine(net)


INPUTS = ["x", "c", "ctx", "c_ctx", "w_ada", "b_ada", "g_mix", "g_ffn", "w_gate_up", "w_down", "swa_w_qkv", "swa_g_q", "swa_g_k",
          "swa_sink", "swa_w_o", "na_w_qkv", "na_g_q", "na_g_k", "na_rpb", "na_w_o", "c_2", "rel_bias_2", "router_w_2",
          "router_b_2", "ada_w_2", "ada_b_2", "norm1_g_2", "norm2_g_2", "w_in_2", "qk_norm_g_2", "cmp_pos_2", "cmp_w1_2",
          "cmp_w2_2", "dn_conv_w_2", "dn_a_log_2", "dn_dt_bias_2", "dn_norm_g_2", "w_branch_a_2", "w_branch_b_2", "w_out_2",
          "moe_w_gate_2", "moe_w_up_2", "moe_w_down_2"]


def kernel(**inputs):
    import concourse.bacc as bacc
    from concourse.bass_utils import run_bass_kernel_spmd

    nc = bacc.Bacc("TRN2", target_bir_lowering=False, num_devices=1)
    t = tables()
    arrays = {f"in_{name}": np.ascontiguousarray(inputs[name]) for name in INPUTS}
    arrays["in_tables"] = np.concatenate([t[n] for n in RESIDENT], 1)
    arrays["in_more_tables"] = np.concatenate([t[n] for n in LOADED], 1)
    dram = {name[3:]: nc.dram_tensor(name, a.shape, F32, kind="ExternalInput").ap() for name, a in arrays.items()}
    out = nc.dram_tensor("out_x", (1, LAT, D), F32, kind="ExternalOutput").ap()
    program(nc, dram, out)
    got = run_bass_kernel_spmd(nc, [arrays], core_ids=[0])
    return got.results[0]["out_x"]
```
